# Optimizing a Trainium2 kernel written in Bass

```python
import jax
import jax.numpy as jnp
from jax import lax
import numpy as np

D_MODEL = 1024
BATCH = 1
SEQ = 512
DEPTH = 1
DEC_BATCH = 1
DEC_SEQ = 32
PAST_LEN = 256

CHUNK = 64
Q_BLOCK = 128
HG_HEADS = 4
HG_KDIM = 128
HG_VDIM = 128
HG_WIDTH = HG_HEADS * HG_KDIM
FOX_HEADS = 8
FOX_HEAD_DIM = 64
FOX_WIDTH = FOX_HEADS * FOX_HEAD_DIM
MIX_WIDTH = HG_WIDTH + FOX_WIDTH
IN_SPLITS = [HG_WIDTH, 2 * HG_WIDTH, 3 * HG_WIDTH, 4 * HG_WIDTH,
             4 * HG_WIDTH + FOX_WIDTH, 4 * HG_WIDTH + 2 * FOX_WIDTH, 4 * HG_WIDTH + 3 * FOX_WIDTH]
IN_COLS = 4 * HG_WIDTH + 3 * FOX_WIDTH + FOX_HEADS
N_EXPERTS = 16
N_GROUPS = 4
EXPERTS_PER_GROUP = N_EXPERTS // N_GROUPS
TOP_K = 2
D_EXPERT = 512
N_MOD = 6
FOX_F_BIAS_INIT = 3.0
EPS = 1e-6

kernel_name = 'hybrid_hgrn2_fox_moe_stream_step'

def rms_norm(x, gain):
    xf = x.astype(jnp.float32)
    y = xf * lax.rsqrt(jnp.mean(xf * xf, axis=-1, keepdims=True) + EPS)
    return (y * gain.astype(jnp.float32)).astype(x.dtype)

def ada_mod(c, w_ada_l, b_ada_l):
    m = jax.nn.silu(c) @ w_ada_l + b_ada_l
    return jnp.split(m[:, None, :], N_MOD, axis=-1)

def hgrn_lower_bound(hg_lower_bounds, l):
    p = jax.nn.softmax(hg_lower_bounds.astype(jnp.float32), axis=0)
    cum = jnp.cumsum(p, axis=0)
    return cum[l] - cum[0]

def hgrn_chunk(S, q, k, v, logf):
    L = q.shape[1]
    b = jnp.cumsum(logf, axis=1)
    o_inter = jnp.einsum('blhk,bhkv->blhv', q * jnp.exp(b), S)
    causal = jnp.tril(jnp.ones((L, L), dtype=bool))[None, :, :, None, None]
    decay = jnp.exp(jnp.where(causal, b[:, :, None] - b[:, None, :], -jnp.inf))
    att = jnp.einsum('bthk,bshk,btshk->bhts', q, k, decay)
    o_intra = jnp.einsum('bhts,bshv->bthv', att, v)
    b_last = b[:, -1]
    S_new = jnp.exp(b_last)[..., None] * S + jnp.einsum(
        'bshk,bshv->bhkv', k * jnp.exp(b_last[:, None] - b), v)
    return S_new, o_intra + o_inter

def hgrn_scan(S0, q, k, v, logf):
    B, L = q.shape[0], q.shape[1]
    if L <= CHUNK:
        return hgrn_chunk(S0, q, k, v, logf)
    n = L // CHUNK

    def to_blocks(a):
        return jnp.moveaxis(a.reshape(B, n, CHUNK, *a.shape[2:]), 1, 0)

    def step(S, inp):
        return hgrn_chunk(S, *inp)

    S_last, o = lax.scan(step, S0, (to_blocks(q), to_blocks(k), to_blocks(v), to_blocks(logf)))
    o = jnp.moveaxis(o, 0, 1).reshape(B, L, HG_HEADS, HG_VDIM)
    return S_last, o

def hgrn_mixer(S0, hq, hf, hi, hg, lb, gain):
    B, L = hq.shape[0], hq.shape[1]
    f32 = jnp.float32
    q = jax.nn.silu(hq.astype(f32)).reshape(B, L, HG_HEADS, HG_KDIM) * (HG_KDIM ** -0.5)
    fr = hf.astype(f32).reshape(B, L, HG_HEADS, HG_KDIM)
    lbh = lb.reshape(HG_HEADS, HG_KDIM)
    logf = jnp.logaddexp(jnp.log(lbh), jnp.log1p(-lbh) + jax.nn.log_sigmoid(fr))
    k = (1.0 - lbh) * jax.nn.sigmoid(-fr)
    v = hi.astype(f32).reshape(B, L, HG_HEADS, HG_VDIM)
    S, o = hgrn_scan(S0.astype(f32), q, k, v, logf)
    o = o * lax.rsqrt(jnp.mean(o * o, axis=-1, keepdims=True) + EPS)
    o = o.reshape(B, L, HG_WIDTH) * gain.astype(f32) * jax.nn.silu(hg.astype(f32))
    return o.astype(hq.dtype), S

def fox_block(q, k, v, cq, ck, q_start):
    Lq, Lk = q.shape[1], k.shape[1]
    s = jnp.einsum('bqhd,bkhd->bhqk', q, k).astype(jnp.float32) * (FOX_HEAD_DIM ** -0.5)
    s = s + jnp.moveaxis(cq, 1, 2)[..., :, None] - jnp.moveaxis(ck, 1, 2)[..., None, :]
    q_pos = q_start + jnp.arange(Lq, dtype=jnp.int32)
    k_pos = jnp.arange(Lk, dtype=jnp.int32)
    s = jnp.where(k_pos[None, :] <= q_pos[:, None], s, -jnp.inf)
    p = jax.nn.softmax(s, axis=-1)
    return jnp.einsum('bhqk,bkhd->bqhd', p.astype(v.dtype), v)

def fox_mixer(fq, fk, fv, ff, f_bias, out_gain, past):
    B, L = fq.shape[0], fq.shape[1]
    q = fq.reshape(B, L, FOX_HEADS, FOX_HEAD_DIM)
    k = fk.reshape(B, L, FOX_HEADS, FOX_HEAD_DIM)
    v = fv.reshape(B, L, FOX_HEADS, FOX_HEAD_DIM)
    logf = jax.nn.log_sigmoid(ff.astype(jnp.float32) + f_bias.astype(jnp.float32))
    if past is None:
        c = jnp.cumsum(logf, axis=1)
        outs = [fox_block(q[:, t0:t0 + Q_BLOCK], k[:, :t0 + Q_BLOCK], v[:, :t0 + Q_BLOCK],
                          c[:, t0:t0 + Q_BLOCK], c[:, :t0 + Q_BLOCK], t0)
                for t0 in range(0, L, Q_BLOCK)]
        o = jnp.concatenate(outs, axis=1)
    else:
        pk, pv, plogf = past
        P = pk.shape[1]
        k_all = jnp.concatenate([pk.astype(k.dtype), k], axis=1)
        v_all = jnp.concatenate([pv.astype(v.dtype), v], axis=1)
        c = jnp.cumsum(jnp.concatenate([plogf.astype(jnp.float32), logf], axis=1), axis=1)
        o = fox_block(q, k_all, v_all, c[:, P:], c, P)
    o = rms_norm(o.reshape(B, L, FOX_WIDTH), out_gain)
    return o, k, v, logf

def moe(h, w_router, b_router, w_gate, w_up, w_down):
    B, L, D = h.shape
    t = h.reshape(B * L, D)
    probs = jax.nn.softmax((t @ w_router).astype(jnp.float32), axis=-1)
    sel = (probs + b_router.astype(jnp.float32)).reshape(-1, N_GROUPS, EXPERTS_PER_GROUP)
    group_score = jnp.sum(lax.top_k(sel, TOP_K)[0], axis=-1)
    g_idx = jnp.argmax(group_score, axis=-1)
    in_group = jnp.sum(sel * jax.nn.one_hot(g_idx, N_GROUPS, dtype=jnp.float32)[:, :, None], axis=1)
    e_local = lax.top_k(in_group, TOP_K)[1]
    e_idx = g_idx[:, None] * EXPERTS_PER_GROUP + e_local
    w = jnp.take_along_axis(probs, e_idx, axis=-1)
    w = w / jnp.sum(w, axis=-1, keepdims=True)
    gates = jnp.sum(jax.nn.one_hot(e_idx, N_EXPERTS, dtype=jnp.float32) * w[..., None], axis=1)
    y = jnp.zeros((B * L, D), jnp.float32)
    for e in range(N_EXPERTS):
        he = jax.nn.silu(t @ w_gate[e]) * (t @ w_up[e])
        y = y + gates[:, e:e + 1] * (he @ w_down[e]).astype(jnp.float32)
    return y.reshape(B, L, D).astype(h.dtype)

def trunk_layer(x, c, l, p, hg_state0, fox_past):
    shift_m, scale_m, gate_m, shift_f, scale_f, gate_f = ada_mod(c, p['w_ada'][l], p['b_ada'][l])
    h = rms_norm(x, p['norm_mix_gain'][l]) * (1.0 + scale_m) + shift_m
    hq, hf, hi, hg, fq, fk, fv, ff = jnp.split(h @ p['w_in'][l], IN_SPLITS, axis=-1)
    lb = hgrn_lower_bound(p['hg_lower_bounds'], l)
    hg_out, hg_state = hgrn_mixer(hg_state0, hq, hf, hi, hg, lb, p['hg_norm_gain'][l])
    fox_out, k_new, v_new, logf_new = fox_mixer(fq, fk, fv, ff, p['fox_f_bias'][l], p['fox_out_gain'][l], fox_past)
    mixed = jnp.concatenate([hg_out, fox_out.astype(hg_out.dtype)], axis=-1) @ p['w_out'][l]
    x = x + gate_m * mixed
    h = rms_norm(x, p['norm_ffn_gain'][l]) * (1.0 + scale_f) + shift_f
    x = x + gate_f * moe(h, p['w_router'], p['b_router'], p['w_exp_gate'][l], p['w_exp_up'][l], p['w_exp_down'][l])
    return x, hg_state, k_new, v_new, logf_new

def setup_inputs(seed: int = 0) -> dict:
    key = jax.random.key(seed)
    ks = jax.random.split(key, 24)
    f32 = jnp.float32

    def nrm(k, shape, scale=1.0):
        return jax.random.normal(k, shape, f32) * scale

    d_in = D_MODEL ** -0.5
    return {
        'x_prompt': nrm(ks[0], (BATCH, SEQ, D_MODEL)),
        'x_sample': nrm(ks[1], (DEC_BATCH, DEC_SEQ, D_MODEL)),
        'cache_fox_k': nrm(ks[2], (DEPTH, DEC_BATCH, PAST_LEN, FOX_HEADS, FOX_HEAD_DIM)),
        'cache_fox_v': nrm(ks[3], (DEPTH, DEC_BATCH, PAST_LEN, FOX_HEADS, FOX_HEAD_DIM)),
        'cache_fox_logf': jax.nn.log_sigmoid(FOX_F_BIAS_INIT + nrm(ks[4], (DEPTH, DEC_BATCH, PAST_LEN, FOX_HEADS))),
        'state_hgrn': nrm(ks[5], (DEPTH, DEC_BATCH, HG_HEADS, HG_KDIM, HG_VDIM), 0.5),
        'c_prompt': nrm(ks[6], (BATCH, D_MODEL)),
        'c_sample': nrm(ks[7], (DEC_BATCH, D_MODEL)),
        'norm_mix_gain': 1.0 + nrm(ks[8], (DEPTH, D_MODEL), 0.02),
        'norm_ffn_gain': 1.0 + nrm(ks[9], (DEPTH, D_MODEL), 0.02),
        'w_ada': nrm(ks[10], (DEPTH, D_MODEL, N_MOD * D_MODEL), 0.5 * d_in),
        'b_ada': nrm(ks[11], (DEPTH, N_MOD * D_MODEL), 0.02),
        'w_in': nrm(ks[12], (DEPTH, D_MODEL, IN_COLS), d_in),
        'hg_lower_bounds': nrm(ks[13], (DEPTH, HG_WIDTH), 0.1),
        'hg_norm_gain': 1.0 + nrm(ks[14], (DEPTH, HG_WIDTH), 0.02),
        'fox_f_bias': FOX_F_BIAS_INIT + nrm(ks[15], (DEPTH, FOX_HEADS), 0.1),
        'fox_out_gain': 1.0 + nrm(ks[16], (DEPTH, FOX_WIDTH), 0.02),
        'w_out': nrm(ks[17], (DEPTH, MIX_WIDTH, D_MODEL), MIX_WIDTH ** -0.5),
        'w_router': nrm(ks[18], (D_MODEL, N_EXPERTS), d_in),
        'b_router': nrm(ks[19], (N_EXPERTS,), 0.01),
        'w_exp_gate': nrm(ks[20], (DEPTH, N_EXPERTS, D_MODEL, D_EXPERT), d_in),
        'w_exp_up': nrm(ks[21], (DEPTH, N_EXPERTS, D_MODEL, D_EXPERT), d_in),
        'w_exp_down': nrm(ks[22], (DEPTH, N_EXPERTS, D_EXPERT, D_MODEL), D_EXPERT ** -0.5),
        'final_norm_gain': 1.0 + nrm(ks[23], (D_MODEL,), 0.02),
    }

def reference(x_prompt, x_sample, cache_fox_k, cache_fox_v, cache_fox_logf, state_hgrn, c_prompt, c_sample,
              norm_mix_gain, norm_ffn_gain, w_ada, b_ada, w_in, hg_lower_bounds, hg_norm_gain,
              fox_f_bias, fox_out_gain, w_out, w_router, b_router, w_exp_gate, w_exp_up, w_exp_down,
              final_norm_gain):
    p = {'norm_mix_gain': norm_mix_gain, 'norm_ffn_gain': norm_ffn_gain, 'w_ada': w_ada, 'b_ada': b_ada,
         'w_in': w_in, 'hg_lower_bounds': hg_lower_bounds, 'hg_norm_gain': hg_norm_gain,
         'fox_f_bias': fox_f_bias, 'fox_out_gain': fox_out_gain, 'w_out': w_out,
         'w_router': w_router, 'b_router': b_router, 'w_exp_gate': w_exp_gate, 'w_exp_up': w_exp_up,
         'w_exp_down': w_exp_down}
    xp, xs = x_prompt, x_sample
    sp_h, sp_k, sp_v, sp_f = [], [], [], []
    ss_h, ss_k, ss_v, ss_f = [], [], [], []
    for l in range(DEPTH):
        s0 = jnp.zeros((xp.shape[0], HG_HEADS, HG_KDIM, HG_VDIM), jnp.float32)
        xp, h_p, k_p, v_p, f_p = trunk_layer(xp, c_prompt, l, p, s0, None)
        xs, h_s, k_s, v_s, f_s = trunk_layer(xs, c_sample, l, p, state_hgrn[l],
                                             (cache_fox_k[l], cache_fox_v[l], cache_fox_logf[l]))
        sp_h.append(h_p); sp_k.append(k_p); sp_v.append(v_p); sp_f.append(f_p)
        ss_h.append(h_s); ss_k.append(k_s); ss_v.append(v_s); ss_f.append(f_s)
    y_prompt = rms_norm(xp, final_norm_gain)
    y_sample = rms_norm(xs, final_norm_gain)
    hgrn_state_prompt = jnp.stack(sp_h)
    fox_k_prompt = jnp.stack(sp_k)
    fox_v_prompt = jnp.stack(sp_v)
    fox_logf_prompt = jnp.stack(sp_f)
    hgrn_state_sample = jnp.stack(ss_h)
    fox_k_sample = jnp.stack(ss_k)
    fox_v_sample = jnp.stack(ss_v)
    fox_logf_sample = jnp.stack(ss_f)
    return (y_prompt, y_sample, hgrn_state_prompt, fox_k_prompt, fox_v_prompt, fox_logf_prompt,
            hgrn_state_sample, fox_k_sample, fox_v_sample, fox_logf_sample)


_drawn_inputs = setup_inputs


def setup_inputs(seed=0):
    import zlib

    import numpy as np

    out = dict(_drawn_inputs(seed))
    spreads = {}
    factors = {'state_hgrn': 8.0,
     'hg_norm_gain': 28.959,
     'fox_out_gain': 16.862,
     'final_norm_gain': 8.467,
     'norm_ffn_gain': 4.035}
    for name, (base, spread) in spreads.items():
        noise = np.random.default_rng([zlib.crc32(name.encode()), seed]).standard_normal(out[name].shape)
        drawn = base * np.exp(spread * noise) if base else spread * noise
        out[name] = jnp.asarray(drawn.astype(out[name].dtype))
    for name, factor in factors.items():
        out[name] = (out[name] * factor).astype(out[name].dtype)
    return out
```

```python
from contextlib import ExitStack

import concourse.bass as bass
from concourse import mybir

F32 = mybir.dt.float32
I32 = mybir.dt.int32
BF16 = mybir.dt.bfloat16
ALU = mybir.AluOpType
ACT = mybir.ActivationFunctionType
AX = mybir.AxisListType

P = 128
D = 1024
KT = D // P
SEQ, NDEC, PAST = 512, 32, 256
TOK = SEQ + NDEC
HALF = TOK // 2
NTILE = 5
ROWS = [P] * 4 + [NDEC]
HGH, HW = 4, 512
FH, FD = 8, 64
NE, NG, EPG = 16, 4, 4
DE = 512
FT = DE // P
CAPT = (TOK + P - 1) // P
MAXT = NE + 2 * TOK // P
EPS = 1e-6
SLOT = 2048
LEVELS = [64, 32, 16, 8, 4, 2, 1]
NEG = -1e30


def wide(ap):
    return ap.unsqueeze(2).broadcast_to([P, NTILE, NE])


def levels(n):
    return [i for i, half in enumerate(LEVELS) if 2 * half <= n]


def bcast(ap, parts):
    return ap.partition_broadcast(parts)


def build(nc, a, out):
    ctx = ExitStack()
    with ctx:
        def sb(name, shape, dt=F32):
            return ctx.enter_context(nc.sbuf_tensor(name, shape, dt))

        def sem(name):
            return ctx.enter_context(nc.semaphore(name))

        W = sb("weights", [P, 12 * SLOT])
        x = sb("x", [P, NTILE, D])
        hT = sb("hT", [P, KT, TOK])
        R = sb("R", [P, 18560])
        ident = sb("ident", [P, P])
        cpad = sb("cpad", [P, KT, 32])
        st = sb("stats", [P, 160])
        bank = [ctx.enter_context(nc.psum_tensor(f"bank{i}", [P, 512], F32)) for i in range(8)]

        def view(t, off, *shape):
            n = 1
            for s in shape:
                n *= s
            v = t[:, off:off + n]
            if len(shape) == 2:
                v = v.rearrange("p (a b) -> p a b", b=shape[1])
            if len(shape) == 3:
                v = v.rearrange("p (a b c) -> p a b c", b=shape[1], c=shape[2])
            return v

        hflat = hT[:, :, :].rearrange("p k t -> p (k t)")
        WA = 8 * SLOT
        qs = view(R, 0, HGH, TOK)
        kk = view(R, 2176, HGH, TOK)
        bb = view(R, 4352, HGH, TOK)
        v_hg = view(R, 6528, NTILE, HW)
        G = view(R, 9088, NTILE, HW)
        v_fox = view(R, 11648, NTILE, HW)
        fqT = view(R, 14208, 4, TOK)
        fkT = view(R, 16384, 4, TOK)
        foxo = v_hg
        X = view(W, WA, 7, HGH, P)
        E = view(W, WA + 3584, HGH, P)
        qE = view(W, WA + 4096, HGH, P)
        kE = view(W, WA + 4608, HGH, P)
        kET = view(W, WA + 5120, HGH, P)
        attT = view(W, WA + 5632, HGH, P)
        att6 = view(W, WA + 6144, 2, 6, 32)
        attd = view(W, WA + 6528, HGH, 32)
        S = view(W, WA + 6656, HGH, P)
        hgain = view(W, WA + 7168, HW)
        lmask = view(W, WA + 7680, 6, 32)
        ip, it, ix = (view(W, WA + 6144 + 32 * n, 32).bitcast(I32) for n in range(3))
        mgt, mxf, mtmp = (view(W, WA + 6240 + 32 * n, 32) for n in range(3))
        h1 = [view(W, WA, D), view(W, WA + D, D)]
        fr = view(W, WA, TOK)
        ex = view(W, WA + 544, TOK)
        lg = view(W, WA + 1088, TOK)
        fkt = [view(W, WA + 1632, HW), view(W, WA + 2144, HW)]
        cf = view(W, WA + 3584, 800)
        msb = view(W, WA + 4608, HW)
        badd = view(W, WA + 5120, HW)
        ssel = view(W, WA + 2656, 800)
        lfo = view(W, WA + 3456, NTILE, FH)
        lpast = view(W, WA + 3496, 2, FH)
        fbias = view(W, WA + 3512, 1)
        mod0 = view(R, 0, 2, 2 * D)
        mgain = view(R, 4096, D)
        crow = view(R, 5120, P)
        ckB = view(R, 0, FH, SEQ)
        ckS = view(R, 4096, FH, PAST + NDEC)
        kc = view(hflat, 0, 2, HW)
        vc = view(hflat, D, 2, HW)
        kcT = view(hflat, 2 * D, 4, PAST)
        lf = view(hflat, 3 * D, 800)
        pp = [view(W, WA, 512), view(W, WA + 512, 512)]
        pT = [view(W, WA + 1024, 4, P), view(W, WA + 1536, 4, P)]
        fgain = view(W, WA + 2048, HW)
        osq = view(W, WA + 2560, HW)
        wff = view(W, WA + 7872, KT, FH)
        mod1 = view(R, 0, 2, 2 * D)
        mod2 = view(R, 11648, 2, 2 * D)
        ngain = view(R, 15744, D)
        wrt = view(R, 16768, KT, NE)
        gt = [view(W, WA + 3072, 512), view(W, WA + 3584, 512)]
        h2 = [view(W, WA + 4096, D), view(W, WA + 5120, D)]
        h2T = view(W, WA + 6144, KT, P)

        def dram(name, shape, dt=F32):
            return nc.dram_tensor(name, shape, dt, kind="Internal").ap()
        mod_d = dram("mod_d", (2, 6 * D))
        ck_d = dram("ck_d", (FH, SEQ))
        cks_d = dram("cks_d", (FH, PAST + NDEC))
        h2_d = dram("h2_d", (TOK, D))
        y_d = dram("y_d", (2 * TOK, D))

        plan, where = [], {}

        def grp(name, b, eng):
            where[name] = len(plan)
            plan.append((name, b, eng))

        grp("cT", 0, "act")
        grp("ada0", 1, "dve")
        for i in range(NTILE):
            grp(f"hT{i}0", 2, "act")
            grp(f"hT{i}1", 3, "act")
        for h in range(HGH):
            grp(f"hq{h}0", 4 + 2 * (h % 2), "act")
            grp(f"hq{h}1", 5 + 2 * (h % 2), "act")
        for i in range(NTILE):
            grp(f"hg{i}", 2 + i % 2, "act")
        for h in range(HGH):
            grp(f"hf{h}0", 4 + 2 * (h % 2), "dve")
            grp(f"hf{h}1", 5 + 2 * (h % 2), "dve")
        for i in range(NTILE):
            grp(f"hi{i}", 2 + i % 2, "dve")
        for i in range(NTILE):
            grp(f"fk{i}", 4 + i % 2, "act")
            if i:
                grp(f"fkT{i - 1}", 6, "dve")
        grp("fkT4", 6, "dve")
        for i in range(NTILE):
            grp(f"fv{i}", 2 + i % 2, "dve")
        for h in range(4):
            grp(f"fq{h}0", 4 + 2 * (h % 2), "act")
            grp(f"fq{h}1", 5 + 2 * (h % 2), "act")
        grp("ff0", 0, "dve")
        grp("ff1", 1, "dve")
        grp("lpT", 2, "dve")
        grp("ada1", 3, "dve")
        grp("lfT", 0, "dve")
        grp("ada2", 1, "dve")
        for i in range(NTILE):
            if i < 4:
                grp(f"L{i}", 0, "dve")
            grp(f"Da{i}", 1, "dve")
            grp(f"Db{i}", 2, "dve")
            grp(f"kT{i}", 3, "act")
            grp(f"ho{i}", 4, "dve")
            grp(f"S{i}", 5, "dve")
        grp("kcT0", 6, "act")
        grp("kcT1", 7, "act")
        QT = [3, 2, 1, 0, 4]
        for n, q in enumerate(QT):
            for h in range(FH + 1):
                if h < FH:
                    grp(f"s{q}{h}", h % 2, "dve")
                if h:
                    grp(f"t{q}{h - 1}", 2 + h % 2, "act")
            grp(f"fo{q}", 4 + n % 2, "dve")
        for i in range(NTILE):
            grp(f"m{i}0", 0, "act")
            grp(f"m{i}1", 1, "dve")
        for i in range(NTILE):
            for c in range(2 if i < 4 else 1):
                grp(f"y{i}{c}", 4 + (2 * i + c) % 4, "dve")
        for i in range(NTILE):
            grp(f"r{i}0", 0, "act")
            grp(f"r{i}1", 1, "act")
        grp("lg", 2, "dve")
        grp("pos", 3, "dve")
        grp("cnt", 4, "dve")
        grp("tab", 5, "dve")

        pe_done = sem("pe_done")
        read_out = {"act": sem("act_read_out"), "dve": sem("dve_read_out")}
        rank, before, last = {}, {}, {}
        count = {"act": 0, "dve": 0}
        for name, b, eng in plan:
            count[eng] += 1
            rank[name] = (eng, count[eng])
            before[name] = last.get(b)
            last[b] = name

        def filled(eng, name):
            eng.wait_ge(pe_done, where[name] + 1)

        def taken(eng, name):
            who, n = rank[name]
            eng.wait_ge(read_out[who], n)

        order = {"act": [], "dve": []}

        def read(eng, name, ins):
            assert rank[name] == (eng, len(order[eng]) + 1), name
            order[eng].append(name)
            ins.then_inc(read_out[eng], 1)

        s_ident = sem("ident_ready")
        s_iota = sem("mask_iotas_ready")
        s_cpad = sem("cpad_zeroed")
        s_x = [sem(f"x_in{i}") for i in range(NTILE)]
        s_c = sem("c_in")
        s_small = sem("small_in")
        s_badd = sem("ada_bias_in")
        s_modw = sem("mod_rows_out")
        s_mod0 = sem("mod0_in")
        s_w = [sem(f"slot{i}_in") for i in range(8)]
        s_ss = sem("x_squares_summed")
        s_h1 = sem("h1_ready")
        s_qs = sem("q_scaled")
        s_G = sem("gate_gained")
        s_ln = sem("softplus_ready")
        s_kx = sem("k_exponent_ready")
        s_kk = sem("k_ready")
        s_lf = sem("fox_logf_ready")
        s_cf = sem("fox_cumsum_ready")
        s_kout = [sem(f"fox_k_stored{i}") for i in range(2)]
        s_vout = sem("fox_v_stored")
        s_lout = sem("fox_logf_stored")
        s_ckw = sem("ck_rows_out")
        s_ckr = sem("ck_rows_in")
        s_cache = sem("caches_in")
        s_sout = sem("state_stored")
        s_S0 = sem("sample_state_in")
        s_lmask = sem("level_masks_ready")
        s_lv = sem("level_exponents")
        s_le = sem("level_exps")
        s_att = sem("hgrn_operands")
        s_sq = sem("ho_squares_summed")
        s_mask = sem("ck_masked")
        s_pmax = sem("fox_max_ready")
        s_pexp = sem("fox_exp_ready")
        s_fq = sem("fox_squares_summed")
        s_fo = sem("fox_out_ready")
        s_mod1 = sem("mod12_in")
        s_x2 = sem("x2_half_ready")
        s_x2q = sem("x2_squares_summed")
        s_h2a = sem("h2_scaled")
        s_h2 = sem("h2_ready")
        s_h2w = [sem(f"h2_stored{i}") for i in range(2)]
        s_brt = sem("router_bias_in")
        s_rc = sem("routing_constants_ready")
        s_lx = sem("logits_centered")
        s_lex = sem("logits_exp")
        s_mk = sem("expert_mask_ready")
        s_oh = sem("onehot_ready")
        s_ohu = sem("onehot_used")
        s_rd = sem("routing_ready")
        s_rs = sem("inverse_roots")
        s_dv = sem("dve_step")
        s_ac = sem("act_step")
        s_pl = sem("pool_step")

        steps = {"dve": 0, "act": 0, "pool": 0}

        def vlink(dve, ins):
            steps["dve"] += 1
            ins.then_inc(s_dv, 1)
            dve.wait_ge(s_dv, steps["dve"])

        def alink(act, ins):
            steps["act"] += 1
            ins.then_inc(s_ac, 1)
            act.wait_ge(s_ac, steps["act"])

        def plink(pool, ins):
            steps["pool"] += 1
            ins.then_inc(s_pl, 1)
            pool.wait_ge(s_pl, steps["pool"])

        def both(eng, pair):
            eng.wait_ge(pair[0], 48)
            eng.wait_ge(pair[1], 32)

        def operands(i, n):
            return sum(len(levels(ROWS[j])) + 2 for j in range(i)) + n

        block = ctx.enter_context(nc.Block())
        w_ada = a["w_ada"].rearrange("l (k p) n -> p (l k) n", p=P)
        w_in = a["w_in"].rearrange("l (k p) n -> p (l k) n", p=P)
        w_out = a["w_out"].rearrange("l (k p) n -> p (l k) n", p=P)
        HQ, HF, HI, HG, FQ, FK, FV, FF = (512 * i for i in range(8))

        ring = [(f"ada0_{k}", k, 1) for k in range(KT)]
        ring += [("hq", 0, 2), ("hg", 2, 2), ("hf", 4, 2), ("hi", 6, 2), ("fk", 0, 2), ("fv", 2, 2), ("fq", 4, 2)]
        ring += [(f"ada1_{k}", (6 + k) % 8, 1) for k in range(KT)]
        ring += [(f"ada2_{k}", (6 + k) % 8, 1) for k in range(KT)]
        ring += [(f"wo{k}", (6 + k) % 8, 1) for k in range(4)]
        lastuse = {"hq": "hq31", "hg": "hg4", "hf": "hf31", "hi": "hi4", "fk": "fk4", "fv": "fv4", "fq": "fq31"}
        for r in range(3):
            for k in range(KT):
                lastuse[f"ada{r}_{k}"] = f"ada{r}"
        loads = {}
        slot_count = [0] * 8
        slot_owner = [None] * 8
        for name, s, n in ring:
            slot_count[s] += 16
            loads[name] = (s, slot_count[s], n, [slot_owner[j] for j in range(s, s + n)])
            for j in range(s, s + n):
                slot_owner[j] = name

        def loaded(eng, name):
            s, value, _, _ = loads[name]
            eng.wait_ge(s_w[s], value)

        def wslot(name, width):
            s, _, n, _ = loads[name]
            return view(W, s * SLOT, n * SLOT // width, width)

        s_we = [sem("expert_even_in"), sem("expert_odd_in")]
        s_gath = sem("rows_gathered")
        s_idx = sem("index_copied")
        s_seq = sem("tables_in_order")
        s_xp = sem("rows_transposed")
        s_xta = sem("xT_low_ready")
        s_xtb = sem("xT_high_ready")
        s_gu = sem("gate_up_done")
        s_sil = sem("silu_done")
        s_he = sem("hidden_ready")
        s_yd = sem("down_done")
        s_yea = sem("y_low_read")
        s_yeb = sem("y_high_read")
        s_yst = sem("y_stored")
        xg = view(R, 0, D)
        XT = view(R, D, KT, P)
        heT = view(R, 2 * D, FT, P)
        hs = view(R, 2 * D + 512, FT, P)
        ysb = view(R, 3 * D, D)
        T0 = 4 * D
        prb = view(R, T0, NTILE, NE)
        sel = view(R, T0 + 80, NTILE, NE)
        msk = view(R, T0 + 160, NTILE, NE)
        gts = view(R, T0 + 240, NTILE, NE)
        t80 = [view(R, T0 + 320 + 80 * n, NTILE, NE) for n in range(6)]
        g20 = [view(R, T0 + 800 + 20 * n, NTILE, NG) for n in range(8)]
        brt = view(R, T0 + 960, NE)
        s5 = [view(R, T0 + 976 + 8 * n, NTILE) for n in range(8)]
        gA, gB = view(R, T0 + 1040, NTILE), view(R, T0 + 1048, NTILE)
        slotA = view(R, T0 + 1056, NTILE)
        slotB = view(R, T0 + 1064, NTILE)
        tri = view(R, T0 + 1072, P)
        ones = view(R, T0 + 1200, P)
        iotaj = view(R, T0 + 1328, P // 2).bitcast(BF16)
        ebase = view(R, T0 + 1456, NE)
        tokid = view(R, T0 + 1472, 2 * NTILE)
        pmod = view(R, T0 + 1488, NTILE, NE)
        pdiv = view(R, T0 + 1568, NTILE, NE)
        tokf = view(R, T0 + 1648, NE * CAPT)
        tf = [view(R, T0 + 1808 + 16 * n, NE) for n in range(4)]
        ntile_i = view(R, T0 + 1888, NE).bitcast(I32)
        base_i = view(R, T0 + 1904, NE + 1).bitcast(I32)
        idx1 = view(R, T0 + 1921, 1).bitcast(I32)
        rsel = view(R, T0 + 1924, 3 * NTILE * CAPT * NE // 2).bitcast(BF16).rearrange(
            "p (n i c e) -> p n i c e", n=NTILE, i=CAPT, c=3)
        oh = view(R, T0 + 2524, NTILE * P).bitcast(BF16).rearrange("p (b n j) -> p b n j", b=2, n=NTILE)
        d80 = view(R, T0 + 3164, NTILE, NE)
        tabi = view(R, T0 + 3244, NE * CAPT, 2).bitcast(I32)
        tseq = view(R, T0 + 3404, MAXT + 1, 2).bitcast(I32)
        idx2 = view(R, T0 + 3460, 1).bitcast(I32)
        dst1 = view(R, T0 + 3461, NE * CAPT)
        dst2 = view(R, T0 + 3541, NE * CAPT)
        ya = [view(W, n * D, D) for n in range(NTILE)]
        yb = [view(W, (NTILE + n) * D, D) for n in range(NTILE)]
        gateF = view(W, 6 * SLOT, 2, D)
        fing = view(W, 7 * SLOT, D)
        jk = view(W, 8 * SLOT, D)
        s_ya = [sem(f"y_rows_in{i}") for i in range(NTILE)]
        s_ph3 = sem("final_in")
        s_comb = sem("combined")
        s_fsq = sem("final_square")
        s_fin = sem("final_ready")
        s_out = [sem(f"y_out{i}") for i in range(2)]

        wg = a["w_exp_gate"].rearrange("l e (k p) f -> p (l e) k f", p=P)
        wu = a["w_exp_up"].rearrange("l e (k p) f -> p (l e) k f", p=P)
        wd = a["w_exp_down"].rearrange("l e (k p) f -> p (l e) k f", p=P)

        def wexp(par):
            b = par * 6 * SLOT
            return (view(W, b, KT, DE), view(W, b + 2 * SLOT, KT, DE), view(W, b + 4 * SLOT, FT, D))

        def load_expert(sp, par, e):
            for dst, src in zip(wexp(par), (wg, wu, wd)):
                sp.dma_start(dst, src[:, bass.ds(e, 1), :, :].rearrange("p o k f -> p (o k) f")).then_inc(s_we[par], 16)

        @block.sync
        def _(sp):
            sp.dma_start(crow[0:8, :], a["c_prompt"].rearrange("b (k q) -> (b k) q", q=P)).then_inc(s_c, 16)
            sp.dma_start(crow[8:16, :], a["c_sample"].rearrange("b (k q) -> (b k) q", q=P)).then_inc(s_c, 16)
            for i in range(4):
                sp.dma_start(x[:, i, :], a["x_prompt"][0, i * P:(i + 1) * P, :]).then_inc(s_x[i], 16)
            sp.dma_start(x[0:NDEC, 4, :], a["x_sample"][0]).then_inc(s_x[4], 16)
            cols = {"hq": HQ, "hg": HG, "hf": HF, "hi": HI, "fk": FK, "fv": FV, "fq": FQ}
            for name, _, _ in ring:
                s, value, n, owners = loads[name]
                for o in dict.fromkeys(owners):
                    if o is not None:
                        filled(sp, lastuse[o])
                if name.startswith("ada"):
                    r, k = int(name[3]), int(name[5])
                    sp.dma_start(wslot(name, SLOT)[:, 0, :], w_ada[:, k, r * SLOT:(r + 1) * SLOT]).then_inc(s_w[s], 16)
                elif name.startswith("wo"):
                    k = int(name[2])
                    sp.dma_start(wslot(name, D), w_out[:, 2 * k:2 * k + 2, :]).then_inc(s_w[s], 16)
                else:
                    sp.dma_start(wslot(name, HW), w_in[:, :, cols[name]:cols[name] + HW]).then_inc(s_w[s], 16)
            filled(sp, "y40")
            load_expert(sp, 0, 0)
            filled(sp, "lg")
            both(sp, s_h2w)
            load_expert(sp, 1, 1)
            sp.wait_ge(s_rd, 1)
            with sp.Fori(1, NE // 2) as pair:
                for par in range(2):
                    done = sp.value_load(base_i[0:1, bass.ds(pair * 2 + (par - 1), 1)], min_val=1, max_val=MAXT)
                    sp.wait_ge(s_yd, done)
                    load_expert(sp, par, pair * 2 + par)
            total = sp.value_load(base_i[0:1, NE:NE + 1], min_val=NE, max_val=MAXT)
            sp.wait_ge(s_yd, total)
            for gi in range(2):
                n = P if gi == 0 else NDEC
                sp.dma_start(gateF[0:n, gi, :], bcast(mod_d[gi, 5 * D:6 * D], n)).then_inc(s_ph3, 16)
            sp.dma_start(fing, bcast(a["final_norm_gain"], P)).then_inc(s_ph3, 16)
            sp.wait_ge(s_yst, total * 16 + 16)

            def load_y(i):
                n = ROWS[i]
                sp.dma_start(ya[i][0:n, :], y_d[i * P:i * P + n, :]).then_inc(s_ya[i], 16)
                sp.dma_start(yb[i][0:n, :], y_d[TOK + i * P:TOK + i * P + n, :]).then_inc(s_ya[i], 16)

            for i in range(NTILE):
                load_y(i)
            for i in range(NTILE):
                n = ROWS[i]
                sp.wait_ge(s_fin, i + 1)
                sp.dma_start(out["y_prompt"][0, i * P:i * P + n, :] if i < 4 else out["y_sample"][0],
                             ya[i][0:n, :]).then_inc(s_out[i % 2], 16)
            both(sp, s_out)
            both(sp, s_kout)
            sp.wait_ge(s_vout, 16 * NTILE)
            sp.wait_ge(s_lout, 32)
            sp.wait_ge(s_sout, 32)

        @block.gpsimd
        def _(pool):
            g = nc.gpsimd
            plink(pool, g.memset(st[:], 0.0))
            plink(pool, g.memset(st[:, 126:127], EPS))
            plink(pool, g.memset(ident[:], 0.0))
            g.affine_select(ident[:], ident[:], [[-1, P]], ALU.not_equal, 1.0, base=0,
                            channel_multiplier=1).then_inc(s_ident, 1)
            g.memset(cpad[:], 0.0).then_inc(s_cpad, 1)
            g.iota(ip, [[0, 32]], base=0, channel_multiplier=1)
            g.iota(it, [[1, 32]], base=0, channel_multiplier=0).then_inc(s_iota, 1)
            pool.dma_start(mgain, bcast(a["norm_mix_gain"][0], P)).then_inc(s_small, 16)
            pool.dma_start(hgain, bcast(a["hg_norm_gain"][0], P)).then_inc(s_small, 16)
            pool.dma_start(wff, w_in[:, :, FF:FF + FH]).then_inc(s_small, 16)
            pool.dma_start(fbias[0:8, :], a["fox_f_bias"].rearrange("l h -> h l")).then_inc(s_small, 16)
            pool.dma_start(lpast, a["cache_fox_logf"].rearrange("l b (j p) h -> p (l b j) h", p=P)).then_inc(s_small, 16)
            bada = a["b_ada"].rearrange("l (r j n) -> r (l j) n", r=3, j=4)
            plink(pool, g.memset(badd, 0.0))

            def bias_rows(r):
                for gi in range(2):
                    pool.dma_start(badd[gi:gi + 97:32, :], bada[r]).then_inc(s_badd, 16)

            def mod_rows(r):
                taken(pool, f"ada{r}")
                for gi in range(2):
                    pool.dma_start(mod_d[gi, r * SLOT:(r + 1) * SLOT].rearrange("(j n) -> j n", j=4),
                                   msb[gi:gi + 97:32, :]).then_inc(s_modw, 16)
                pool.wait_ge(s_modw, 32 * (r + 1))

            bias_rows(0)
            mod_rows(0)
            for gi in range(2):
                n = P if gi == 0 else NDEC
                pool.dma_start(mod0[0:n, gi, :], bcast(mod_d[gi, 0:2 * D], n)).then_inc(s_mod0, 16)
            bias_rows(1)
            pool.wait_ge(s_small, 80)
            for h in range(HGH):
                taken(pool, f"hq{h}1")
                g.tensor_scalar(qs[:, h, :], qs[:, h, :], float(P) ** -0.5, None, ALU.mult).then_inc(s_qs, 1)
            for i in range(NTILE):
                n = ROWS[i]
                taken(pool, f"hg{i}")
                g.tensor_tensor(G[0:n, i, :], G[0:n, i, :], hgain[0:n, :], ALU.mult).then_inc(s_G, 1)
            kout = out["fox_k_prompt"].rearrange("l b t h d -> (l b t) (h d)")
            vout = out["fox_v_prompt"].rearrange("l b t h d -> (l b t) (h d)")
            kous = out["fox_k_sample"].rearrange("l b t h d -> (l b t) (h d)")
            vous = out["fox_v_sample"].rearrange("l b t h d -> (l b t) (h d)")
            for i in range(NTILE):
                taken(pool, f"fk{i}")
                pool.dma_start(kout[i * P:(i + 1) * P, :] if i < 4 else kous, fkt[i % 2][0:ROWS[i], :]).then_inc(s_kout[i % 2], 16)
            for i in range(NTILE):
                taken(pool, f"fv{i}")
                pool.dma_start(vout[i * P:(i + 1) * P, :] if i < 4 else vous, v_fox[0:ROWS[i], i, :]).then_inc(s_vout, 16)
            mod_rows(1)
            bias_rows(2)
            filled(pool, "ff1")
            pool.dma_start(kc, a["cache_fox_k"].rearrange("l b (j p) h d -> p (l b j) (h d)", p=P)).then_inc(s_cache, 16)
            pool.dma_start(vc, a["cache_fox_v"].rearrange("l b (j p) h d -> p (l b j) (h d)", p=P)).then_inc(s_cache, 16)
            taken(pool, "lfT")
            pool.wait_ge(s_cf, 1)
            pool.dma_start(out["fox_logf_prompt"].rearrange("l b (i p) h -> p (l b i) h", p=P), lfo[:, 0:4, :]).then_inc(s_lout, 16)
            pool.dma_start(out["fox_logf_sample"][0, 0], lfo[0:NDEC, 4, :]).then_inc(s_lout, 16)
            pool.dma_start(ck_d, cf[0:8, 0:SEQ]).then_inc(s_ckw, 16)
            pool.dma_start(cks_d, cf[0:8, SEQ:SEQ + PAST + NDEC]).then_inc(s_ckw, 16)
            mod_rows(2)
            sp_o = out["hgrn_state_prompt"].rearrange("l b h k v -> k (l b h) v")
            ss_o = out["hgrn_state_sample"].rearrange("l b h k v -> k (l b h) v")
            taken(pool, "S3")
            pool.dma_start(sp_o, S).then_inc(s_sout, 16)
            pool.wait_ge(s_sout, 16)
            pool.dma_start(S, a["state_hgrn"].rearrange("l b h k v -> k (l b h) v")).then_inc(s_S0, 16)
            taken(pool, "S4")
            pool.dma_start(ss_o, S).then_inc(s_sout, 16)
            taken(pool, "ho4")
            pool.wait_ge(s_ckw, 32)
            pool.dma_start(ckB.rearrange("p h t -> p (h t)"), bcast(ck_d.rearrange("h t -> (h t)"), P)).then_inc(s_ckr, 16)
            pool.dma_start(ckS[0:NDEC].rearrange("p h t -> p (h t)"),
                           bcast(cks_d.rearrange("h t -> (h t)"), NDEC)).then_inc(s_ckr, 16)
            pool.dma_start(fgain, bcast(a["fox_out_gain"][0], P)).then_inc(s_ckr, 16)
            pool.wait_ge(s_ckr, 48)
            for n, q in enumerate(QT):
                if n and q < 4:
                    taken(pool, f"s{q + 1}{FH - 1}")
                blk = ckB[:, :, q * P:(q + 1) * P] if q < 4 else ckS[0:NDEC, :, PAST:]
                w = ROWS[q]
                g.affine_select(blk, blk, [[0, FH], [-1, w]], ALU.is_ge, NEG, base=0,
                                channel_multiplier=1).then_inc(s_mask, 1)
            taken(pool, "fo4")
            pool.wait_ge(s_vout, 16 * NTILE)
            for gi in range(2):
                n = P if gi == 0 else NDEC
                pool.dma_start(mod1[0:n, gi, :], bcast(mod_d[gi, SLOT:2 * SLOT], n)).then_inc(s_mod1, 16)
                pool.dma_start(mod2[0:n, gi, :], bcast(mod_d[gi, 2 * SLOT:3 * SLOT], n)).then_inc(s_mod1, 16)
            pool.dma_start(ngain, bcast(a["norm_ffn_gain"][0], P)).then_inc(s_mod1, 16)
            pool.dma_start(wrt, a["w_router"].rearrange("(k p) e -> p k e", p=P)).then_inc(s_mod1, 16)
            for i in range(NTILE):
                n = ROWS[i]
                for c in range(2):
                    taken(pool, f"y{i}{c if i < 4 else 0}")
                    xs = x[0:n, i, c * 512:(c + 1) * 512]
                    g.tensor_tensor(xs, xs, gt[c][0:n, :], ALU.add).then_inc(s_x2, 1)
            for i in range(NTILE):
                n, gi = ROWS[i], i // 4
                pool.wait_ge(s_h2a, i + 1)
                g.tensor_tensor(h2[i % 2][0:n, :], h2[i % 2][0:n, :], mod1[0:n, gi, D:2 * D], ALU.add).then_inc(s_h2, 1)
                pool.wait_ge(s_h2, i + 1)
                pool.dma_start(h2_d[i * P:i * P + n, :], h2[i % 2][0:n, :]).then_inc(s_h2w[i % 2], 16)
            filled(pool, "lg")
            pool.dma_start(brt, bcast(a["b_router"], P)).then_inc(s_brt, 16)
            plink(pool, g.memset(ones, 1.0))
            plink(pool, g.memset(tri, 1.0))
            plink(pool, g.affine_select(tri, tri, [[1, P]], ALU.is_gt, 0.0, base=0, channel_multiplier=-1))
            plink(pool, g.iota(iotaj, [[1, P]], base=0, channel_multiplier=0, allow_small_or_imprecise_dtypes=True))
            plink(pool, g.iota(ebase, [[CAPT * P, NE]], base=1, channel_multiplier=0, allow_small_or_imprecise_dtypes=True))
            plink(pool, g.iota(tokid[:, 0:NTILE], [[1, NTILE]], base=0, channel_multiplier=0, allow_small_or_imprecise_dtypes=True))
            g.iota(tokid[:, NTILE:], [[0, NTILE]], base=0, channel_multiplier=1, allow_small_or_imprecise_dtypes=True).then_inc(s_rc, 1)
            pool.wait_ge(s_rd, 1)
            g.memset(tseq, 0).then_inc(s_seq, 1)
            pool.wait_ge(s_seq, 1)
            with pool.Fori(0, NE) as e:
                nt = pool.value_load(ntile_i[0:1, bass.ds(e, 1)], min_val=1, max_val=CAPT)
                base = pool.value_load(base_i[0:1, bass.ds(e, 1)], min_val=0, max_val=MAXT - CAPT)
                with pool.Fori(0, nt) as i:
                    g.tensor_copy(tseq[:, bass.ds(base + i, 1), :], tabi[:, bass.ds(e * CAPT + i, 1), :]).then_inc(s_seq, 1)
            total = pool.value_load(base_i[0:1, NE:NE + 1], min_val=NE, max_val=MAXT)
            pool.wait_ge(s_seq, total + 1)
            both(pool, s_h2w)
            pool.sem_inc(s_xp, 1)
            pool.dma_start(ysb[0:1, :], h2_d[0:1, :]).then_inc(s_yst, 16)

            last_token, last_y = pool.to_reg(TOK - 1), pool.to_reg(2 * TOK - 1)

            gathers, scatters = pool.alloc_register("gathers"), pool.alloc_register("scatters")
            pool.reg_mov(gathers, 0)
            pool.reg_mov(scatters, 1)

            def gather():
                pool.reg_add(gathers, gathers, 1)
                pool.indirect_dma_start(xg, None, h2_d, bass.IndirectOffsetOnAxis(ap=idx1, axis=0),
                                        bounds_check=last_token, oob_is_err=False).then_inc(s_gath, 16)

            g.tensor_copy(idx1, tseq[:, 0, 0:1]).then_inc(s_idx, 1)
            pool.wait_ge(s_idx, 1)
            gather()
            with pool.Fori(0, total) as t:
                pool.wait_ge(s_xp, t + 2)
                g.tensor_copy(idx1, tseq[:, bass.ds(t + 1, 1), 0]).then_inc(s_idx, 1)
                pool.wait_ge(s_idx, t * 2 + 2)
                gather()
                pool.wait_ge(s_yst, t * 16 + 16)
                g.tensor_copy(idx2, tseq[:, bass.ds(t, 1), 1]).then_inc(s_idx, 1)
                pool.wait_ge(s_idx, t * 2 + 3)
                pool.wait_ge(s_yea, t + 2)
                pool.wait_ge(s_yeb, t + 2)
                pool.reg_add(scatters, scatters, 1)
                pool.indirect_dma_start(y_d, bass.IndirectOffsetOnAxis(ap=idx2, axis=0), ysb, None,
                                        bounds_check=last_y, oob_is_err=False).then_inc(s_yst, 16)
            pool.wait_ge(s_gath, pool.snap(gathers, min_val=1, max_val=MAXT + 1) * 16)
            pool.wait_ge(s_yst, pool.snap(scatters, min_val=1, max_val=MAXT + 1) * 16)

        @block.scalar
        def _(act):
            A = nc.scalar

            def root(y, ss, width):
                alink(act, A.activation(y, ss, ACT.Ln, bias=st[0:y.shape[0], 126:127], scale=1.0 / width))
                return A.activation(y, y, ACT.Exp, scale=-0.5)

            filled(act, "cT")
            act.wait_ge(s_cpad, 1)
            read("act", "cT", A.activation(cpad[:, :, 0:2].rearrange("p k g -> p g k"),
                                           bank[0][:, 0:16].rearrange("p (g k) -> p g k", g=2), ACT.Silu))
            act.wait_ge(s_ident, 1)
            for i in range(NTILE):
                n = ROWS[i]
                act.wait_ge(s_x[i], 16)
                if i:
                    act.wait_ge(s_ss, i)
                A.activation(h1[0][0:n, :], x[0:n, i, :], ACT.Square, accum_out=st[0:n, i:i + 1]).then_inc(s_ss, 1)
            act.wait_ge(s_ss, NTILE)
            root(st[:, 5:10], st[:, 0:5], D).then_inc(s_rs, 1)
            for i in range(NTILE):
                n = ROWS[i]
                for c in range(2):
                    filled(act, f"hT{i}{c}")
                    read("act", f"hT{i}{c}", A.copy(hT[:, 4 * c:4 * c + 4, i * P:i * P + n],
                                                    bank[2 + c][:, :].rearrange("p (k t) -> p k t", k=4)[:, :, 0:n]))
            for h in range(HGH):
                for c in range(2):
                    filled(act, f"hq{h}{c}")
                    if h == 0 and c == 0:
                        act.wait_ge(s_h1, NTILE)
                    read("act", f"hq{h}{c}", A.activation(qs[:, h, c * HALF:(c + 1) * HALF],
                                                          bank[4 + 2 * (h % 2) + c][:, 0:HALF], ACT.Silu))
            for i in range(NTILE):
                filled(act, f"hg{i}")
                b = bank[2 + i % 2]
                if i < 4:
                    read("act", f"hg{i}", A.activation(G[:, i, :], b[:, :], ACT.Silu))
                else:
                    for j in range(4):
                        ins = A.activation(G[0:NDEC, 4, j * P:(j + 1) * P], b[32 * j:32 * j + 32, 0:P], ACT.Silu)
                    read("act", f"hg{i}", ins)
            for h in range(HGH):
                taken(act, f"hf{h}1")
                alink(act, A.activation(ex, fr, ACT.Abs))
                alink(act, A.activation(ex, ex, ACT.Exp, scale=-1.0))
                A.activation(ex, ex, ACT.Ln, bias=1.0).then_inc(s_ln, 1)
                act.wait_ge(s_kx, h + 1)
                A.activation(kk[:, h, :], fr, ACT.Exp).then_inc(s_kk, 1)
            for i in range(NTILE):
                n = ROWS[i]
                filled(act, f"fk{i}")
                if i >= 2:
                    act.wait_ge(s_kout[i % 2], 16 * (i // 2))
                    filled(act, f"fkT{i - 2}")
                b = bank[4 + i % 2]
                if i < 4:
                    read("act", f"fk{i}", A.copy(fkt[i % 2], b[:, :]))
                else:
                    for j in range(4):
                        ins = A.copy(fkt[0][0:NDEC, j * P:(j + 1) * P], b[32 * j:32 * j + 32, 0:P])
                    read("act", f"fk{i}", ins)
            for h in range(4):
                for c in range(2):
                    filled(act, f"fq{h}{c}")
                    read("act", f"fq{h}{c}", A.copy(fqT[:, h, c * HALF:(c + 1) * HALF],
                                                    bank[4 + 2 * (h % 2) + c][:, 0:HALF]))
            taken(act, "ff1")
            alink(act, A.activation(ssel[0:8, 0:TOK], cf[0:8, 0:TOK], ACT.Abs))
            alink(act, A.activation(ssel[0:8, 0:TOK], ssel[0:8, 0:TOK], ACT.Exp, scale=-1.0))
            A.activation(ssel[0:8, 0:TOK], ssel[0:8, 0:TOK], ACT.Ln, bias=1.0).then_inc(s_ln, 1)
            n_lv = 0
            for i in range(NTILE):
                n = ROWS[i]
                cols = slice(i * P, i * P + n)
                for lv in levels(n):
                    n_lv += 1
                    act.wait_ge(s_lv, n_lv)
                    A.activation(X[:, lv, :, 0:n], X[:, lv, :, 0:n], ACT.Exp).then_inc(s_le, 1)
                act.wait_ge(s_lv, n_lv)
                n_lv += 1
                act.wait_ge(s_lv, n_lv)
                A.activation(E[:, :, 0:n], bb[:, :, cols], ACT.Exp).then_inc(s_le, 1)
                act.wait_ge(s_lv, n_lv)
                A.activation(kE[:, :, 0:n], kE[:, :, 0:n], ACT.Exp).then_inc(s_le, 1)
                filled(act, f"kT{i}")
                read("act", f"kT{i}", A.copy(kET[0:n], bank[3][0:n, :].rearrange("p (h k) -> p h k", h=HGH)))
                filled(act, f"ho{i}")
                for h in range(HGH):
                    ins = A.activation(att6[0:n, 0, 0:4, :].rearrange("p a b -> p (a b)"), bank[4][0:n, h * P:(h + 1) * P],
                                       ACT.Square, accum_out=st[0:n, 10 + 4 * i + h:11 + 4 * i + h])
                    ins.then_inc(s_sq, 1)
                    act.wait_ge(s_sq, 4 * i + h + 1)
                root(st[0:n, 30:34], st[0:n, 10 + 4 * i:14 + 4 * i], P).then_inc(s_rs, 1)
            for c in range(2):
                filled(act, f"kcT{c}")
                read("act", f"kcT{c}", A.copy(kcT[:, :, c * P:(c + 1) * P], bank[6 + c][:, :].rearrange("p (a b) -> p a b", a=4)))
            m = 0
            for n_q, q in enumerate(QT):
                n = ROWS[q]
                nb = q + 1 if q < 4 else 3
                L = (q + 1) * P if q < 4 else PAST + NDEC
                for h in range(FH + 1):
                    if h < FH:
                        act.wait_ge(s_pmax, m + 1)
                        A.activation(pp[h % 2][0:n, 0:L], pp[h % 2][0:n, 0:L], ACT.Exp, bias=st[0:n, 50 + h:51 + h],
                                     accum_out=st[0:n, 60 + 8 * (n_q % 2) + h:61 + 8 * (n_q % 2) + h]).then_inc(s_pexp, 1)
                        m += 1
                    if h:
                        hh = h - 1
                        filled(act, f"t{q}{hh}")
                        src = bank[2 + h % 2][:, :].rearrange("p (a b) -> p a b", a=4)
                        if q < 4:
                            ins = A.copy(pT[h % 2][:, 0:nb, :], src[:, 0:nb, :])
                        else:
                            alink(act, A.copy(pT[h % 2][:, 0:2, 0:NDEC], src[:, 0:2, 0:NDEC]))
                            ins = A.copy(pT[h % 2][0:NDEC, 2, 0:NDEC], src[0:NDEC, 2, 0:NDEC])
                        read("act", f"t{q}{hh}", ins)
                taken(act, f"fo{q}")
                if n_q:
                    act.wait_ge(s_fq, n_q)
                A.activation(osq[0:n, :], foxo[0:n, q, :], ACT.Square, accum_out=st[0:n, 80 + n_q:81 + n_q]).then_inc(s_fq, 1)
                act.wait_ge(s_fq, n_q + 1)
                root(st[0:n, 85 + n_q:86 + n_q], st[0:n, 80 + n_q:81 + n_q], HW).then_inc(s_rs, 1)
            for i in range(NTILE):
                n = ROWS[i]
                filled(act, f"m{i}0")
                if i == 0:
                    filled(act, "fo4")
                read("act", f"m{i}0", A.copy(hT[:, 0:4, i * P:i * P + n],
                                             bank[0][:, :].rearrange("p (k t) -> p k t", k=4)[:, :, 0:n]))
            for i in range(NTILE):
                n = ROWS[i]
                act.wait_ge(s_x2, 2 * i + 2)
                if i >= 2:
                    act.wait_ge(s_h2w[i % 2], 16 * (i // 2))
                    filled(act, f"r{i - 2}1")
                A.activation(h2[i % 2][0:n, :], x[0:n, i, :], ACT.Square, accum_out=st[0:n, 90 + i:91 + i]).then_inc(s_x2q, 1)
                act.wait_ge(s_x2q, i + 1)
                root(st[0:n, 95 + i:96 + i], st[0:n, 90 + i:91 + i], D).then_inc(s_rs, 1)
                if i == 0:
                    act.wait_ge(s_sout, 32)
                for c in range(2):
                    filled(act, f"r{i}{c}")
                    read("act", f"r{i}{c}", A.copy(h2T[:, 4 * c:4 * c + 4, 0:n],
                                                   bank[c][:, :].rearrange("p (k t) -> p k t", k=4)[:, :, 0:n]))
            act.wait_ge(s_lx, 1)
            A.activation(prb, prb, ACT.Exp).then_inc(s_lex, 1)
            act.wait_ge(s_rd, 1)
            act.sem_inc(s_yea, 1)
            with act.Fori(0, NE) as e:
                nt = act.value_load(ntile_i[0:1, bass.ds(e, 1)], min_val=1, max_val=CAPT)
                base = act.value_load(base_i[0:1, bass.ds(e, 1)], min_val=0, max_val=MAXT)
                with act.Fori(0, nt) as i:
                    t = base + i
                    act.wait_ge(s_xp, t + 2)
                    A.copy(XT[:, 0:4, :], bank[0][:, :].rearrange("p (k t) -> p k t", k=4)).then_inc(s_xta, 1)
                    for f in range(FT):
                        act.wait_ge(s_gu, t * 4 + (f + 1))
                        A.activation(hs[:, f, :], bank[2 + f][:, 0:P], ACT.Silu).then_inc(s_sil, 1)
                    act.wait_ge(s_yd, t + 1)
                    act.wait_ge(s_yst, t * 16 + 16)
                    A.copy(ysb[:, 0:512], bank[6][:, :]).then_inc(s_yea, 1)
            for i in range(NTILE):
                n = ROWS[i]
                act.wait_ge(s_comb, i + 1)
                A.activation(jk[0:n, :], x[0:n, i, :], ACT.Square, accum_out=st[0:n, 100 + i:101 + i]).then_inc(s_fsq, 1)
                act.wait_ge(s_fsq, i + 1)
                root(st[0:n, 105 + i:106 + i], st[0:n, 100 + i:101 + i], D).then_inc(s_rs, 1)

        def route(dve, V):
            vlink(dve, V.memset(prb, 0.0))
            filled(dve, "lg")
            lb = bank[2][:, 0:NTILE * NE].rearrange("p (n e) -> p n e", e=NE)
            vlink(dve, V.tensor_copy(prb[:, 0:4, :], lb[:, 0:4, :]))
            read("dve", "lg", V.tensor_copy(prb[0:NDEC, 4, :], lb[0:NDEC, 4, :]))
            taken(dve, "lg")
            vlink(dve, V.tensor_reduce(s5[0], prb, AX.X, ALU.max))
            V.tensor_tensor(prb, prb, wide(s5[0]), ALU.subtract).then_inc(s_lx, 1)
            dve.wait_ge(s_lex, 1)
            vlink(dve, V.tensor_reduce(s5[1], prb, AX.X, ALU.add))
            vlink(dve, V.reciprocal(s5[1], s5[1]))
            vlink(dve, V.tensor_tensor(prb, prb, wide(s5[1]), ALU.mult))
            dve.wait_ge(s_brt, 16)
            vlink(dve, V.tensor_tensor(sel, prb, brt.unsqueeze(1).broadcast_to([P, NTILE, NE]), ALU.add))

            def ranks(values, rk, tmp):
                for j in range(4):
                    vlink(dve, V.memset(rk[:, :, j], float(3 - j)))
                for j in range(4):
                    for jj in range(j):
                        vlink(dve, V.tensor_tensor(tmp, values[:, :, jj], values[:, :, j], ALU.is_ge))
                        vlink(dve, V.tensor_tensor(rk[:, :, j], rk[:, :, j], tmp, ALU.add))
                        vlink(dve, V.tensor_tensor(rk[:, :, jj], rk[:, :, jj], tmp, ALU.subtract))

            fours = "p n (g j) -> p (n g) j"
            sel4, rk4, msk4 = (v.rearrange(fours, j=EPG) for v in (sel, t80[0], msk))
            ranks(sel4, rk4, g20[0].rearrange("p n g -> p (n g)"))
            vlink(dve, V.tensor_scalar(msk, t80[0], 2.0, None, ALU.is_lt))
            vlink(dve, V.tensor_tensor(t80[1], sel, msk, ALU.mult))
            vlink(dve, V.tensor_reduce(g20[1].rearrange("p n g -> p (n g)"), t80[1].rearrange(fours, j=EPG), AX.X, ALU.add))
            ranks(g20[1], g20[2], s5[2])
            vlink(dve, V.tensor_scalar(g20[3], g20[2], 0.0, None, ALU.is_equal))
            vlink(dve, V.tensor_tensor(msk4, msk4, g20[3].rearrange("p n g -> p (n g)").unsqueeze(2).broadcast_to([P, NTILE * NG, EPG]), ALU.mult))
            vlink(dve, V.memset(msk[32:64, 4, :], 0.0))
            V.memset(msk[64:128, 4, :], 0.0).then_inc(s_mk, 1)
            dve.wait_ge(s_mk, 1)
            vlink(dve, V.tensor_tensor(gts, prb, msk, ALU.mult))
            vlink(dve, V.tensor_reduce(s5[3], gts, AX.X, ALU.add))
            vlink(dve, V.memset(s5[3][32:64, 4:5], 1.0))
            vlink(dve, V.memset(s5[3][64:128, 4:5], 1.0))
            vlink(dve, V.reciprocal(s5[3], s5[3]))
            vlink(dve, V.tensor_tensor(gts, gts, wide(s5[3]), ALU.mult))
            dve.wait_ge(s_rc, 1)
            filled(dve, "pos")
            pb = bank[3][:, 0:NTILE * NE].rearrange("p (n e) -> p n e", e=NE)
            read("dve", "pos", V.tensor_copy(pmod, pb))
            taken(dve, "pos")
            vlink(dve, V.tensor_tensor(t80[2], pmod, ebase.unsqueeze(1).broadcast_to([P, NTILE, NE]), ALU.add))
            vlink(dve, V.tensor_tensor(t80[2], t80[2], msk, ALU.mult))
            vlink(dve, V.tensor_reduce(s5[4], t80[2], AX.X, ALU.max))
            vlink(dve, V.tensor_tensor(t80[3], t80[2], wide(s5[4]), ALU.is_equal))
            vlink(dve, V.scalar_tensor_tensor(t80[4], msk, 2.0, t80[3], ALU.mult, ALU.subtract))
            vlink(dve, V.tensor_tensor(t80[4], t80[4], msk, ALU.mult))
            vlink(dve, V.tensor_tensor(t80[3], t80[3], gts, ALU.mult))
            vlink(dve, V.tensor_reduce(gA, t80[3], AX.X, ALU.add))
            vlink(dve, V.tensor_tensor(t80[3], gts, t80[3], ALU.subtract))
            vlink(dve, V.tensor_reduce(gB, t80[3], AX.X, ALU.add))
            vlink(dve, V.tensor_scalar(pdiv, pmod, float(P), None, ALU.is_ge))
            for i in range(2, CAPT):
                vlink(dve, V.scalar_tensor_tensor(pdiv, pmod, float(P * i), pdiv, ALU.is_ge, ALU.add))
            vlink(dve, V.scalar_tensor_tensor(pmod, pdiv, -float(P), pmod, ALU.mult, ALU.add))
            for i in range(CAPT):
                vlink(dve, V.scalar_tensor_tensor(d80, pdiv, float(i), msk, ALU.is_equal, ALU.mult))
                for c in range(2):
                    vlink(dve, V.tensor_tensor(rsel[:, :, i, c, :], d80, wide(tokid[:, c * NTILE:(c + 1) * NTILE]), ALU.mult))
                vlink(dve, V.tensor_tensor(rsel[:, :, i, 2, :], d80, t80[4], ALU.mult))
            for e in range(NE):
                if e >= 2:
                    dve.wait_ge(s_ohu, e - 1)
                for n in range(NTILE):
                    ins = V.tensor_scalar(oh[:, e % 2, n, :], iotaj, pmod[:, n, e:e + 1], None, ALU.is_equal)
                ins.then_inc(s_oh, 1)
            filled(dve, "cnt")
            read("dve", "cnt", V.tensor_copy(tf[0][0:1, :], bank[4][0:1, 0:NE]))
            taken(dve, "cnt")
            vlink(dve, V.memset(tf[1][0:1, :], 1.0))
            for i in range(1, CAPT):
                vlink(dve, V.scalar_tensor_tensor(tf[1][0:1, :], tf[0][0:1, :], float(P * i), tf[1][0:1, :], ALU.is_gt, ALU.add))
            vlink(dve, V.tensor_tensor_scan(tf[2][0:1, :], tf[1][0:1, :], tf[1][0:1, :], 0.0, ALU.add, ALU.bypass))
            vlink(dve, V.tensor_copy(ntile_i[0:1, :], tf[1][0:1, :]))
            vlink(dve, V.memset(base_i[0:1, 0:1], 0))
            vlink(dve, V.tensor_copy(base_i[0:1, 1:NE + 1], tf[2][0:1, :]))
            filled(dve, "tab")
            tb = bank[5][:, 0:NE * CAPT * 3].rearrange("p (s c) -> p s c", c=3)
            vlink(dve, V.tensor_scalar(tokf, tb[:, :, 0], float(P), None, ALU.mult))
            vlink(dve, V.tensor_tensor(tokf, tb[:, :, 1], tokf, ALU.add))
            read("dve", "tab", V.tensor_copy(dst1, tb[:, :, 2]))
            taken(dve, "tab")
            vlink(dve, V.tensor_copy(tabi[:, :, 0], tokf))
            vlink(dve, V.tensor_scalar(dst2, dst1, 0.0, float(8 * TOK), ALU.is_equal, ALU.mult))
            vlink(dve, V.scalar_tensor_tensor(dst1, dst1, float(TOK), dst2, ALU.mult, ALU.add))
            vlink(dve, V.scalar_tensor_tensor(dst1, dst1, -float(TOK), tokf, ALU.add, ALU.add))
            V.tensor_copy(tabi[:, :, 1], dst1).then_inc(s_rd, 1)

        @block.vector
        def _(dve):
            V = nc.vector

            def rstd(y, ss, width):
                n, w = y.shape[0], y.shape[1]
                v, t = st[0:n, 110:110 + w], st[0:n, 118:118 + w]
                vlink(dve, V.tensor_scalar(v, ss, 1.0 / width, EPS, ALU.mult, ALU.add))
                vlink(dve, V.tensor_tensor(t, y, y, ALU.mult))
                vlink(dve, V.tensor_tensor(t, t, v, ALU.mult))
                vlink(dve, V.tensor_scalar(t, t, -0.5, 1.5, ALU.mult, ALU.add))
                vlink(dve, V.tensor_tensor(y, y, t, ALU.mult))

            dve.wait_ge(s_iota, 1)
            vlink(dve, V.tensor_scalar(ip, ip, 31, None, ALU.bitwise_and))
            vlink(dve, V.tensor_tensor(ix, ip, it, ALU.bitwise_xor))
            vlink(dve, V.tensor_tensor(mgt, it, ip, ALU.is_gt))
            vlink(dve, V.tensor_copy(mxf, ix))
            for n, half in enumerate(LEVELS[2:]):
                vlink(dve, V.tensor_scalar(mtmp, mxf, float(half), None, ALU.is_ge))
                vlink(dve, V.scalar_tensor_tensor(mtmp, mxf, float(2 * half), mtmp, ALU.is_lt, ALU.mult))
                vlink(dve, V.tensor_tensor(lmask[:, n, :], mtmp, mgt, ALU.mult))
            vlink(dve, V.tensor_scalar(lmask[:, 5, :], mxf, 0.0, None, ALU.is_equal))
            dve.wait_ge(s_badd, 32)
            filled(dve, "ada0")
            read("dve", "ada0", V.tensor_tensor(msb, bank[1][:, :], badd, ALU.add))
            dve.wait_ge(s_mod0, 32)
            dve.wait_ge(s_small, 80)
            for gi in range(2):
                n = P if gi == 0 else NDEC
                sc = mod0[0:n, gi, D:2 * D]
                vlink(dve, V.scalar_tensor_tensor(sc, sc, 1.0, mgain[0:n, :], ALU.add, ALU.mult))
            dve.wait_ge(s_rs, 1)
            rstd(st[:, 5:10], st[:, 0:5], D)
            for i in range(NTILE):
                n, gi = ROWS[i], i // 4
                if i >= 2:
                    filled(dve, f"hT{i - 2}1")
                vlink(dve, V.scalar_tensor_tensor(h1[i % 2][0:n, :], x[0:n, i, :], st[0:n, 5 + i:6 + i],
                                                  mod0[0:n, gi, D:2 * D], ALU.mult, ALU.mult))
                V.tensor_tensor(h1[i % 2][0:n, :], h1[i % 2][0:n, :], mod0[0:n, gi, 0:D], ALU.add).then_inc(s_h1, 1)
            filled(dve, "hT41")
            for h in range(HGH):
                if h:
                    dve.wait_ge(s_kk, h)
                for c in range(2):
                    filled(dve, f"hf{h}{c}")
                    read("dve", f"hf{h}{c}", V.tensor_copy(fr[:, c * HALF:(c + 1) * HALF], bank[4 + 2 * (h % 2) + c][:, 0:HALF]))
                taken(dve, f"hf{h}1")
                dve.wait_ge(s_ln, h + 1)
                vlink(dve, V.scalar_tensor_tensor(lg, fr, 0.0, ex, ALU.min, ALU.subtract))
                V.tensor_tensor(fr, lg, fr, ALU.subtract).then_inc(s_kx, 1)
                for i in range(NTILE):
                    cs = slice(i * P, i * P + ROWS[i])
                    ins = V.tensor_tensor_scan(bb[:, h, cs], lg[:, cs], lg[:, cs], 0.0, ALU.add, ALU.bypass)
                vlink(dve, ins)
            for i in range(NTILE):
                filled(dve, f"hi{i}")
                b = bank[2 + i % 2]
                if i < 4:
                    read("dve", f"hi{i}", V.tensor_copy(v_hg[:, i, :], b[:, :]))
                else:
                    for j in range(4):
                        ins = V.tensor_copy(v_hg[0:NDEC, 4, j * P:(j + 1) * P], b[32 * j:32 * j + 32, 0:P])
                    read("dve", f"hi{i}", ins)
            for i in range(NTILE):
                n = ROWS[i]
                filled(dve, f"fkT{i}")
                read("dve", f"fkT{i}", V.tensor_copy(fkT[:, :, i * P:i * P + n], bank[6][:, :].rearrange("p (a b) -> p a b", a=4)[:, :, 0:n]))
            for i in range(NTILE):
                filled(dve, f"fv{i}")
                b = bank[2 + i % 2]
                if i < 4:
                    read("dve", f"fv{i}", V.tensor_copy(v_fox[:, i, :], b[:, :]))
                else:
                    for j in range(4):
                        ins = V.tensor_copy(v_fox[0:NDEC, 4, j * P:(j + 1) * P], b[32 * j:32 * j + 32, 0:P])
                    read("dve", f"fv{i}", ins)
            for c in range(2):
                filled(dve, f"ff{c}")
                read("dve", f"ff{c}", V.tensor_scalar(cf[0:8, c * HALF:(c + 1) * HALF], bank[c][0:8, 0:HALF], fbias[0:8, 0:1], None, ALU.add))
            filled(dve, "lpT")
            read("dve", "lpT", V.tensor_copy(lf[0:8, SEQ:SEQ + PAST], bank[2][0:8, 0:PAST]))
            dve.wait_ge(s_badd, 64)
            dve.wait_ge(s_modw, 32)
            filled(dve, "ada1")
            read("dve", "ada1", V.tensor_tensor(msb, bank[3][:, :], badd, ALU.add))
            dve.wait_ge(s_ln, HGH + 1)
            taken(dve, "ff1")
            vlink(dve, V.scalar_tensor_tensor(lf[0:8, 0:SEQ], cf[0:8, 0:SEQ], 0.0, ssel[0:8, 0:SEQ], ALU.min, ALU.subtract))
            V.scalar_tensor_tensor(lf[0:8, SEQ + PAST:], cf[0:8, SEQ:TOK], 0.0, ssel[0:8, SEQ:TOK], ALU.min, ALU.subtract).then_inc(s_lf, 1)
            dve.wait_ge(s_lf, 1)
            vlink(dve, V.tensor_tensor_scan(cf[0:8, 0:SEQ], lf[0:8, 0:SEQ], lf[0:8, 0:SEQ], 0.0, ALU.add, ALU.bypass))
            vlink(dve, V.tensor_tensor_scan(cf[0:8, SEQ:], lf[0:8, SEQ:SEQ + 288], lf[0:8, SEQ:SEQ + 288], 0.0, ALU.add, ALU.bypass))
            V.tensor_scalar(cf[0:8, :], cf[0:8, :], -float(FD) ** 0.5, None, ALU.mult).then_inc(s_cf, 1)
            filled(dve, "lfT")
            vlink(dve, V.tensor_copy(lfo[:, 0:4, :], bank[0][:, 0:32].rearrange("p (a b) -> p a b", a=4)))
            read("dve", "lfT", V.tensor_copy(lfo[0:NDEC, 4, :], bank[0][0:NDEC, 32:40]))
            dve.wait_ge(s_badd, 96)
            dve.wait_ge(s_modw, 64)
            filled(dve, "ada2")
            read("dve", "ada2", V.tensor_tensor(msb, bank[1][:, :], badd, ALU.add))
            dve.wait_ge(s_ckw, 32)
            dve.wait_ge(s_lout, 32)
            dve.wait_ge(s_modw, 96)
            both(dve, s_kout)
            vlink(dve, V.memset(attT, 0.0))
            dve.wait_ge(s_qs, HGH)
            dve.wait_ge(s_G, NTILE)
            n_le = 0
            for i in range(NTILE):
                n = ROWS[i]
                t0 = i * P
                bt = bb[:, :, t0:t0 + n]
                for lv in levels(n):
                    H = LEVELS[lv]
                    bv = bt.rearrange("p h (c w) -> p h c w", w=2 * H)
                    Xv = X[:, lv, :, 0:n].rearrange("p h (c w) -> p h c w", w=2 * H)
                    anc = bv[:, :, :, H - 1:H].broadcast_to([P, HGH, n // (2 * H), H])
                    V.tensor_tensor(Xv[:, :, :, 0:H], anc, bv[:, :, :, 0:H], ALU.subtract)
                    V.tensor_tensor(Xv[:, :, :, H:], bv[:, :, :, H:], anc, ALU.subtract).then_inc(s_lv, 1)
                V.tensor_tensor(kE[:, :, 0:n], bt[:, :, n - 1:n].broadcast_to([P, HGH, n]), bt, ALU.subtract).then_inc(s_lv, 1)
                for lv in levels(n):
                    H = LEVELS[lv]
                    n_le += 1
                    dve.wait_ge(s_le, n_le)
                    Xv = X[:, lv, :, 0:n].rearrange("p h (c w) -> p h c w", w=2 * H)
                    kv = kk[:, :, t0:t0 + n].rearrange("p h (c w) -> p h c w", w=2 * H)
                    qv = qs[:, :, t0:t0 + n].rearrange("p h (c w) -> p h c w", w=2 * H)
                    V.tensor_tensor(Xv[:, :, :, 0:H], Xv[:, :, :, 0:H], kv[:, :, :, 0:H], ALU.mult)
                    V.tensor_tensor(Xv[:, :, :, H:], Xv[:, :, :, H:], qv[:, :, :, H:], ALU.mult).then_inc(s_att, 1)
                n_le += 2
                dve.wait_ge(s_le, n_le)
                V.tensor_tensor(qE[:, :, 0:n], E[:, :, 0:n], qs[:, :, t0:t0 + n], ALU.mult)
                V.tensor_tensor(kE[:, :, 0:n], kE[:, :, 0:n], kk[:, :, t0:t0 + n], ALU.mult).then_inc(s_att, 1)
                if i < 4:
                    filled(dve, f"L{i}")
                    Lb = bank[0][:, 0:384].rearrange("p (h c) -> p h c", h=HGH)
                    V.tensor_copy(attT[0:64, :, 64:128], Lb[0:64, :, 0:64])
                    V.tensor_copy(attT[0:32, :, 32:64], Lb[0:32, :, 64:96])
                    read("dve", f"L{i}", V.tensor_copy(attT[64:96, :, 96:128], Lb[64:96, :, 64:96]))
                for c, nm in enumerate(("Da", "Db")):
                    filled(dve, f"{nm}{i}")
                    src = bank[1 + c][0:n, 0:384].rearrange("p (h l t) -> p h l t", h=2, l=6)
                    for hh in range(2):
                        ins = V.tensor_tensor(att6[0:n, hh], src[:, hh], lmask[0:n], ALU.mult)
                    read("dve", f"{nm}{i}", ins)
                    taken(dve, f"{nm}{i}")
                    vlink(dve, V.tensor_reduce(attd[0:n, 2 * c:2 * c + 2, :], att6[0:n].rearrange("p h l t -> p h t l"), AX.X, ALU.add))
                for j in range((n + 31) // 32):
                    ins = V.tensor_copy(attT[32 * j:32 * j + 32, :, 32 * j:32 * j + 32], attd[32 * j:32 * j + 32, :, :])
                ins.then_inc(s_att, 1)
                dve.wait_ge(s_rs, 2 + i)
                rstd(st[0:n, 30:34], st[0:n, 10 + 4 * i:14 + 4 * i], P)
                for h in range(HGH):
                    ins = V.scalar_tensor_tensor(G[0:n, i, h * P:(h + 1) * P], bank[4][0:n, h * P:(h + 1) * P], st[0:n, 30 + h:31 + h],
                                                 G[0:n, i, h * P:(h + 1) * P], ALU.mult, ALU.mult)
                read("dve", f"ho{i}", ins)
                filled(dve, f"S{i}")
                if i == 4:
                    dve.wait_ge(s_S0, 16)
                for h in range(HGH):
                    if i == 0:
                        ins = V.tensor_copy(S[:, h, :], bank[5][:, h * P:(h + 1) * P])
                    else:
                        ins = V.scalar_tensor_tensor(S[:, h, :], S[:, h, :], E[:, h, n - 1:n], bank[5][:, h * P:(h + 1) * P], ALU.mult, ALU.add)
                read("dve", f"S{i}", ins)
                taken(dve, f"S{i}")
            dve.wait_ge(s_ckr, 48)
            for n_q, q in enumerate(QT):
                n = ROWS[q]
                L = (q + 1) * P if q < 4 else PAST + NDEC
                cb = (ckB if q < 4 else ckS)
                dve.wait_ge(s_mask, 1 + n_q)
                for h in range(FH):
                    m = n_q * FH + h
                    filled(dve, f"s{q}{h}")
                    if m >= 2:
                        pq, ph = (QT[(m - 2) // FH], (m - 2) % FH)
                        filled(dve, f"t{pq}{ph}")
                    read("dve", f"s{q}{h}", V.tensor_tensor_reduce(pp[h % 2][0:n, 0:L], bank[h % 2][0:n, 0:L], cb[0:n, h, 0:L],
                                                                   float(FD) ** -0.5, -3e38, ALU.add, ALU.max, st[0:n, 40 + h:41 + h]))
                    taken(dve, f"s{q}{h}")
                    V.tensor_scalar(st[0:n, 50 + h:51 + h], st[0:n, 40 + h:41 + h], -1.0, None, ALU.mult).then_inc(s_pmax, 1)
                filled(dve, f"fo{q}")
                dve.wait_ge(s_pexp, (n_q + 1) * FH)
                ls = 60 + 8 * (n_q % 2)
                vlink(dve, V.reciprocal(st[0:n, ls:ls + 8], st[0:n, ls:ls + 8]))
                for h in range(FH):
                    ins = V.tensor_scalar(foxo[0:n, q, h * FD:(h + 1) * FD], bank[4 + n_q % 2][0:n, h * FD:(h + 1) * FD],
                                          st[0:n, ls + h:ls + h + 1], None, ALU.mult)
                read("dve", f"fo{q}", ins)
                dve.wait_ge(s_rs, 7 + n_q)
                rstd(st[0:n, 85 + n_q:86 + n_q], st[0:n, 80 + n_q:81 + n_q], HW)
                V.scalar_tensor_tensor(foxo[0:n, q, :], foxo[0:n, q, :], st[0:n, 85 + n_q:86 + n_q], fgain[0:n, :], ALU.mult, ALU.mult).then_inc(s_fo, 1)
            for i in range(NTILE):
                n = ROWS[i]
                filled(dve, f"m{i}1")
                read("dve", f"m{i}1", V.tensor_copy(hT[:, 4:8, i * P:i * P + n],
                                                    bank[1][:, :].rearrange("p (k t) -> p k t", k=4)[:, :, 0:n]))
            dve.wait_ge(s_mod1, 96)
            for i in range(4):
                for c in range(2):
                    filled(dve, f"y{i}{c}")
                    if i:
                        dve.wait_ge(s_x2, 2 * (i - 1) + c + 1)
                    read("dve", f"y{i}{c}", V.tensor_tensor(gt[c], bank[4 + (2 * i + c) % 4][:, :],
                                                            mod1[:, 0, c * 512:(c + 1) * 512], ALU.mult))
            filled(dve, "y40")
            dve.wait_ge(s_x2, 8)
            for j in range(4):
                ins = V.tensor_tensor(gt[j // 2][0:32, (j % 2) * 256:(j % 2) * 256 + 256], bank[4][32 * j:32 * j + 32, 0:256],
                                      mod1[0:32, 1, j * 256:(j + 1) * 256], ALU.mult)
            read("dve", "y40", ins)
            for gi in range(2):
                n = P if gi == 0 else NDEC
                sc = mod2[0:n, gi, 0:D]
                vlink(dve, V.scalar_tensor_tensor(sc, sc, 1.0, ngain[0:n, :], ALU.add, ALU.mult))
            for i in range(NTILE):
                n, gi = ROWS[i], i // 4
                dve.wait_ge(s_rs, 12 + i)
                rstd(st[0:n, 95 + i:96 + i], st[0:n, 90 + i:91 + i], D)
                V.scalar_tensor_tensor(h2[i % 2][0:n, :], x[0:n, i, :], st[0:n, 95 + i:96 + i], mod2[0:n, gi, 0:D],
                                       ALU.mult, ALU.mult).then_inc(s_h2a, 1)
            route(dve, V)
            dve.wait_ge(s_rd, 1)
            dve.sem_inc(s_yeb, 1)
            with dve.Fori(0, NE) as e:
                nt = dve.value_load(ntile_i[0:1, bass.ds(e, 1)], min_val=1, max_val=CAPT)
                base = dve.value_load(base_i[0:1, bass.ds(e, 1)], min_val=0, max_val=MAXT)
                with dve.Fori(0, nt) as i:
                    t = base + i
                    dve.wait_ge(s_xp, t + 2)
                    V.tensor_copy(XT[:, 4:8, :], bank[1][:, :].rearrange("p (k t) -> p k t", k=4)).then_inc(s_xtb, 1)
                    for f in range(FT):
                        dve.wait_ge(s_sil, t * 4 + (f + 1))
                        V.tensor_tensor(heT[:, f, :], hs[:, f, :], bank[2 + f][:, P:2 * P], ALU.mult).then_inc(s_he, 1)
                    dve.wait_ge(s_yd, t + 1)
                    dve.wait_ge(s_yst, t * 16 + 16)
                    V.tensor_copy(ysb[:, 512:1024], bank[7][:, :]).then_inc(s_yeb, 1)
            dve.wait_ge(s_ph3, 48)
            for i in range(NTILE):
                n, gi = ROWS[i], i // 4
                A_, B_ = ya[i][0:n, :], yb[i][0:n, :]
                dve.wait_ge(s_ya[i], 32)
                vlink(dve, V.tensor_scalar(A_, A_, gA[0:n, i:i + 1], None, ALU.mult))
                vlink(dve, V.scalar_tensor_tensor(A_, B_, gB[0:n, i:i + 1], A_, ALU.mult, ALU.add))
                vlink(dve, V.tensor_tensor(A_, A_, gateF[0:n, gi, :], ALU.mult))
                V.tensor_tensor(x[0:n, i, :], x[0:n, i, :], A_, ALU.add).then_inc(s_comb, 1)
                dve.wait_ge(s_rs, 17 + i)
                rstd(st[0:n, 105 + i:106 + i], st[0:n, 100 + i:101 + i], D)
                V.scalar_tensor_tensor(A_, x[0:n, i, :], st[0:n, 105 + i:106 + i], fing[0:n, :], ALU.mult, ALU.mult).then_inc(s_fin, 1)

        def fox_values(pe, T, n_q, q, h, end=None):
            n = ROWS[q]
            taken(pe, f"t{q}{h}")
            widths = [P] * (q + 1) if q < 4 else [P, P, NDEC]
            hc = slice(h * FD, (h + 1) * FD)
            for j, w in enumerate(widths):
                if q < 4:
                    v = v_fox[:, j, hc]
                else:
                    v = vc[:, j, hc] if j < 2 else v_fox[0:NDEC, 4, hc]
                ins = T.matmul(bank[4 + n_q % 2][0:n, hc], pT[(h + 1) % 2][0:w, j, 0:n], v, start=(j == 0), stop=(j == len(widths) - 1))
            if end:
                end(f"fo{q}", ins)

        @block.tensor
        def _(pe):
            T = nc.tensor
            issued = []

            def begin(name):
                if before[name]:
                    taken(pe, before[name])

            def end(name, ins):
                assert where[name] == len(issued), (name, len(issued), plan[len(issued)])
                issued.append(name)
                ins.then_inc(pe_done, 1)

            def chunk(b, k4=4):
                return b[:, :].rearrange("p (k t) -> p k t", k=k4)

            pe.wait_ge(s_ident, 1)
            pe.wait_ge(s_c, 32)
            end("cT", T.transpose(bank[0][:, 0:16], crow[0:16, :], ident[0:16, 0:16]))

            def ada(r, b):
                begin(f"ada{r}")
                for k in range(KT):
                    loaded(pe, f"ada{r}_{k}")
                    w = wslot(f"ada{r}_{k}", SLOT)[:, 0, :]
                    for j in range(4):
                        ins = T.matmul(bank[b][32 * j:32 * j + 32, :], cpad[:, k, :], w[:, j * 512:(j + 1) * 512],
                                       start=(k == 0), stop=(k == KT - 1))
                end(f"ada{r}", ins)

            def turned(name, b, src, n, blocks):
                begin(name)
                for j in range(blocks):
                    ins = T.transpose(chunk(bank[b])[:, j, 0:n], src[0:n, j * P:(j + 1) * P], ident[0:n, 0:n])
                end(name, ins)

            def feature_major(name, wname):
                loaded(pe, wname)
                w = wslot(wname, HW)
                for h in range(4):
                    for c in range(2):
                        b = 4 + 2 * (h % 2) + c
                        begin(f"{name}{h}{c}")
                        for k in range(KT):
                            ins = T.matmul(bank[b][:, 0:HALF], w[:, k, h * P:(h + 1) * P], hT[:, k, c * HALF:(c + 1) * HALF],
                                           start=(k == 0), stop=(k == KT - 1))
                        end(f"{name}{h}{c}", ins)

            def token_major(name, i, b):
                w = wslot(name, HW)
                begin(f"{name}{i}")
                for k in range(KT):
                    if i < 4:
                        ins = T.matmul(bank[b][:, :], hT[:, k, i * P:(i + 1) * P], w[:, k, :], start=(k == 0), stop=(k == KT - 1))
                    else:
                        for j in range(4):
                            ins = T.matmul(bank[b][32 * j:32 * j + 32, 0:P], hT[:, k, SEQ:], w[:, k, j * P:(j + 1) * P],
                                           start=(k == 0), stop=(k == KT - 1))
                end(f"{name}{i}", ins)

            taken(pe, "cT")
            ada(0, 1)
            for i in range(NTILE):
                pe.wait_ge(s_h1, i + 1)
                for c in range(2):
                    turned(f"hT{i}{c}", 2 + c, h1[i % 2][:, c * 512:(c + 1) * 512], ROWS[i], 4)
            taken(pe, "hT41")
            feature_major("hq", "hq")
            loaded(pe, "hg")
            for i in range(NTILE):
                token_major("hg", i, 2 + i % 2)
            feature_major("hf", "hf")
            loaded(pe, "hi")
            for i in range(NTILE):
                token_major("hi", i, 2 + i % 2)
            loaded(pe, "fk")
            for i in range(NTILE):
                token_major("fk", i, 4 + i % 2)
                if i:
                    taken(pe, f"fk{i - 1}")
                    turned(f"fkT{i - 1}", 6, fkt[(i - 1) % 2], ROWS[i - 1], 4)
            taken(pe, "fk4")
            turned("fkT4", 6, fkt[0], NDEC, 4)
            loaded(pe, "fv")
            for i in range(NTILE):
                token_major("fv", i, 2 + i % 2)
            feature_major("fq", "fq")
            pe.wait_ge(s_small, 80)
            for c in range(2):
                begin(f"ff{c}")
                for k in range(KT):
                    ins = T.matmul(bank[c][0:FH, 0:HALF], wff[:, k, :], hT[:, k, c * HALF:(c + 1) * HALF],
                                   start=(k == 0), stop=(k == KT - 1))
                end(f"ff{c}", ins)
            begin("lpT")
            for j in range(2):
                ins = T.transpose(bank[2][0:FH, j * P:(j + 1) * P], lpast[:, j, :], ident[:, :])
            end("lpT", ins)
            ada(1, 3)
            begin("lfT")
            pe.wait_ge(s_lf, 1)
            for i in range(NTILE):
                n = ROWS[i]
                c0 = i * P if i < 4 else SEQ + PAST
                ins = T.transpose(bank[0][0:n, i * FH:(i + 1) * FH], lf[0:8, c0:c0 + n], ident[0:8, 0:8])
            end("lfT", ins)
            ada(2, 1)

            for i in range(NTILE):
                n, t0 = ROWS[i], i * P
                lvs = levels(n)
                if i < 4:
                    begin(f"L{i}")
                    Lb = bank[0][:, 0:384].rearrange("p (h c) -> p h c", h=HGH)
                    pe.wait_ge(s_att, operands(i, 2))
                    for h in range(HGH):
                        T.matmul(Lb[0:64, h, 0:64], X[:, 0, h, 0:64], X[:, 0, h, 64:128], start=True, stop=True)
                        for j in range(2):
                            ins = T.matmul(Lb[64 * j:64 * j + 32, h, 64:96], X[:, 1, h, 64 * j:64 * j + 32],
                                           X[:, 1, h, 64 * j + 32:64 * j + 64], start=True, stop=True)
                    end(f"L{i}", ins)
                for c, nm in enumerate(("Da", "Db")):
                    begin(f"{nm}{i}")
                    pe.wait_ge(s_att, operands(i, len(lvs)))
                    src = bank[1 + c][:, 0:384].rearrange("p (h l t) -> p h l t", h=2, l=6)
                    for hh in range(2):
                        h = 2 * c + hh
                        for lv in range(2, 8):
                            for j in range(n // 32):
                                b = slice(32 * j, 32 * j + 32)
                                tb = slice(t0 + 32 * j, t0 + 32 * j + 32)
                                left, right = (X[:, lv, h, b], X[:, lv, h, b]) if lv < 7 else (kk[:, h, tb], qs[:, h, tb])
                                ins = T.matmul(src[32 * j:32 * j + 32, hh, lv - 2, :], left, right, start=True, stop=True)
                    end(f"{nm}{i}", ins)
                begin(f"kT{i}")
                pe.wait_ge(s_att, operands(i, len(lvs) + 1))
                for h in range(HGH):
                    ins = T.transpose(chunk(bank[3])[0:n, h, :], kE[:, h, 0:n], ident[:, :])
                end(f"kT{i}", ins)
                begin(f"ho{i}")
                pe.wait_ge(s_att, operands(i, len(lvs) + 2))
                if 0 < i < 4:
                    taken(pe, f"S{i - 1}")
                if i == 4:
                    pe.wait_ge(s_S0, 16)
                for h in range(HGH):
                    o = bank[4][0:n, h * P:(h + 1) * P]
                    if i:
                        T.matmul(o, qE[:, h, 0:n], S[:, h, :], start=True, stop=False)
                    ins = T.matmul(o, attT[0:n, h, 0:n], v_hg[0:n, i, h * P:(h + 1) * P], start=(i == 0), stop=True)
                end(f"ho{i}", ins)
                begin(f"S{i}")
                taken(pe, f"kT{i}")
                for h in range(HGH):
                    ins = T.matmul(bank[5][:, h * P:(h + 1) * P], kET[0:n, h, :], v_hg[0:n, i, h * P:(h + 1) * P], start=True, stop=True)
                end(f"S{i}", ins)

            pe.wait_ge(s_cache, 32)
            for c in range(2):
                turned(f"kcT{c}", 6 + c, kc[:, c, :], P, 4)
            m = 0
            for n_q, q in enumerate(QT):
                n = ROWS[q]
                qc = slice(q * P, q * P + n)
                begin(f"fo{q}")
                for h in range(FH + 1):
                    if h < FH:
                        begin(f"s{q}{h}")
                        r = slice(64 * (h % 2), 64 * (h % 2) + 64)
                        lhs = fqT[r, h // 2, qc]
                        if q < 4:
                            ins = T.matmul(bank[h % 2][0:n, 0:(q + 1) * P], lhs, fkT[r, h // 2, 0:(q + 1) * P], start=True, stop=True)
                        else:
                            taken(pe, "kcT1")
                            T.matmul(bank[h % 2][0:n, 0:PAST], lhs, kcT[r, h // 2, :], start=True, stop=True)
                            ins = T.matmul(bank[h % 2][0:n, PAST:PAST + n], lhs, fkT[r, h // 2, qc], start=True, stop=True)
                        end(f"s{q}{h}", ins)
                    if h:
                        hh = h - 1
                        begin(f"t{q}{hh}")
                        m += 1
                        pe.wait_ge(s_pexp, m)
                        tb = chunk(bank[2 + h % 2])
                        widths = [P] * (q + 1) if q < 4 else [P, P, NDEC]
                        for j, w in enumerate(widths):
                            ins = T.transpose(tb[0:w, j, 0:n], pp[hh % 2][0:n, j * P:j * P + w], ident[0:n, 0:n])
                        end(f"t{q}{hh}", ins)
                        if hh:
                            fox_values(pe, T, n_q, q, hh - 1)
                fox_values(pe, T, n_q, q, FH - 1, end)

            for i in range(NTILE):
                n = ROWS[i]
                pe.wait_ge(s_fo, QT.index(i) + 1)
                turned(f"m{i}0", 0, G[:, i, :], n, 4)
                turned(f"m{i}1", 1, foxo[:, i, :], n, 4)
            taken(pe, "m40")
            taken(pe, "m41")
            for k in range(4):
                loaded(pe, f"wo{k}")
            for i in range(4):
                for c in range(2):
                    b = bank[4 + (2 * i + c) % 4]
                    begin(f"y{i}{c}")
                    for k in range(KT):
                        ins = T.matmul(b[:, :], hT[:, k, i * P:(i + 1) * P], wslot(f"wo{k // 2}", D)[:, k % 2, c * 512:(c + 1) * 512],
                                       start=(k == 0), stop=(k == KT - 1))
                    end(f"y{i}{c}", ins)
            begin("y40")
            for k in range(KT):
                for j in range(4):
                    ins = T.matmul(bank[4][32 * j:32 * j + 32, 0:256], hT[:, k, SEQ:], wslot(f"wo{k // 2}", D)[:, k % 2, j * 256:(j + 1) * 256],
                                   start=(k == 0), stop=(k == KT - 1))
            end("y40", ins)

            pe.wait_ge(s_mod1, 96)
            begin("lg")
            for i in range(NTILE):
                n = ROWS[i]
                pe.wait_ge(s_h2, i + 1)
                for c in range(2):
                    turned(f"r{i}{c}", c, h2[i % 2][:, c * 512:(c + 1) * 512], n, 4)
                taken(pe, f"r{i}0")
                taken(pe, f"r{i}1")
                for k in range(KT):
                    ins = T.matmul(bank[2][0:n, i * NE:(i + 1) * NE], h2T[:, k, 0:n], wrt[:, k, :], start=(k == 0), stop=(k == KT - 1))
            end("lg", ins)
            begin("pos")
            pe.wait_ge(s_mk, 1)
            pe.wait_ge(s_rc, 1)
            for i in range(NTILE):
                for j in range(i + 1):
                    ins = T.matmul(bank[3][:, i * NE:(i + 1) * NE], tri if j == i else ones, msk[:, j, :], start=(j == 0), stop=(j == i))
            end("pos", ins)
            begin("cnt")
            for j in range(NTILE):
                ins = T.matmul(bank[4][0:1, 0:NE], ones[:, 0:1], msk[:, j, :], start=(j == 0), stop=(j == NTILE - 1))
            end("cnt", ins)
            begin("tab")
            tb = bank[5][:, 0:NE * CAPT * 3].rearrange("p (e i c) -> p e i c", i=CAPT, c=3)
            for e in range(NE):
                pe.wait_ge(s_oh, e + 1)
                for j in range(NTILE):
                    ins = T.matmul(tb[:, e, :, :], oh[:, e % 2, j, :], rsel[:, j, :, :, e], start=(j == 0), stop=(j == NTILE - 1))
                if e < NE - 1:
                    ins.then_inc(s_ohu, 1)
            end("tab", ins)

            taken(pe, "tab")
            pe.wait_ge(s_rd, 1)
            with pe.Fori(0, NE // 2) as pair:
                for par in range(2):
                    Wg, Wu, Wd = wexp(par)
                    pe.wait_ge(s_we[par], pair * 48 + 48)
                    nt = pe.value_load(ntile_i[0:1, bass.ds(pair * 2 + par, 1)], min_val=1, max_val=CAPT)
                    base = pe.value_load(base_i[0:1, bass.ds(pair * 2 + par, 1)], min_val=0, max_val=MAXT)
                    with pe.Fori(0, nt) as i:
                        t = base + i
                        pe.wait_ge(s_gath, t * 16 + 16)
                        for k in range(KT):
                            ins = T.transpose(chunk(bank[k // 4])[:, k % 4, :], xg[:, k * P:(k + 1) * P], ident[:, :])
                        ins.then_inc(s_xp, 1)
                        for f in range(FT):
                            if f == 0:
                                pe.wait_ge(s_xta, t + 1)
                            for w, off in ((Wg, 0), (Wu, P)):
                                for k in range(KT):
                                    if f == 0 and off == 0 and k == 4:
                                        pe.wait_ge(s_xtb, t + 1)
                                    ins = T.matmul(bank[2 + f][:, off:off + P], w[:, k, f * P:(f + 1) * P], XT[:, k, :],
                                                   start=(k == 0), stop=(k == KT - 1))
                            ins.then_inc(s_gu, 1)
                        pe.wait_ge(s_yea, t + 1)
                        pe.wait_ge(s_yeb, t + 1)
                        for f in range(FT):
                            pe.wait_ge(s_he, t * 4 + (f + 1))
                            for c in range(2):
                                ins = T.matmul(bank[6 + c][:, :], heT[:, f, :], Wd[:, f, c * 512:(c + 1) * 512],
                                               start=(f == 0), stop=(f == FT - 1))
                        ins.then_inc(s_yd, 1)


_INS = ['x_prompt', 'x_sample', 'cache_fox_k', 'cache_fox_v', 'cache_fox_logf', 'state_hgrn', 'c_prompt', 'c_sample',
        'norm_mix_gain', 'norm_ffn_gain', 'w_ada', 'b_ada', 'w_in', 'hg_lower_bounds', 'hg_norm_gain', 'fox_f_bias',
        'fox_out_gain', 'w_out', 'w_router', 'b_router', 'w_exp_gate', 'w_exp_up', 'w_exp_down', 'final_norm_gain']
_OUTS = [('y_prompt', (1, 512, 1024)), ('y_sample', (1, 32, 1024)), ('hgrn_state_prompt', (1, 1, 4, 128, 128)),
         ('fox_k_prompt', (1, 1, 512, 8, 64)), ('fox_v_prompt', (1, 1, 512, 8, 64)), ('fox_logf_prompt', (1, 1, 512, 8)),
         ('hgrn_state_sample', (1, 1, 4, 128, 128)), ('fox_k_sample', (1, 1, 32, 8, 64)), ('fox_v_sample', (1, 1, 32, 8, 64)),
         ('fox_logf_sample', (1, 1, 32, 8))]


def kernel(**inputs):
    import numpy as _np
    import concourse.bacc as _bacc
    from concourse import mybir as _mybir
    from concourse.bass_utils import run_bass_kernel_spmd as _run

    nc = _bacc.Bacc("TRN2", target_bir_lowering=False, num_devices=1)
    arrays, args, outs = {}, {}, {}
    for name in _INS:
        if name == 'hg_lower_bounds':
            continue
        v = _np.ascontiguousarray(inputs[name])
        arrays[f"in_{name}"] = v
        args[name] = nc.dram_tensor(f"in_{name}", v.shape, _mybir.dt.from_np(v.dtype), kind="ExternalInput").ap()
    for name, shape in _OUTS:
        outs[name] = nc.dram_tensor(f"out_{name}", shape, _mybir.dt.float32, kind="ExternalOutput").ap()
    build(nc, args, outs)
    r = _run(nc, [arrays], core_ids=[0])
    return tuple(r.results[0][f"out_{name}"] for name, _ in _OUTS)
```

```python
from contextlib import ExitStack

import concourse.bass as bass
from concourse import mybir

F32 = mybir.dt.float32
I32 = mybir.dt.int32
ALU = mybir.AluOpType
ACT = mybir.ActivationFunctionType
AX = mybir.AxisListType

P = 128
D = 1024
KT = D // P
SEQ, NDEC, PAST = 512, 32, 256
TOK = SEQ + NDEC
HALF = TOK // 2
NTILE = 5
ROWS = [P] * 4 + [NDEC]
HGH, HW = 4, 512
FH, FD = 8, 64
NE, NG, EPG = 16, 4, 4
DE = 512
FT = DE // P
ET = 64
CAPT = (TOK + ET - 1) // ET
MAXT = NE + 2 * TOK // ET
EPS = 1e-6
SLOT = 2048
LEVELS = [64, 32, 16, 8, 4, 2, 1]
NEG = -1e30


def wide(ap):
    return ap.unsqueeze(2).broadcast_to([P, NTILE, NE])


def levels(n):
    return [i for i, half in enumerate(LEVELS) if 2 * half <= n]


def bcast(ap, parts):
    return ap.partition_broadcast(parts)


def build(nc, a, out):
    ctx = ExitStack()
    with ctx:
        def sb(name, shape, dt=F32):
            return ctx.enter_context(nc.sbuf_tensor(name, shape, dt))

        def sem(name):
            return ctx.enter_context(nc.semaphore(name))

        W = sb("weights", [P, 12 * SLOT])
        x = sb("x", [P, NTILE, D])
        hT = sb("hT", [P, KT, TOK])
        R = sb("R", [P, 18560])
        ident = sb("ident", [P, P])
        cpad = sb("cpad", [P, KT, 32])
        st = sb("stats", [P, 160])
        bank = [ctx.enter_context(nc.psum_tensor(f"bank{i}", [P, 512], F32)) for i in range(8)]

        def view(t, off, *shape):
            n = 1
            for s in shape:
                n *= s
            v = t[:, off:off + n]
            if len(shape) == 2:
                v = v.rearrange("p (a b) -> p a b", b=shape[1])
            if len(shape) == 3:
                v = v.rearrange("p (a b c) -> p a b c", b=shape[1], c=shape[2])
            return v

        hflat = hT[:, :, :].rearrange("p k t -> p (k t)")
        WA = 8 * SLOT
        qs = view(R, 0, HGH, TOK)
        kk = view(R, 2176, HGH, TOK)
        bb = view(R, 4352, HGH, TOK)
        v_hg = view(R, 6528, NTILE, HW)
        G = view(R, 9088, NTILE, HW)
        v_fox = view(R, 11648, NTILE, HW)
        fqT = view(R, 14208, 4, TOK)
        fkT = view(R, 16384, 4, TOK)
        foxo = v_hg
        hgrn_at = [0, 4 * SLOT]
        X = [view(W, o, 7, HGH, P) for o in hgrn_at]
        E = [view(W, o + 3584, HGH, P) for o in hgrn_at]
        qE = [view(W, o + 4096, HGH, P) for o in hgrn_at]
        kE = [view(W, o + 4608, HGH, P) for o in hgrn_at]
        attT = [view(W, 4 * SLOT + 5120 + 512 * n, HGH, P) for n in range(2)]
        att6s = view(W, WA + 5632, P)
        S_sample = view(W, 4 * SLOT + 6144, HGH, P)
        kET = view(W, WA + 5120, HGH, P)
        att6 = view(W, WA + 6144, 2, 6, 32)
        attd = view(W, WA + 6528, HGH, 32)
        S = view(W, WA + 6656, HGH, P)
        hgain = view(W, WA + 7168, HW)
        lmask = view(W, WA + 7680, 6, 32)
        ip, it, ix = (view(W, WA + 6144 + 32 * n, 32).bitcast(I32) for n in range(3))
        mgt, mxf, mtmp = (view(W, WA + 6240 + 32 * n, 32) for n in range(3))
        h1 = [view(W, WA, D), view(W, WA + D, D)]
        fr = view(W, WA, TOK)
        ex = view(W, WA + 544, TOK)
        lg = view(W, WA + 1088, TOK)
        fkt = [view(W, WA + 1632, HW), view(W, WA + 2144, HW)]
        cf = view(W, WA + 3584, 800)
        msb = view(W, WA + 4608, HW)
        badd = view(W, WA + 5120, HW)
        ssel = view(W, WA + 2656, 800)
        lfo = view(W, WA + 3456, NTILE, FH)
        lpast = view(W, WA + 3496, 2, FH)
        fbias = view(W, WA + 3512, 1)
        crow = view(R, 5120, P)
        modT = view(R, 5248, 2, 2 * KT)
        gainT = view(R, 5280, KT)
        ckB = view(W, WA, FH, SEQ)
        ckS = view(W, 5120, FH, PAST + NDEC)
        fgain = view(W, 7424, HW)
        kc = view(hflat, 0, 2, HW)
        vc = view(hflat, D, 2, HW)
        kcT = view(hflat, 2 * D, 4, PAST)
        lf = view(hflat, 3 * D, 800)
        pp = [view(W, 0, 512), view(W, 512, 512)]
        pT = [view(W, 1024, 4, P), view(W, 1536, 4, P)]
        osq = view(W, 2048, HW)
        wff = view(W, WA + 7872, KT, FH)
        mod1 = view(R, 0, 2, 2 * D)
        mod2 = view(R, 11648, 2, 2 * D)
        ngain = view(R, 15744, D)
        wrt = view(R, 16768, KT, NE)
        gt = [view(W, WA + 3072, 512), view(W, WA + 3584, 512)]
        h2 = [view(R, 6528 + n * D, D) for n in range(NTILE)]
        x2sq = [view(W, WA + 4096, D), view(W, WA + 5120, D)]
        h2T = [view(W, WA + 6144, KT, P), view(W, WA + 7168, KT, P)]

        def dram(name, shape, dt=F32):
            return nc.dram_tensor(name, shape, dt, kind="Internal").ap()
        mod_d = dram("mod_d", (2, 6 * D))
        ck_d = dram("ck_d", (FH, SEQ))
        cks_d = dram("cks_d", (FH, PAST + NDEC))
        h2_d = dram("h2_d", (TOK, D))
        tab_d = dram("tab_d", ((MAXT + 2) * ET, 2), I32)
        y_d = dram("y_d", (2 * TOK, D))

        plan, where = [], {}

        def grp(name, b, eng):
            where[name] = len(plan)
            plan.append((name, b, eng))

        grp("cT", 0, "act")
        for i in range(NTILE):
            grp(f"hT{i}0", 2 + 2 * (i % 2), "act")
            grp(f"hT{i}1", 3 + 2 * (i % 2), "act")
        grp("ada0", 1, "dve")
        grp("modT", 0, "dve")
        for h in range(HGH):
            grp(f"hq{h}0", 4 + 2 * (h % 2), "act")
            grp(f"hq{h}1", 5 + 2 * (h % 2), "act")
        for i in range(NTILE):
            grp(f"hg{i}", 2 + i % 2, "act")
        for h in range(HGH):
            grp(f"hf{h}0", 4 + 2 * (h % 2), "dve")
            grp(f"hf{h}1", 5 + 2 * (h % 2), "dve")
        grp("ada1", 1, "dve")
        for i in range(NTILE):
            grp(f"hi{i}", 2 + i % 2, "dve")
        for i in range(NTILE):
            grp(f"fk{i}", 4 + i % 2, "act")
            if i:
                grp(f"fkT{i - 1}", 6, "dve")
        grp("fkT4", 6, "dve")
        grp("ada2", 0, "dve")
        for i in range(NTILE):
            grp(f"fv{i}", 2 + i % 2, "dve")
        for h in range(4):
            grp(f"fq{h}0", 4 + 2 * (h % 2), "act")
            grp(f"fq{h}1", 5 + 2 * (h % 2), "act")
        grp("ff0", 0, "dve")
        grp("ff1", 1, "dve")
        grp("lpT", 2, "dve")
        grp("lfT", 3, "dve")
        for i in range(-1, NTILE):
            if i + 1 < NTILE:
                if i + 1 < 4:
                    grp(f"L{i + 1}", 0, "dve")
                grp(f"Da{i + 1}", 1, "dve")
                grp(f"Db{i + 1}", 2, "dve")
            if i >= 0:
                grp(f"kT{i}", 3, "act")
                grp(f"ho{i}", 4, "dve")
                grp(f"S{i}", 5, "dve")
        grp("kcT0", 6, "act")
        grp("kcT1", 7, "act")
        QT = [3, 2, 1, 0, 4]
        for n, q in enumerate(QT):
            for h in range(FH + 1):
                if h < FH:
                    grp(f"s{q}{h}", h % 2, "dve")
                if h == 1 and n:
                    grp(f"fo{QT[n - 1]}", 4 + (n - 1) % 2, "dve")
                if h:
                    grp(f"t{q}{h - 1}", 2 + h % 2, "act")
        grp(f"fo{QT[4]}", 4, "dve")
        for i in range(NTILE):
            grp(f"m{i}0", 0, "act")
            grp(f"m{i}1", 1, "dve")
        for i in range(NTILE):
            for c in range(2 if i < 4 else 1):
                grp(f"y{i}{c}", 4 + (2 * i + c) % 4, "dve")
            if i >= 2:
                grp(f"r{i - 2}0", 0, "act")
                grp(f"r{i - 2}1", 1, "act")
        for i in (3, 4):
            grp(f"r{i}0", 0, "act")
            grp(f"r{i}1", 1, "act")
        grp("lg", 2, "dve")
        grp("cnt", 4, "dve")
        grp("pos", 3, "dve")

        pe_done = sem("pe_done")
        read_out = {"act": sem("act_read_out"), "dve": sem("dve_read_out")}
        rank, before, last = {}, {}, {}
        count = {"act": 0, "dve": 0}
        for name, b, eng in plan:
            count[eng] += 1
            rank[name] = (eng, count[eng])
            before[name] = last.get(b)
            last[b] = name

        def filled(eng, name):
            eng.wait_ge(pe_done, where[name] + 1)

        def taken(eng, name):
            who, n = rank[name]
            eng.wait_ge(read_out[who], n)

        order = {"act": [], "dve": []}

        def read(eng, name, ins):
            assert rank[name] == (eng, len(order[eng]) + 1), name
            order[eng].append(name)
            ins.then_inc(read_out[eng], 1)

        s_ident = sem("ident_ready")
        s_iota = sem("mask_iotas_ready")
        s_cpad = sem("cpad_zeroed")
        s_x = [sem(f"x_in{i}") for i in range(NTILE)]
        s_c = sem("c_in")
        s_small = sem("small_in")
        s_badd = sem("ada_bias_in")
        s_modw = sem("mod_rows_out")
        s_w = [sem(f"slot{i}_in") for i in range(8)]
        s_ss = sem("x_squares_summed")
        s_h1 = sem("x_normalised")
        s_ma0 = sem("mod_rows0_ready")
        s_modT = sem("modT_ready")
        s_hma = sem("hT_low_modulated")
        s_hmd = sem("hT_high_modulated")
        s_qs = sem("q_scaled")
        s_G = sem("gate_gained")
        s_ln = sem("softplus_ready")
        s_kx = sem("k_exponent_ready")
        s_kk = sem("k_ready")
        s_lf = sem("fox_logf_ready")
        s_cf = sem("fox_cumsum_ready")
        s_kout = [sem(f"fox_k_stored{i}") for i in range(2)]
        s_vout = sem("fox_v_stored")
        s_lout = sem("fox_logf_stored")
        s_ckw = sem("ck_rows_out")
        s_ckr = sem("ck_rows_in")
        s_cache = sem("caches_in")
        s_sout = sem("state_stored")
        s_S0 = sem("sample_state_in")
        s_lmask = sem("level_masks_ready")
        s_lv = sem("level_exponents")
        s_le = sem("level_exps")
        s_zero = sem("attention_zeroed")
        s_xm = sem("level_operands_ready")
        s_qk = sem("qE_kE_ready")
        s_att = sem("attention_ready")
        s_sq = sem("ho_squares_summed")
        s_mask = sem("ck_masked")
        s_pmax = sem("fox_max_ready")
        s_pexp = sem("fox_exp_ready")
        s_fq = sem("fox_squares_summed")
        s_fo = sem("fox_out_ready")
        s_mod1 = sem("mod12_in")
        s_x2 = sem("x2_half_ready")
        s_x2q = sem("x2_squares_summed")
        s_h2a = sem("h2_scaled")
        s_h2 = sem("h2_ready")
        s_h2w = [sem(f"h2_stored{i}") for i in range(2)]
        s_brt = sem("router_bias_in")
        s_rc = sem("routing_constants_ready")
        s_lx = sem("logits_centered")
        s_lex = sem("logits_exp")
        s_mk = sem("expert_mask_ready")
        s_tfill = sem("table_fill_ready")
        s_tab0 = sem("table_filled")
        s_dst = sem("table_rows_ready")
        s_tabw = sem("table_written")
        s_tab = sem("table_in")
        s_rd = sem("routing_ready")
        s_rs = sem("inverse_roots")
        s_dv = sem("dve_step")
        s_ac = sem("act_step")
        s_pl = sem("pool_step")

        steps = {"dve": 0, "act": 0, "pool": 0}

        def vlink(dve, ins):
            steps["dve"] += 1
            ins.then_inc(s_dv, 1)
            dve.wait_ge(s_dv, steps["dve"])

        def alink(act, ins):
            steps["act"] += 1
            ins.then_inc(s_ac, 1)
            act.wait_ge(s_ac, steps["act"])

        def plink(pool, ins):
            steps["pool"] += 1
            ins.then_inc(s_pl, 1)
            pool.wait_ge(s_pl, steps["pool"])

        def both(eng, pair):
            eng.wait_ge(pair[0], 48)
            eng.wait_ge(pair[1], 32)

        def level_operands(i, n):
            return sum(len(levels(ROWS[j])) for j in range(i)) + n

        block = ctx.enter_context(nc.Block())
        w_ada = a["w_ada"].rearrange("l (k p) n -> p (l k) n", p=P)
        w_in = a["w_in"].rearrange("l (k p) n -> p (l k) n", p=P)
        w_out = a["w_out"].rearrange("l (k p) n -> p (l k) n", p=P)
        HQ, HF, HI, HG, FQ, FK, FV, FF = (512 * i for i in range(8))

        ring = [(f"ada0_{k}", k % 6, 1) for k in range(KT)]
        ring += [("hq", 6, 2), ("hg", 4, 2)] + [(f"ada1_{k}", k, 1) for k in range(4)]
        ring += [("hf", 6, 2), ("hi", 4, 2)] + [(f"ada1_{k}", k - 4, 1) for k in range(4, 8)]
        ring += [("fk", 6, 2)] + [(f"ada2_{k}", k, 1) for k in range(4)]
        ring += [("fv", 4, 2)] + [(f"ada2_{k}", k - 4, 1) for k in range(4, 8)]
        ring += [("fq", 6, 2)]
        ring += [(f"wo{k}", 4 + k, 1) for k in range(4)]
        lastuse = {"hq": "hq31", "hg": "hg4", "hf": "hf31", "hi": "hi4", "fk": "fk4", "fv": "fv4", "fq": "fq31"}
        for r, first in enumerate(("hT00", "hf00", "fk0")):
            for k in range(KT):
                lastuse[f"ada{r}_{k}"] = first if k < (2 if r == 0 else 4) else f"ada{r}"
        loads = {}
        slot_count = [0] * 8
        slot_owner = [None] * 8
        for name, s, n in ring:
            slot_count[s] += 16
            loads[name] = (s, slot_count[s], n, [slot_owner[j] for j in range(s, s + n)])
            for j in range(s, s + n):
                slot_owner[j] = name

        def loaded(eng, name):
            s, value, _, _ = loads[name]
            eng.wait_ge(s_w[s], value)

        def wslot(name, width):
            s, _, n, _ = loads[name]
            return view(W, s * SLOT, n * SLOT // width, width)

        s_we = [sem(f"expert_buffer{n}_in") for n in range(3)]
        s_gath = sem("rows_gathered")
        s_idx = sem("index_copied")
        s_xp = sem("rows_transposed")
        s_xta = sem("xT_low_ready")
        s_xtb = sem("xT_high_ready")
        s_gu = sem("gate_up_half_done")
        s_sil = sem("silu_done")
        s_he = sem("hidden_ready")
        s_begun = sem("transposes_begun")
        s_ht = sem("hidden_transposed")
        s_hc = sem("hiddenT_ready")
        s_yd = sem("down_done")
        s_yea = sem("y_low_read")
        s_yeb = sem("y_high_read")
        s_yst = sem("y_stored")
        xg = view(R, 0, D)
        XT = view(R, D, KT, ET)
        heT = view(R, D + 512, FT, ET)
        hs = view(R, 2 * D, DE)
        he = view(R, 2 * D + 512, DE)
        ysb = view(R, 3 * D, D)
        T0 = 4 * D
        prb = view(R, T0, NTILE, NE)
        sel = view(R, T0 + 80, NTILE, NE)
        msk = view(R, T0 + 160, NTILE, NE)
        gts = view(R, T0 + 240, NTILE, NE)
        t80 = [view(R, T0 + 320 + 80 * n, NTILE, NE) for n in range(6)]
        g20 = [view(R, T0 + 800 + 20 * n, NTILE, NG) for n in range(8)]
        brt = view(R, T0 + 960, NE)
        s5 = [view(R, T0 + 976 + 8 * n, NTILE) for n in range(8)]
        gA, gB = view(R, T0 + 1040, NTILE), view(R, T0 + 1048, NTILE)
        tri = view(R, T0 + 1072, P)
        ones = view(R, T0 + 1200, P)
        tf = [view(R, T0 + 1328 + 16 * n, NE) for n in range(4)]
        cnt_i = view(R, T0 + 1392, NE).bitcast(I32)
        ntile_i = view(R, T0 + 1408, NE).bitcast(I32)
        base_i = view(R, T0 + 1424, NE + 1).bitcast(I32)
        idx1 = view(R, T0 + 1441, 1).bitcast(I32)
        idx2 = view(R, T0 + 1442, 1).bitcast(I32)
        dst = view(R, T0 + 1444, 2 * NTILE)
        dst_i = view(R, T0 + 1454, 2 * NTILE).bitcast(I32)
        entry = view(R, T0 + 1464, 2, NTILE, 2).bitcast(I32)
        tfill = view(R, T0 + 1484, MAXT + 2, 2).bitcast(I32)
        tseq = view(R, T0 + 1484 + 2 * (MAXT + 2), MAXT + 2, 2).bitcast(I32)
        ya = [view(W, 6 * SLOT + n * D, D) for n in range(NTILE)]
        yb = [view(W, 6 * SLOT + (NTILE + n) * D, D) for n in range(NTILE)]
        gateF = view(hflat, 0, 2, D)
        fing = view(hflat, 2 * D, D)
        jk = view(hflat, 3 * D, D)
        s_ya = [sem(f"y_rows_in{i}") for i in range(NTILE)]
        s_ph3 = sem("final_in")
        s_ga = sem("higher_output_gated")
        s_gated = sem("combined_and_gated")
        s_comb = sem("residual_added")
        s_fsq = sem("final_square")
        s_fin = sem("final_ready")
        s_out = [sem(f"y_out{i}") for i in range(2)]

        wg = a["w_exp_gate"].rearrange("l e (k p) f -> p (l e) k f", p=P)
        wu = a["w_exp_up"].rearrange("l e (k p) f -> p (l e) k f", p=P)
        wd = a["w_exp_down"].rearrange("l e (k p) f -> p (l e) k f", p=P)

        wmem = [(W, 0), (W, 6 * SLOT), (R, 18560 - 6 * SLOT)]

        def wexp(par):
            t, b = wmem[par]
            return (view(t, b, KT, DE), view(t, b + 2 * SLOT, KT, DE), view(t, b + 4 * SLOT, FT, D))

        def load_expert(sp, par, e, parts=(0, 1, 2)):
            for n in parts:
                src = (wg, wu, wd)[n]
                sp.dma_start(wexp(par)[n], src[:, bass.ds(e, 1), :, :].rearrange("p o k f -> p (o k) f")).then_inc(s_we[par], 16)

        @block.sync
        def _(sp):
            sp.dma_start(crow[0:8, :], a["c_prompt"].rearrange("b (k q) -> (b k) q", q=P)).then_inc(s_c, 16)
            sp.dma_start(crow[8:16, :], a["c_sample"].rearrange("b (k q) -> (b k) q", q=P)).then_inc(s_c, 16)
            sp.dma_start(crow[16:24, :], a["norm_mix_gain"].rearrange("l (k q) -> (l k) q", q=P)).then_inc(s_c, 16)
            for i in range(4):
                sp.dma_start(x[:, i, :], a["x_prompt"][0, i * P:(i + 1) * P, :]).then_inc(s_x[i], 16)
            sp.dma_start(x[0:NDEC, 4, :], a["x_sample"][0]).then_inc(s_x[4], 16)
            cols = {"hq": HQ, "hg": HG, "hf": HF, "hi": HI, "fk": FK, "fv": FV, "fq": FQ}
            for name, _, _ in ring:
                s, value, n, owners = loads[name]
                if name == "wo0":
                    sp.wait_ge(s_sout, 32)
                for o in dict.fromkeys(owners):
                    if o is not None:
                        filled(sp, lastuse[o])
                if name.startswith("ada"):
                    r, k = int(name[3]), int(name[5])
                    sp.dma_start(wslot(name, SLOT)[:, 0, :], w_ada[:, k, r * SLOT:(r + 1) * SLOT]).then_inc(s_w[s], 16)
                elif name.startswith("wo"):
                    k = int(name[2])
                    sp.dma_start(wslot(name, D), w_out[:, 2 * k:2 * k + 2, :]).then_inc(s_w[s], 16)
                else:
                    sp.dma_start(wslot(name, HW), w_in[:, :, cols[name]:cols[name] + HW]).then_inc(s_w[s], 16)
            sp.wait_ge(s_fo, NTILE)
            load_expert(sp, 0, 0, (0, 1))
            filled(sp, "y40")
            load_expert(sp, 0, 0, (2,))
            load_expert(sp, 1, 1, (0,))
            filled(sp, "lg")
            both(sp, s_h2w)
            load_expert(sp, 1, 1, (1, 2))
            load_expert(sp, 2, 2)
            for gi in range(2):
                n = P if gi == 0 else NDEC
                sp.dma_start(gateF[0:n, gi, :], bcast(mod_d[gi, 5 * D:6 * D], n)).then_inc(s_ph3, 16)
            sp.dma_start(fing, bcast(a["final_norm_gain"], P)).then_inc(s_ph3, 16)
            sp.wait_ge(s_rd, 1)

            def next_expert(par, e):
                done = sp.value_load(base_i[0:1, bass.ds(e - 2, 1)], min_val=1, max_val=MAXT)
                sp.wait_ge(s_yd, done)
                load_expert(sp, par, e)

            with sp.Fori(1, NE // 3) as three:
                for par in range(3):
                    next_expert(par, three * 3 + par)
            next_expert(0, NE - 1)
            total = sp.value_load(base_i[0:1, NE:NE + 1], min_val=NE, max_val=MAXT)
            sp.wait_ge(s_yd, total)
            sp.wait_ge(s_yst, total * 16 + 16)

            def load_y(i):
                n = ROWS[i]
                sp.dma_start(ya[i][0:n, :], y_d[i * P:i * P + n, :]).then_inc(s_ya[i], 16)
                sp.dma_start(yb[i][0:n, :], y_d[TOK + i * P:TOK + i * P + n, :]).then_inc(s_ya[i], 16)

            for i in range(NTILE):
                load_y(i)
            for i in range(NTILE):
                n = ROWS[i]
                sp.wait_ge(s_fin, i + 1)
                sp.dma_start(out["y_prompt"][0, i * P:i * P + n, :] if i < 4 else out["y_sample"][0],
                             ya[i][0:n, :]).then_inc(s_out[i % 2], 16)
            both(sp, s_out)
            both(sp, s_kout)
            sp.wait_ge(s_vout, 16 * NTILE)
            sp.wait_ge(s_lout, 32)
            sp.wait_ge(s_sout, 32)

        @block.gpsimd
        def _(pool):
            g = nc.gpsimd
            plink(pool, g.memset(st[:], 0.0))
            plink(pool, g.memset(st[:, 126:127], EPS))
            plink(pool, g.memset(ident[:], 0.0))
            g.affine_select(ident[:], ident[:], [[-1, P]], ALU.not_equal, 1.0, base=0,
                            channel_multiplier=1).then_inc(s_ident, 1)
            g.memset(cpad[:], 0.0).then_inc(s_cpad, 1)
            g.iota(ip, [[0, 32]], base=0, channel_multiplier=1)
            g.iota(it, [[1, 32]], base=0, channel_multiplier=0).then_inc(s_iota, 1)
            pool.dma_start(hgain, bcast(a["hg_norm_gain"][0], P)).then_inc(s_small, 16)
            pool.dma_start(wff, w_in[:, :, FF:FF + FH]).then_inc(s_small, 16)
            pool.dma_start(fbias[0:8, :], a["fox_f_bias"].rearrange("l h -> h l")).then_inc(s_small, 16)
            pool.dma_start(lpast, a["cache_fox_logf"].rearrange("l b (j p) h -> p (l b j) h", p=P)).then_inc(s_small, 16)
            bada = a["b_ada"].rearrange("l (r j n) -> r (l j) n", r=3, j=4)
            plink(pool, g.memset(badd, 0.0))

            def bias_rows(r):
                for gi in range(2):
                    pool.dma_start(badd[gi:gi + 97:32, :], bada[r]).then_inc(s_badd, 16)

            def mod_rows(r):
                taken(pool, f"ada{r}")
                for gi in range(2):
                    pool.dma_start(mod_d[gi, r * SLOT:(r + 1) * SLOT].rearrange("(j n) -> j n", j=4),
                                   msb[gi:gi + 97:32, :]).then_inc(s_modw, 16)
                pool.wait_ge(s_modw, 32 * r)

            bias_rows(0)
            taken(pool, "ada0")
            bias_rows(1)
            pool.wait_ge(s_small, 64)
            for h in range(HGH):
                taken(pool, f"hq{h}1")
                g.tensor_scalar(qs[:, h, :], qs[:, h, :], float(P) ** -0.5, None, ALU.mult).then_inc(s_qs, 1)
            for i in range(NTILE):
                n = ROWS[i]
                taken(pool, f"hg{i}")
                g.tensor_tensor(G[0:n, i, :], G[0:n, i, :], hgain[0:n, :], ALU.mult).then_inc(s_G, 1)
            kout = out["fox_k_prompt"].rearrange("l b t h d -> (l b t) (h d)")
            vout = out["fox_v_prompt"].rearrange("l b t h d -> (l b t) (h d)")
            kous = out["fox_k_sample"].rearrange("l b t h d -> (l b t) (h d)")
            vous = out["fox_v_sample"].rearrange("l b t h d -> (l b t) (h d)")
            mod_rows(1)
            bias_rows(2)
            for i in range(NTILE):
                taken(pool, f"fk{i}")
                pool.dma_start(kout[i * P:(i + 1) * P, :] if i < 4 else kous, fkt[i % 2][0:ROWS[i], :]).then_inc(s_kout[i % 2], 16)
            mod_rows(2)
            for i in range(NTILE):
                taken(pool, f"fv{i}")
                pool.dma_start(vout[i * P:(i + 1) * P, :] if i < 4 else vous, v_fox[0:ROWS[i], i, :]).then_inc(s_vout, 16)
            filled(pool, "fq31")
            pool.dma_start(S_sample, a["state_hgrn"].rearrange("l b h k v -> k (l b h) v")).then_inc(s_S0, 16)
            filled(pool, "ff1")
            pool.dma_start(kc, a["cache_fox_k"].rearrange("l b (j p) h d -> p (l b j) (h d)", p=P)).then_inc(s_cache, 16)
            pool.dma_start(vc, a["cache_fox_v"].rearrange("l b (j p) h d -> p (l b j) (h d)", p=P)).then_inc(s_cache, 16)
            taken(pool, "lfT")
            pool.wait_ge(s_cf, 1)
            pool.dma_start(out["fox_logf_prompt"].rearrange("l b (i p) h -> p (l b i) h", p=P), lfo[:, 0:4, :]).then_inc(s_lout, 16)
            pool.dma_start(out["fox_logf_sample"][0, 0], lfo[0:NDEC, 4, :]).then_inc(s_lout, 16)
            pool.dma_start(ck_d, cf[0:8, 0:SEQ]).then_inc(s_ckw, 16)
            pool.dma_start(cks_d, cf[0:8, SEQ:SEQ + PAST + NDEC]).then_inc(s_ckw, 16)
            pool.wait_ge(s_ckw, 32)
            pool.wait_ge(s_lout, 32)
            both(pool, s_kout)
            pool.dma_start(ckB.rearrange("p h t -> p (h t)"), bcast(ck_d.rearrange("h t -> (h t)"), P)).then_inc(s_ckr, 16)
            pool.dma_start(ckS[0:NDEC].rearrange("p h t -> p (h t)"),
                           bcast(cks_d.rearrange("h t -> (h t)"), NDEC)).then_inc(s_ckr, 16)
            pool.dma_start(fgain, bcast(a["fox_out_gain"][0], P)).then_inc(s_ckr, 16)

            def mask_future(q):
                blk = ckB[:, :, q * P:(q + 1) * P] if q < 4 else ckS[0:NDEC, :, PAST:]
                g.affine_select(blk, blk, [[0, FH], [-1, ROWS[q]]], ALU.is_ge, NEG, base=0,
                                channel_multiplier=1).then_inc(s_mask, 1)

            pool.wait_ge(s_ckr, 48)
            mask_future(QT[0])
            sp_o = out["hgrn_state_prompt"].rearrange("l b h k v -> k (l b h) v")
            ss_o = out["hgrn_state_sample"].rearrange("l b h k v -> k (l b h) v")
            taken(pool, "S3")
            pool.dma_start(sp_o, S).then_inc(s_sout, 16)
            taken(pool, "S4")
            pool.dma_start(ss_o, S_sample).then_inc(s_sout, 16)
            for n, q in enumerate(QT[1:]):
                taken(pool, f"s{QT[n]}{FH - 1}")
                mask_future(q)
            taken(pool, "fo4")
            pool.wait_ge(s_vout, 16 * NTILE)
            for gi in range(2):
                n = P if gi == 0 else NDEC
                pool.dma_start(mod1[0:n, gi, :], bcast(mod_d[gi, SLOT:2 * SLOT], n)).then_inc(s_mod1, 16)
                pool.dma_start(mod2[0:n, gi, :], bcast(mod_d[gi, 2 * SLOT:3 * SLOT], n)).then_inc(s_mod1, 16)
            pool.dma_start(ngain, bcast(a["norm_ffn_gain"][0], P)).then_inc(s_mod1, 16)
            pool.dma_start(wrt, a["w_router"].rearrange("(k p) e -> p k e", p=P)).then_inc(s_mod1, 16)
            taken(pool, "fo4")
            pool.dma_start(brt, bcast(a["b_router"], P)).then_inc(s_brt, 16)
            g.memset(tfill[:, :, 0], 0)
            g.memset(tfill[:, :, 1], 8 * TOK).then_inc(s_tfill, 1)
            pool.wait_ge(s_tfill, 1)
            pool.dma_start(tab_d.rearrange("(t r) c -> r t c", r=ET), tfill[0:ET]).then_inc(s_tab0, 16)
            g.memset(ones, 1.0)
            plink(pool, g.memset(tri, 1.0))
            g.affine_select(tri, tri, [[1, P]], ALU.is_gt, 0.0, base=0, channel_multiplier=-1)
            for c in range(2):
                g.iota(entry[:, c, :, 0], [[P, NTILE]], base=0, channel_multiplier=1)
                ins = g.iota(entry[:, c, :, 1], [[P, NTILE]], base=c * TOK, channel_multiplier=1)
            ins.then_inc(s_rc, 1)
            def residual(i):
                n = ROWS[i]
                for c in range(2):
                    taken(pool, f"y{i}{c if i < 4 else 0}")
                    xs = x[0:n, i, c * 512:(c + 1) * 512]
                    g.tensor_tensor(xs, xs, gt[c][0:n, :], ALU.add).then_inc(s_x2, 1)

            def shift_h2(i):
                n, gi = ROWS[i], i // 4
                pool.wait_ge(s_h2a, i + 1)
                g.tensor_tensor(h2[i][0:n, :], h2[i][0:n, :], mod1[0:n, gi, D:2 * D], ALU.add).then_inc(s_h2, 1)
                pool.wait_ge(s_h2, i + 1)
                pool.dma_start(h2_d[i * P:i * P + n, :], h2[i][0:n, :]).then_inc(s_h2w[i % 2], 16)

            residual(0)
            for i in range(1, NTILE):
                residual(i)
                shift_h2(i - 1)
            shift_h2(NTILE - 1)
            pool.wait_ge(s_dst, 1)
            pool.wait_ge(s_tab0, 16)
            last_row = pool.to_reg((MAXT + 2) * ET - 1)
            for c in range(2):
                for i in range(NTILE):
                    j, n = c * NTILE + i, ROWS[i]
                    pool.indirect_dma_start(tab_d, bass.IndirectOffsetOnAxis(ap=dst_i[0:n, j:j + 1], axis=0),
                                            entry[0:n, c, i, :], None, bounds_check=last_row,
                                            oob_is_err=False).then_inc(s_tabw, 16)
            pool.wait_ge(s_tabw, 32 * NTILE)
            pool.dma_start(tseq[0:ET], tab_d.rearrange("(t r) c -> r t c", r=ET)).then_inc(s_tab, 16)
            pool.wait_ge(s_rd, 1)
            total = pool.value_load(base_i[0:1, NE:NE + 1], min_val=NE, max_val=MAXT)
            both(pool, s_h2w)
            pool.wait_ge(s_tab, 16)
            pool.dma_start(ysb[0:1, :], h2_d[0:1, :]).then_inc(s_yst, 16)

            last_token, last_y = pool.to_reg(TOK - 1), pool.to_reg(2 * TOK - 1)

            gathers, scatters = pool.alloc_register("gathers"), pool.alloc_register("scatters")
            pool.reg_mov(gathers, 0)
            pool.reg_mov(scatters, 1)

            def gather():
                pool.reg_add(gathers, gathers, 1)
                pool.indirect_dma_start(xg[0:ET], None, h2_d, bass.IndirectOffsetOnAxis(ap=idx1[0:ET], axis=0),
                                        bounds_check=last_token, oob_is_err=False).then_inc(s_gath, 16)

            g.tensor_copy(idx1[0:ET], tseq[0:ET, 0, 0:1]).then_inc(s_idx, 1)
            pool.wait_ge(s_idx, 1)
            gather()
            pool.wait_ge(s_xp, 1)
            g.tensor_copy(idx1[0:ET], tseq[0:ET, 1, 0:1]).then_inc(s_idx, 1)
            pool.wait_ge(s_idx, 2)
            gather()
            with pool.Fori(0, total) as t:
                pool.wait_ge(s_xp, t + 2)
                g.tensor_copy(idx1[0:ET], tseq[0:ET, bass.ds(t + 2, 1), 0]).then_inc(s_idx, 1)
                pool.wait_ge(s_idx, t * 2 + 3)
                gather()
                pool.wait_ge(s_yst, t * 16 + 16)
                g.tensor_copy(idx2[0:ET], tseq[0:ET, bass.ds(t, 1), 1]).then_inc(s_idx, 1)
                pool.wait_ge(s_idx, t * 2 + 4)
                pool.wait_ge(s_yea, t + 2)
                pool.wait_ge(s_yeb, t + 2)
                pool.reg_add(scatters, scatters, 1)
                pool.indirect_dma_start(y_d, bass.IndirectOffsetOnAxis(ap=idx2[0:ET], axis=0), ysb[0:ET], None,
                                        bounds_check=last_y, oob_is_err=False).then_inc(s_yst, 16)
            pool.wait_ge(s_gath, pool.snap(gathers, min_val=1, max_val=MAXT + 2) * 16)
            pool.wait_ge(s_yst, pool.snap(scatters, min_val=1, max_val=MAXT + 1) * 16)
            for i in range(NTILE):
                n = ROWS[i]
                pool.wait_ge(s_gated, i + 1)
                g.tensor_tensor(x[0:n, i, :], x[0:n, i, :], ya[i][0:n, :], ALU.add).then_inc(s_comb, 1)

        @block.scalar
        def _(act):
            A = nc.scalar

            def root(y, ss, width):
                alink(act, A.activation(y, ss, ACT.Ln, bias=st[0:y.shape[0], 126:127], scale=1.0 / width))
                return A.activation(y, y, ACT.Exp, scale=-0.5)

            filled(act, "cT")
            act.wait_ge(s_cpad, 1)
            A.copy(gainT, bank[0][:, 16:24])
            read("act", "cT", A.activation(cpad[:, :, 0:2].rearrange("p k g -> p g k"),
                                           bank[0][:, 0:16].rearrange("p (g k) -> p g k", g=2), ACT.Silu))
            act.wait_ge(s_ident, 1)
            for i in range(NTILE):
                n = ROWS[i]
                act.wait_ge(s_x[i], 16)
                if i:
                    act.wait_ge(s_ss, i)
                A.activation(h1[0][0:n, :], x[0:n, i, :], ACT.Square, accum_out=st[0:n, i:i + 1]).then_inc(s_ss, 1)
            act.wait_ge(s_ss, NTILE)
            root(st[:, 5:10], st[:, 0:5], D).then_inc(s_rs, 1)
            for i in range(NTILE):
                n = ROWS[i]
                for c in range(2):
                    filled(act, f"hT{i}{c}")
                    read("act", f"hT{i}{c}", A.copy(hT[:, 4 * c:4 * c + 4, i * P:i * P + n],
                                                    bank[2 + 2 * (i % 2) + c][:, :].rearrange("p (k t) -> p k t", k=4)[:, :, 0:n]))
            act.wait_ge(s_modT, 1)
            taken(act, "hT41")
            for k in range(4):
                for gi, ts in ((0, slice(0, SEQ)), (1, slice(SEQ, TOK))):
                    ins = A.activation(hT[:, k, ts], hT[:, k, ts], ACT.Identity, bias=modT[:, gi, k:k + 1],
                                       scale=modT[:, gi, KT + k:KT + k + 1])
            ins.then_inc(s_hma, 1)
            for h in range(HGH):
                for c in range(2):
                    filled(act, f"hq{h}{c}")
                    read("act", f"hq{h}{c}", A.activation(qs[:, h, c * HALF:(c + 1) * HALF],
                                                          bank[4 + 2 * (h % 2) + c][:, 0:HALF], ACT.Silu))
            for i in range(NTILE):
                filled(act, f"hg{i}")
                b = bank[2 + i % 2]
                if i < 4:
                    read("act", f"hg{i}", A.activation(G[:, i, :], b[:, :], ACT.Silu))
                else:
                    for j in range(4):
                        ins = A.activation(G[0:NDEC, 4, j * P:(j + 1) * P], b[32 * j:32 * j + 32, 0:P], ACT.Silu)
                    read("act", f"hg{i}", ins)
            for h in range(HGH):
                taken(act, f"hf{h}1")
                alink(act, A.activation(ex, fr, ACT.Abs))
                alink(act, A.activation(ex, ex, ACT.Exp, scale=-1.0))
                A.activation(ex, ex, ACT.Ln, bias=1.0).then_inc(s_ln, 1)
                act.wait_ge(s_kx, h + 1)
                A.activation(kk[:, h, :], fr, ACT.Exp).then_inc(s_kk, 1)
            for i in range(NTILE):
                n = ROWS[i]
                filled(act, f"fk{i}")
                if i >= 2:
                    act.wait_ge(s_kout[i % 2], 16 * (i // 2))
                    filled(act, f"fkT{i - 2}")
                b = bank[4 + i % 2]
                if i < 4:
                    read("act", f"fk{i}", A.copy(fkt[i % 2], b[:, :]))
                else:
                    for j in range(4):
                        ins = A.copy(fkt[0][0:NDEC, j * P:(j + 1) * P], b[32 * j:32 * j + 32, 0:P])
                    read("act", f"fk{i}", ins)
            seen = {"lv": 0}

            def exp_levels(i):
                n = ROWS[i]
                for lv in levels(n):
                    seen["lv"] += 1
                    act.wait_ge(s_lv, seen["lv"])
                    A.activation(X[i % 2][:, lv, :, 0:n], X[i % 2][:, lv, :, 0:n], ACT.Exp).then_inc(s_le, 1)

            def exp_ends(i):
                n = ROWS[i]
                seen["lv"] += 1
                act.wait_ge(s_lv, seen["lv"])
                A.activation(E[i % 2][:, :, 0:n], bb[:, :, i * P:i * P + n], ACT.Exp).then_inc(s_le, 1)
                A.activation(kE[i % 2][:, :, 0:n], kE[i % 2][:, :, 0:n], ACT.Exp).then_inc(s_le, 1)

            exp_levels(0)
            exp_ends(0)
            for h in range(4):
                for c in range(2):
                    filled(act, f"fq{h}{c}")
                    read("act", f"fq{h}{c}", A.copy(fqT[:, h, c * HALF:(c + 1) * HALF],
                                                    bank[4 + 2 * (h % 2) + c][:, 0:HALF]))
            taken(act, "ff1")
            alink(act, A.activation(ssel[0:8, 0:TOK], cf[0:8, 0:TOK], ACT.Abs))
            alink(act, A.activation(ssel[0:8, 0:TOK], ssel[0:8, 0:TOK], ACT.Exp, scale=-1.0))
            A.activation(ssel[0:8, 0:TOK], ssel[0:8, 0:TOK], ACT.Ln, bias=1.0).then_inc(s_ln, 1)
            exp_levels(1)
            for i in range(-1, NTILE):
                if i >= 0:
                    n = ROWS[i]
                    if i + 2 < NTILE:
                        exp_levels(i + 2)
                    filled(act, f"kT{i}")
                    read("act", f"kT{i}", A.copy(kET[0:n], bank[3][0:n, :].rearrange("p (h k) -> p h k", h=HGH)))
                    filled(act, f"ho{i}")
                    for h in range(HGH):
                        ins = A.activation(att6s[0:n, :], bank[4][0:n, h * P:(h + 1) * P],
                                           ACT.Square, accum_out=st[0:n, 10 + 4 * i + h:11 + 4 * i + h])
                        ins.then_inc(s_sq, 1)
                        act.wait_ge(s_sq, 4 * i + h + 1)
                    root(st[0:n, 30:34], st[0:n, 10 + 4 * i:14 + 4 * i], P).then_inc(s_rs, 1)
                if i + 2 < NTILE:
                    exp_ends(i + 2)
            for c in range(2):
                filled(act, f"kcT{c}")
                read("act", f"kcT{c}", A.copy(kcT[:, :, c * P:(c + 1) * P], bank[6 + c][:, :].rearrange("p (a b) -> p a b", a=4)))
            def fox_root(n_q):
                q = QT[n_q]
                n = ROWS[q]
                taken(act, f"fo{q}")
                if n_q:
                    act.wait_ge(s_fq, n_q)
                A.activation(osq[0:n, :], foxo[0:n, q, :], ACT.Square, accum_out=st[0:n, 80 + n_q:81 + n_q]).then_inc(s_fq, 1)
                act.wait_ge(s_fq, n_q + 1)
                root(st[0:n, 85 + n_q:86 + n_q], st[0:n, 80 + n_q:81 + n_q], HW).then_inc(s_rs, 1)

            m = 0
            for n_q, q in enumerate(QT):
                n = ROWS[q]
                nb = q + 1 if q < 4 else 3
                L = (q + 1) * P if q < 4 else PAST + NDEC
                for h in range(FH + 1):
                    if h < FH:
                        act.wait_ge(s_pmax, m + 1)
                        A.activation(pp[h % 2][0:n, 0:L], pp[h % 2][0:n, 0:L], ACT.Exp, bias=st[0:n, 50 + h:51 + h],
                                     accum_out=st[0:n, 60 + 8 * (n_q % 2) + h:61 + 8 * (n_q % 2) + h]).then_inc(s_pexp, 1)
                        m += 1
                    if h:
                        hh = h - 1
                        filled(act, f"t{q}{hh}")
                        src = bank[2 + h % 2][:, :].rearrange("p (a b) -> p a b", a=4)
                        if q < 4:
                            ins = A.copy(pT[h % 2][:, 0:nb, :], src[:, 0:nb, :])
                        else:
                            alink(act, A.copy(pT[h % 2][:, 0:2, 0:NDEC], src[:, 0:2, 0:NDEC]))
                            ins = A.copy(pT[h % 2][0:NDEC, 2, 0:NDEC], src[0:NDEC, 2, 0:NDEC])
                        read("act", f"t{q}{hh}", ins)
                    if n_q and h == 2:
                        fox_root(n_q - 1)
            fox_root(4)
            for i in range(NTILE):
                n = ROWS[i]
                filled(act, f"m{i}0")
                if i == 0:
                    filled(act, "fo4")
                read("act", f"m{i}0", A.copy(hT[:, 0:4, i * P:i * P + n],
                                             bank[0][:, :].rearrange("p (k t) -> p k t", k=4)[:, :, 0:n]))
            def square_x2(i):
                n = ROWS[i]
                act.wait_ge(s_x2, 2 * i + 2)
                if i >= 2:
                    act.wait_ge(s_x2q, i - 1)
                A.activation(x2sq[i % 2][0:n, :], x[0:n, i, :], ACT.Square, accum_out=st[0:n, 90 + i:91 + i]).then_inc(s_x2q, 1)
                act.wait_ge(s_x2q, i + 1)
                root(st[0:n, 95 + i:96 + i], st[0:n, 90 + i:91 + i], D).then_inc(s_rs, 1)

            def h2_turned(i):
                n = ROWS[i]
                if i == 0:
                    act.wait_ge(s_sout, 32)
                for c in range(2):
                    filled(act, f"r{i}{c}")
                    read("act", f"r{i}{c}", A.copy(h2T[i % 2][:, 4 * c:4 * c + 4, 0:n],
                                                   bank[c][:, :].rearrange("p (k t) -> p k t", k=4)[:, :, 0:n]))

            square_x2(0)
            square_x2(1)
            for i in range(NTILE):
                h2_turned(i)
                if i + 2 < NTILE:
                    square_x2(i + 2)
            act.wait_ge(s_lx, 1)
            A.activation(prb, prb, ACT.Exp).then_inc(s_lex, 1)
            def xt_low():
                A.copy(XT[:, 0:4, :], bank[0][:, 0:4 * ET].rearrange("p (k t) -> p k t", k=4)).then_inc(s_xta, 1)

            act.wait_ge(s_rd, 1)
            act.sem_inc(s_yea, 1)
            total = act.value_load(base_i[0:1, NE:NE + 1], min_val=NE, max_val=MAXT)
            act.wait_ge(s_xp, 1)
            xt_low()
            with act.Fori(0, total) as t:
                for c in range(2):
                    act.wait_ge(s_gu, t * 2 + (c + 1))
                    A.activation(hs[ET:2 * ET, c * 256:(c + 1) * 256], bank[2 + c][0:ET, 0:256], ACT.Silu).then_inc(s_sil, 1)
                act.wait_ge(s_xp, t + 2)
                xt_low()
                act.wait_ge(s_yd, t + 1)
                act.wait_ge(s_yst, t * 16 + 16)
                A.copy(ysb[0:ET, 0:512], bank[6][0:ET, :]).then_inc(s_yea, 1)
            def gate_a(i):
                n = ROWS[i]
                act.wait_ge(s_ya[i], 32)
                A.activation(ya[i][0:n, :], ya[i][0:n, :], ACT.Copy, scale=gA[0:n, i:i + 1]).then_inc(s_ga, 1)

            gate_a(0)
            gate_a(1)
            gate_a(2)
            for i in range(NTILE):
                n = ROWS[i]
                if i + 3 < NTILE:
                    gate_a(i + 3)
                act.wait_ge(s_comb, i + 1)
                if i:
                    act.wait_ge(s_fsq, i)
                A.activation(jk[0:n, :], x[0:n, i, :], ACT.Square, accum_out=st[0:n, 100 + i:101 + i]).then_inc(s_fsq, 1)
                act.wait_ge(s_fsq, i + 1)
                root(st[0:n, 105 + i:106 + i], st[0:n, 100 + i:101 + i], D).then_inc(s_rs, 1)

        def route(dve, V):
            vlink(dve, V.memset(prb, 0.0))
            filled(dve, "lg")
            lb = bank[2][:, 0:NTILE * NE].rearrange("p (n e) -> p n e", e=NE)
            vlink(dve, V.tensor_copy(prb[:, 0:4, :], lb[:, 0:4, :]))
            read("dve", "lg", V.tensor_copy(prb[0:NDEC, 4, :], lb[0:NDEC, 4, :]))
            taken(dve, "lg")
            vlink(dve, V.tensor_reduce(s5[0], prb, AX.X, ALU.max))
            V.tensor_tensor(prb, prb, wide(s5[0]), ALU.subtract).then_inc(s_lx, 1)
            dve.wait_ge(s_lex, 1)
            vlink(dve, V.tensor_reduce(s5[1], prb, AX.X, ALU.add))
            vlink(dve, V.reciprocal(s5[1], s5[1]))
            vlink(dve, V.tensor_tensor(prb, prb, wide(s5[1]), ALU.mult))
            dve.wait_ge(s_brt, 16)
            vlink(dve, V.tensor_tensor(sel, prb, brt.unsqueeze(1).broadcast_to([P, NTILE, NE]), ALU.add))

            def ranks(values, rk, tmp):
                for j in range(4):
                    vlink(dve, V.memset(rk[:, :, j], float(3 - j)))
                for j in range(4):
                    for jj in range(j):
                        vlink(dve, V.tensor_tensor(tmp, values[:, :, jj], values[:, :, j], ALU.is_ge))
                        vlink(dve, V.tensor_tensor(rk[:, :, j], rk[:, :, j], tmp, ALU.add))
                        vlink(dve, V.tensor_tensor(rk[:, :, jj], rk[:, :, jj], tmp, ALU.subtract))

            fours = "p n (g j) -> p (n g) j"
            sel4, rk4, msk4 = (v.rearrange(fours, j=EPG) for v in (sel, t80[0], msk))
            ranks(sel4, rk4, g20[0].rearrange("p n g -> p (n g)"))
            vlink(dve, V.tensor_scalar(msk, t80[0], 2.0, None, ALU.is_lt))
            vlink(dve, V.tensor_tensor(t80[1], sel, msk, ALU.mult))
            vlink(dve, V.tensor_reduce(g20[1].rearrange("p n g -> p (n g)"), t80[1].rearrange(fours, j=EPG), AX.X, ALU.add))
            ranks(g20[1], g20[2], s5[2])
            vlink(dve, V.tensor_scalar(g20[3], g20[2], 0.0, None, ALU.is_equal))
            vlink(dve, V.tensor_tensor(msk4, msk4, g20[3].rearrange("p n g -> p (n g)").unsqueeze(2).broadcast_to([P, NTILE * NG, EPG]), ALU.mult))
            vlink(dve, V.memset(msk[32:64, 4, :], 0.0))
            V.memset(msk[64:128, 4, :], 0.0).then_inc(s_mk, 1)
            dve.wait_ge(s_mk, 1)
            filled(dve, "cnt")
            read("dve", "cnt", V.tensor_scalar(cnt_i, bank[4][:, 0:NE], float(ET - 1), None, ALU.add))
            taken(dve, "cnt")
            vlink(dve, V.tensor_scalar(cnt_i, cnt_i, -ET, None, ALU.bitwise_and))
            vlink(dve, V.tensor_scalar(tf[1], cnt_i, 1.0 / ET, 1.0, ALU.mult, ALU.max))
            vlink(dve, V.tensor_tensor_scan(tf[2], tf[1], tf[1], 0.0, ALU.add, ALU.bypass))
            vlink(dve, V.tensor_tensor(tf[3], tf[2], tf[1], ALU.subtract))
            vlink(dve, V.tensor_scalar(tf[3], tf[3], float(ET), 1.0, ALU.mult, ALU.add))
            dve.wait_ge(s_rc, 1)
            filled(dve, "pos")
            pb = bank[3][:, 0:NTILE * NE].rearrange("p (n e) -> p n e", e=NE)
            read("dve", "pos", V.tensor_tensor(t80[2], pb, tf[3].unsqueeze(1).broadcast_to([P, NTILE, NE]), ALU.add))
            taken(dve, "pos")
            vlink(dve, V.tensor_tensor(t80[2], t80[2], msk, ALU.mult))
            V.tensor_reduce(s5[4], t80[2], AX.X, ALU.max)
            vlink(dve, V.tensor_reduce(s5[5], t80[2], AX.X, ALU.add))
            V.tensor_scalar(dst[:, 0:NTILE], s5[4], -1.0, None, ALU.add)
            vlink(dve, V.scalar_tensor_tensor(dst[:, NTILE:], s5[5], -1.0, s5[4], ALU.add, ALU.subtract))
            V.tensor_copy(dst_i, dst).then_inc(s_dst, 1)
            V.tensor_copy(ntile_i[0:1, :], tf[1][0:1, :])
            V.memset(base_i[0:1, 0:1], 0)
            V.tensor_copy(base_i[0:1, 1:NE + 1], tf[2][0:1, :]).then_inc(s_rd, 1)
            vlink(dve, V.tensor_tensor(gts, prb, msk, ALU.mult))
            vlink(dve, V.tensor_reduce(s5[3], gts, AX.X, ALU.add))
            V.memset(s5[3][32:64, 4:5], 1.0)
            vlink(dve, V.memset(s5[3][64:128, 4:5], 1.0))
            vlink(dve, V.reciprocal(s5[3], s5[3]))
            vlink(dve, V.tensor_tensor(gts, gts, wide(s5[3]), ALU.mult))
            vlink(dve, V.tensor_tensor(t80[3], t80[2], wide(s5[4]), ALU.is_equal))
            vlink(dve, V.tensor_tensor(t80[3], t80[3], gts, ALU.mult))
            V.tensor_reduce(gA, t80[3], AX.X, ALU.add)
            vlink(dve, V.tensor_tensor(t80[4], gts, t80[3], ALU.subtract))
            vlink(dve, V.tensor_reduce(gB, t80[4], AX.X, ALU.add))

        @block.vector
        def _(dve):
            V = nc.vector

            def rstd(y, ss, width):
                n, w = y.shape[0], y.shape[1]
                v, t = st[0:n, 110:110 + w], st[0:n, 118:118 + w]
                vlink(dve, V.tensor_scalar(v, ss, 1.0 / width, EPS, ALU.mult, ALU.add))
                vlink(dve, V.tensor_tensor(t, y, y, ALU.mult))
                vlink(dve, V.tensor_tensor(t, t, v, ALU.mult))
                vlink(dve, V.tensor_scalar(t, t, -0.5, 1.5, ALU.mult, ALU.add))
                vlink(dve, V.tensor_tensor(y, y, t, ALU.mult))

            dve.wait_ge(s_iota, 1)
            vlink(dve, V.tensor_scalar(ip, ip, 31, None, ALU.bitwise_and))
            vlink(dve, V.tensor_tensor(ix, ip, it, ALU.bitwise_xor))
            vlink(dve, V.tensor_tensor(mgt, it, ip, ALU.is_gt))
            vlink(dve, V.tensor_copy(mxf, ix))
            for n, half in enumerate(LEVELS[2:]):
                vlink(dve, V.tensor_scalar(mtmp, mxf, float(half), None, ALU.is_ge))
                vlink(dve, V.scalar_tensor_tensor(mtmp, mxf, float(2 * half), mtmp, ALU.is_lt, ALU.mult))
                vlink(dve, V.tensor_tensor(lmask[:, n, :], mtmp, mgt, ALU.mult))
            vlink(dve, V.tensor_scalar(lmask[:, 5, :], mxf, 0.0, None, ALU.is_equal))
            dve.wait_ge(s_rs, 1)
            rstd(st[:, 5:10], st[:, 0:5], D)
            for i in range(NTILE):
                n = ROWS[i]
                if i >= 2:
                    filled(dve, f"hT{i - 2}1")
                V.tensor_scalar(h1[i % 2][0:n, :], x[0:n, i, :], st[0:n, 5 + i:6 + i], None, ALU.mult).then_inc(s_h1, 1)
            dve.wait_ge(s_badd, 32)
            filled(dve, "ada0")
            read("dve", "ada0", V.tensor_tensor(msb, bank[1][:, :], badd, ALU.add))
            filled(dve, "modT")
            mt = bank[0][:, :].rearrange("p (q j c) -> p j q c", q=4, j=4)
            for gi in range(2):
                for r in range(2):
                    ins = V.tensor_copy(modT[:, gi, r * KT:(r + 1) * KT].rearrange("p (j q) -> p j q", q=4), mt[:, 2 * r:2 * r + 2, :, gi])
            read("dve", "modT", ins)
            taken(dve, "modT")
            for gi in range(2):
                sc = modT[:, gi, KT:]
                ins = V.scalar_tensor_tensor(sc, sc, 1.0, gainT, ALU.add, ALU.mult)
            ins.then_inc(s_modT, 1)
            dve.wait_ge(s_modT, 1)
            taken(dve, "hT41")
            for k in range(4, KT):
                for gi, ts in ((0, slice(0, SEQ)), (1, slice(SEQ, TOK))):
                    ins = V.tensor_scalar(hT[:, k, ts], hT[:, k, ts], modT[:, gi, KT + k:KT + k + 1], modT[:, gi, k:k + 1],
                                          ALU.mult, ALU.add)
            ins.then_inc(s_hmd, 1)
            filled(dve, "hT41")
            for h in range(HGH):
                if h:
                    dve.wait_ge(s_kk, h)
                for c in range(2):
                    filled(dve, f"hf{h}{c}")
                    read("dve", f"hf{h}{c}", V.tensor_copy(fr[:, c * HALF:(c + 1) * HALF], bank[4 + 2 * (h % 2) + c][:, 0:HALF]))
                taken(dve, f"hf{h}1")
                dve.wait_ge(s_ln, h + 1)
                vlink(dve, V.scalar_tensor_tensor(lg, fr, 0.0, ex, ALU.min, ALU.subtract))
                V.tensor_tensor(fr, lg, fr, ALU.subtract).then_inc(s_kx, 1)
                for i in range(NTILE):
                    cs = slice(i * P, i * P + ROWS[i])
                    ins = V.tensor_tensor_scan(bb[:, h, cs], lg[:, cs], lg[:, cs], 0.0, ALU.add, ALU.bypass)
                vlink(dve, ins)
            dve.wait_ge(s_badd, 64)
            filled(dve, "modT")
            filled(dve, "ada1")
            read("dve", "ada1", V.tensor_tensor(msb, bank[1][:, :], badd, ALU.add))
            for i in range(NTILE):
                filled(dve, f"hi{i}")
                b = bank[2 + i % 2]
                if i < 4:
                    read("dve", f"hi{i}", V.tensor_copy(v_hg[:, i, :], b[:, :]))
                else:
                    for j in range(4):
                        ins = V.tensor_copy(v_hg[0:NDEC, 4, j * P:(j + 1) * P], b[32 * j:32 * j + 32, 0:P])
                    read("dve", f"hi{i}", ins)
            for i in range(NTILE):
                n = ROWS[i]
                filled(dve, f"fkT{i}")
                read("dve", f"fkT{i}", V.tensor_copy(fkT[:, :, i * P:i * P + n], bank[6][:, :].rearrange("p (a b) -> p a b", a=4)[:, :, 0:n]))
            dve.wait_ge(s_badd, 96)
            dve.wait_ge(s_modw, 32)
            filled(dve, "ada2")
            read("dve", "ada2", V.tensor_tensor(msb, bank[0][:, :], badd, ALU.add))
            known = {"le": 0}

            def exponents(i):
                n, t0 = ROWS[i], i * P
                for lv in levels(n):
                    H = LEVELS[lv]
                    bv = bb[:, :, t0:t0 + n].rearrange("p h (c w) -> p h c w", w=2 * H)
                    Xv = X[i % 2][:, lv, :, 0:n].rearrange("p h (c w) -> p h c w", w=2 * H)
                    anc = bv[:, :, :, H - 1:H].broadcast_to([P, HGH, n // (2 * H), H])
                    V.tensor_tensor(Xv[:, :, :, 0:H], anc, bv[:, :, :, 0:H], ALU.subtract)
                    V.tensor_tensor(Xv[:, :, :, H:], bv[:, :, :, H:], anc, ALU.subtract).then_inc(s_lv, 1)

            def end_exponents(i):
                n = ROWS[i]
                bt = bb[:, :, i * P:i * P + n]
                V.tensor_tensor(kE[i % 2][:, :, 0:n], bt[:, :, n - 1:n].broadcast_to([P, HGH, n]), bt, ALU.subtract).then_inc(s_lv, 1)

            def operands(i):
                n, t0 = ROWS[i], i * P
                for lv in levels(n):
                    H = LEVELS[lv]
                    known["le"] += 1
                    dve.wait_ge(s_le, known["le"])
                    Xv = X[i % 2][:, lv, :, 0:n].rearrange("p h (c w) -> p h c w", w=2 * H)
                    kv = kk[:, :, t0:t0 + n].rearrange("p h (c w) -> p h c w", w=2 * H)
                    qv = qs[:, :, t0:t0 + n].rearrange("p h (c w) -> p h c w", w=2 * H)
                    V.tensor_tensor(Xv[:, :, :, 0:H], Xv[:, :, :, 0:H], kv[:, :, :, 0:H], ALU.mult)
                    V.tensor_tensor(Xv[:, :, :, H:], Xv[:, :, :, H:], qv[:, :, :, H:], ALU.mult).then_inc(s_xm, 1)

            def end_operands(i):
                n, t0 = ROWS[i], i * P
                known["le"] += 2
                dve.wait_ge(s_le, known["le"])
                V.tensor_tensor(qE[i % 2][:, :, 0:n], E[i % 2][:, :, 0:n], qs[:, :, t0:t0 + n], ALU.mult)
                V.tensor_tensor(kE[i % 2][:, :, 0:n], kE[i % 2][:, :, 0:n], kk[:, :, t0:t0 + n], ALU.mult).then_inc(s_qk, 1)

            dve.wait_ge(s_qs, HGH)
            exponents(0)
            end_exponents(0)
            operands(0)
            end_operands(0)
            for i in range(NTILE):
                filled(dve, f"fv{i}")
                b = bank[2 + i % 2]
                if i < 4:
                    read("dve", f"fv{i}", V.tensor_copy(v_fox[:, i, :], b[:, :]))
                else:
                    for j in range(4):
                        ins = V.tensor_copy(v_fox[0:NDEC, 4, j * P:(j + 1) * P], b[32 * j:32 * j + 32, 0:P])
                    read("dve", f"fv{i}", ins)
            for c in range(2):
                filled(dve, f"ff{c}")
                read("dve", f"ff{c}", V.tensor_scalar(cf[0:8, c * HALF:(c + 1) * HALF], bank[c][0:8, 0:HALF], fbias[0:8, 0:1], None, ALU.add))
            filled(dve, "lpT")
            read("dve", "lpT", V.tensor_copy(lf[0:8, SEQ:SEQ + PAST], bank[2][0:8, 0:PAST]))
            dve.wait_ge(s_ln, HGH + 1)
            taken(dve, "ff1")
            vlink(dve, V.scalar_tensor_tensor(lf[0:8, 0:SEQ], cf[0:8, 0:SEQ], 0.0, ssel[0:8, 0:SEQ], ALU.min, ALU.subtract))
            V.scalar_tensor_tensor(lf[0:8, SEQ + PAST:], cf[0:8, SEQ:TOK], 0.0, ssel[0:8, SEQ:TOK], ALU.min, ALU.subtract).then_inc(s_lf, 1)
            dve.wait_ge(s_lf, 1)
            vlink(dve, V.tensor_tensor_scan(cf[0:8, 0:SEQ], lf[0:8, 0:SEQ], lf[0:8, 0:SEQ], 0.0, ALU.add, ALU.bypass))
            vlink(dve, V.tensor_tensor_scan(cf[0:8, SEQ:], lf[0:8, SEQ:SEQ + 288], lf[0:8, SEQ:SEQ + 288], 0.0, ALU.add, ALU.bypass))
            V.tensor_scalar(cf[0:8, :], cf[0:8, :], -float(FD) ** 0.5, None, ALU.mult).then_inc(s_cf, 1)
            filled(dve, "lfT")
            vlink(dve, V.tensor_copy(lfo[:, 0:4, :], bank[3][:, 0:32].rearrange("p (a b) -> p a b", a=4)))
            read("dve", "lfT", V.tensor_copy(lfo[0:NDEC, 4, :], bank[3][0:NDEC, 32:40]))
            for n in range(2):
                V.memset(attT[n], 0.0).then_inc(s_zero, 1)
            dve.wait_ge(s_zero, 2)
            dve.wait_ge(s_G, NTILE)

            def attention(i):
                n = ROWS[i]
                at = attT[i % 2]
                if i < 4:
                    filled(dve, f"L{i}")
                    Lb = bank[0][:, 0:384].rearrange("p (h c) -> p h c", h=HGH)
                    V.tensor_copy(at[0:64, :, 64:128], Lb[0:64, :, 0:64])
                    V.tensor_copy(at[0:32, :, 32:64], Lb[0:32, :, 64:96])
                    read("dve", f"L{i}", V.tensor_copy(at[64:96, :, 96:128], Lb[64:96, :, 64:96]))
                for c, nm in enumerate(("Da", "Db")):
                    filled(dve, f"{nm}{i}")
                    src = bank[1 + c][0:n, 0:384].rearrange("p (h l t) -> p h l t", h=2, l=6)
                    for hh in range(2):
                        ins = V.tensor_tensor(att6[0:n, hh], src[:, hh], lmask[0:n], ALU.mult)
                    read("dve", f"{nm}{i}", ins)
                    taken(dve, f"{nm}{i}")
                    vlink(dve, V.tensor_reduce(attd[0:n, 2 * c:2 * c + 2, :], att6[0:n].rearrange("p h l t -> p h t l"), AX.X, ALU.add))
                for j in range((n + 31) // 32):
                    ins = V.tensor_copy(at[32 * j:32 * j + 32, :, 32 * j:32 * j + 32], attd[32 * j:32 * j + 32, :, :])
                ins.then_inc(s_att, 1)

            def output_and_state(i):
                n = ROWS[i]
                dve.wait_ge(s_rs, 2 + i)
                rstd(st[0:n, 30:34], st[0:n, 10 + 4 * i:14 + 4 * i], P)
                for h in range(HGH):
                    ins = V.scalar_tensor_tensor(G[0:n, i, h * P:(h + 1) * P], bank[4][0:n, h * P:(h + 1) * P], st[0:n, 30 + h:31 + h],
                                                 G[0:n, i, h * P:(h + 1) * P], ALU.mult, ALU.mult)
                read("dve", f"ho{i}", ins)
                filled(dve, f"S{i}")
                St = S if i < 4 else S_sample
                for h in range(HGH):
                    if i == 0:
                        ins = V.tensor_copy(St[:, h, :], bank[5][:, h * P:(h + 1) * P])
                    else:
                        ins = V.scalar_tensor_tensor(St[:, h, :], St[:, h, :], E[i % 2][:, h, n - 1:n], bank[5][:, h * P:(h + 1) * P], ALU.mult, ALU.add)
                read("dve", f"S{i}", ins)
                taken(dve, f"S{i}")

            for i in range(-1, NTILE):
                if 0 < i + 2 < NTILE:
                    exponents(i + 2)
                if i + 1 < NTILE:
                    attention(i + 1)
                if 0 < i + 2 < NTILE:
                    operands(i + 2)
                if i >= 0:
                    output_and_state(i)
                if 0 < i + 2 < NTILE:
                    end_exponents(i + 2)
                    end_operands(i + 2)
            dve.wait_ge(s_ckr, 48)

            def fox_normalise(n_q):
                q = QT[n_q]
                n = ROWS[q]
                filled(dve, f"fo{q}")
                dve.wait_ge(s_pexp, (n_q + 1) * FH)
                ls = 60 + 8 * (n_q % 2)
                vlink(dve, V.reciprocal(st[0:n, ls:ls + 8], st[0:n, ls:ls + 8]))
                read("dve", f"fo{q}", V.tensor_tensor(
                    foxo[0:n, q, :].rearrange("p (h d) -> p h d", h=FH), bank[4 + n_q % 2][0:n, :].rearrange("p (h d) -> p h d", h=FH),
                    st[0:n, ls:ls + 8].unsqueeze(2).broadcast_to([n, FH, FD]), ALU.mult))

            def fox_gain(n_q):
                q = QT[n_q]
                n = ROWS[q]
                dve.wait_ge(s_rs, 7 + n_q)
                rstd(st[0:n, 85 + n_q:86 + n_q], st[0:n, 80 + n_q:81 + n_q], HW)
                V.scalar_tensor_tensor(foxo[0:n, q, :], foxo[0:n, q, :], st[0:n, 85 + n_q:86 + n_q], fgain[0:n, :], ALU.mult, ALU.mult).then_inc(s_fo, 1)

            for n_q, q in enumerate(QT):
                n = ROWS[q]
                L = (q + 1) * P if q < 4 else PAST + NDEC
                cb = (ckB if q < 4 else ckS)
                dve.wait_ge(s_mask, 1 + n_q)
                for h in range(FH):
                    m = n_q * FH + h
                    filled(dve, f"s{q}{h}")
                    if m >= 2:
                        pq, ph = (QT[(m - 2) // FH], (m - 2) % FH)
                        filled(dve, f"t{pq}{ph}")
                    read("dve", f"s{q}{h}", V.tensor_tensor_reduce(pp[h % 2][0:n, 0:L], bank[h % 2][0:n, 0:L], cb[0:n, h, 0:L],
                                                                   float(FD) ** -0.5, -3e38, ALU.add, ALU.max, st[0:n, 40 + h:41 + h]))
                    taken(dve, f"s{q}{h}")
                    V.tensor_scalar(st[0:n, 50 + h:51 + h], st[0:n, 40 + h:41 + h], -1.0, None, ALU.mult).then_inc(s_pmax, 1)
                    if n_q and h == 1:
                        fox_normalise(n_q - 1)
                    if n_q and h == 4:
                        fox_gain(n_q - 1)
            fox_normalise(4)
            fox_gain(4)
            for i in range(NTILE):
                n = ROWS[i]
                filled(dve, f"m{i}1")
                read("dve", f"m{i}1", V.tensor_copy(hT[:, 4:8, i * P:i * P + n],
                                                    bank[1][:, :].rearrange("p (k t) -> p k t", k=4)[:, :, 0:n]))
            dve.wait_ge(s_mod1, 96)
            for gi in range(2):
                n = P if gi == 0 else NDEC
                sc = mod2[0:n, gi, 0:D]
                ins = V.scalar_tensor_tensor(sc, sc, 1.0, ngain[0:n, :], ALU.add, ALU.mult)
            vlink(dve, ins)

            def scale_h2(i):
                n, gi = ROWS[i], i // 4
                dve.wait_ge(s_rs, 12 + i)
                rstd(st[0:n, 95 + i:96 + i], st[0:n, 90 + i:91 + i], D)
                V.scalar_tensor_tensor(h2[i][0:n, :], x[0:n, i, :], st[0:n, 95 + i:96 + i], mod2[0:n, gi, 0:D],
                                       ALU.mult, ALU.mult).then_inc(s_h2a, 1)

            for i in range(4):
                for c in range(2):
                    filled(dve, f"y{i}{c}")
                    if i:
                        dve.wait_ge(s_x2, 2 * (i - 1) + c + 1)
                    read("dve", f"y{i}{c}", V.tensor_tensor(gt[c], bank[4 + (2 * i + c) % 4][:, :],
                                                            mod1[:, 0, c * 512:(c + 1) * 512], ALU.mult))
                if i:
                    scale_h2(i - 1)
            filled(dve, "y40")
            dve.wait_ge(s_x2, 8)
            for j in range(4):
                ins = V.tensor_tensor(gt[j // 2][0:32, (j % 2) * 256:(j % 2) * 256 + 256], bank[4][32 * j:32 * j + 32, 0:256],
                                      mod1[0:32, 1, j * 256:(j + 1) * 256], ALU.mult)
            read("dve", "y40", ins)
            scale_h2(3)
            scale_h2(4)
            route(dve, V)
            def xt_high():
                V.tensor_copy(XT[:, 4:8, :], bank[1][:, 0:4 * ET].rearrange("p (k t) -> p k t", k=4)).then_inc(s_xtb, 1)

            def hidden(t, c):
                dve.wait_ge(s_sil, t * 2 + (c + 1))
                fs = slice(c * 256, (c + 1) * 256)
                V.tensor_tensor(he[0:ET, fs], hs[ET:2 * ET, fs], bank[2 + c][ET:2 * ET, 0:256], ALU.mult).then_inc(s_he, 1)

            def hidden_t(t, c):
                dve.wait_ge(s_ht, t * 2 + (c + 1))
                V.tensor_copy(heT[:, 2 * c:2 * c + 2, :], bank[4 + c][:, 0:2 * ET].rearrange("p (f t) -> p f t", f=2)).then_inc(s_hc, 1)

            dve.wait_ge(s_rd, 1)
            dve.sem_inc(s_yeb, 1)
            total = dve.value_load(base_i[0:1, NE:NE + 1], min_val=NE, max_val=MAXT)
            dve.wait_ge(s_xp, 1)
            xt_high()
            with dve.Fori(0, total) as t:
                hidden(t, 0)
                hidden(t, 1)
                hidden_t(t, 0)
                dve.wait_ge(s_xp, t + 2)
                xt_high()
                hidden_t(t, 1)
                dve.wait_ge(s_yd, t + 1)
                dve.wait_ge(s_yst, t * 16 + 16)
                V.tensor_copy(ysb[0:ET, 512:1024], bank[6][ET:2 * ET, :]).then_inc(s_yeb, 1)
            dve.wait_ge(s_ph3, 48)

            def combine(i):
                n, gi = ROWS[i], i // 4
                A_, B_ = ya[i][0:n, :], yb[i][0:n, :]
                dve.wait_ge(s_ga, i + 1)
                vlink(dve, V.scalar_tensor_tensor(A_, B_, gB[0:n, i:i + 1], A_, ALU.mult, ALU.add))
                V.tensor_tensor(A_, A_, gateF[0:n, gi, :], ALU.mult).then_inc(s_gated, 1)

            def normalise(i):
                n = ROWS[i]
                dve.wait_ge(s_rs, 17 + i)
                rstd(st[0:n, 105 + i:106 + i], st[0:n, 100 + i:101 + i], D)
                V.scalar_tensor_tensor(ya[i][0:n, :], x[0:n, i, :], st[0:n, 105 + i:106 + i], fing[0:n, :],
                                       ALU.mult, ALU.mult).then_inc(s_fin, 1)

            combine(0)
            combine(1)
            for i in range(NTILE):
                if i + 2 < NTILE:
                    combine(i + 2)
                normalise(i)

        def fox_values(pe, T, n_q, q, h, end=None):
            n = ROWS[q]
            taken(pe, f"t{q}{h}")
            widths = [P] * (q + 1) if q < 4 else [P, P, NDEC]
            hc = slice(h * FD, (h + 1) * FD)
            for j, w in enumerate(widths):
                if q < 4:
                    v = v_fox[:, j, hc]
                else:
                    v = vc[:, j, hc] if j < 2 else v_fox[0:NDEC, 4, hc]
                ins = T.matmul(bank[4 + n_q % 2][0:n, hc], pT[(h + 1) % 2][0:w, j, 0:n], v, start=(j == 0), stop=(j == len(widths) - 1))
            if end:
                end(f"fo{q}", ins)

        @block.tensor
        def _(pe):
            T = nc.tensor
            issued = []

            def begin(name):
                if before[name]:
                    taken(pe, before[name])

            def end(name, ins):
                assert where[name] == len(issued), (name, len(issued), plan[len(issued)])
                issued.append(name)
                ins.then_inc(pe_done, 1)

            def chunk(b, k4=4):
                return b[:, :].rearrange("p (k t) -> p k t", k=k4)

            pe.wait_ge(s_ident, 1)
            pe.wait_ge(s_c, 48)
            end("cT", T.transpose(bank[0][:, 0:24], crow[0:24, :], ident[0:24, 0:24]))

            def ada(r, b, first, stop):
                if first == 0:
                    begin(f"ada{r}")
                for k in range(first, stop):
                    loaded(pe, f"ada{r}_{k}")
                    w = wslot(f"ada{r}_{k}", SLOT)[:, 0, :]
                    for j in range(4):
                        ins = T.matmul(bank[b][32 * j:32 * j + 32, :], cpad[:, k, :], w[:, j * 512:(j + 1) * 512],
                                       start=(k == 0), stop=(k == KT - 1))
                if stop == KT:
                    end(f"ada{r}", ins)

            def turned(name, b, src, n, blocks):
                begin(name)
                for j in range(blocks):
                    ins = T.transpose(chunk(bank[b])[:, j, 0:n], src[0:n, j * P:(j + 1) * P], ident[0:n, 0:n])
                end(name, ins)

            def feature_major(name, wname):
                loaded(pe, wname)
                w = wslot(wname, HW)
                for h in range(4):
                    for c in range(2):
                        b = 4 + 2 * (h % 2) + c
                        begin(f"{name}{h}{c}")
                        for k in range(KT):
                            ins = T.matmul(bank[b][:, 0:HALF], w[:, k, h * P:(h + 1) * P], hT[:, k, c * HALF:(c + 1) * HALF],
                                           start=(k == 0), stop=(k == KT - 1))
                        end(f"{name}{h}{c}", ins)

            def token_major(name, i, b):
                w = wslot(name, HW)
                begin(f"{name}{i}")
                for k in range(KT):
                    if i < 4:
                        ins = T.matmul(bank[b][:, :], hT[:, k, i * P:(i + 1) * P], w[:, k, :], start=(k == 0), stop=(k == KT - 1))
                    else:
                        for j in range(4):
                            ins = T.matmul(bank[b][32 * j:32 * j + 32, 0:P], hT[:, k, SEQ:], w[:, k, j * P:(j + 1) * P],
                                           start=(k == 0), stop=(k == KT - 1))
                end(f"{name}{i}", ins)

            taken(pe, "cT")
            ada(0, 1, 0, 2)
            for i in range(NTILE):
                pe.wait_ge(s_h1, i + 1)
                for c in range(2):
                    turned(f"hT{i}{c}", 2 + 2 * (i % 2) + c, h1[i % 2][:, c * 512:(c + 1) * 512], ROWS[i], 4)
            ada(0, 1, 2, KT)
            taken(pe, "ada0")
            turned("modT", 0, msb, P, 4)
            pe.wait_ge(s_hma, 1)
            pe.wait_ge(s_hmd, 1)
            feature_major("hq", "hq")
            loaded(pe, "hg")
            for i in range(NTILE):
                token_major("hg", i, 2 + i % 2)
            ada(1, 1, 0, 4)
            feature_major("hf", "hf")
            ada(1, 1, 4, KT)
            loaded(pe, "hi")
            for i in range(NTILE):
                token_major("hi", i, 2 + i % 2)
            ada(2, 0, 0, 4)
            loaded(pe, "fk")
            for i in range(NTILE):
                token_major("fk", i, 4 + i % 2)
                if i:
                    taken(pe, f"fk{i - 1}")
                    turned(f"fkT{i - 1}", 6, fkt[(i - 1) % 2], ROWS[i - 1], 4)
            taken(pe, "fk4")
            turned("fkT4", 6, fkt[0], NDEC, 4)
            ada(2, 0, 4, KT)
            loaded(pe, "fv")
            for i in range(NTILE):
                token_major("fv", i, 2 + i % 2)
            feature_major("fq", "fq")
            pe.wait_ge(s_small, 64)
            for c in range(2):
                begin(f"ff{c}")
                for k in range(KT):
                    ins = T.matmul(bank[c][0:FH, 0:HALF], wff[:, k, :], hT[:, k, c * HALF:(c + 1) * HALF],
                                   start=(k == 0), stop=(k == KT - 1))
                end(f"ff{c}", ins)
            begin("lpT")
            for j in range(2):
                ins = T.transpose(bank[2][0:FH, j * P:(j + 1) * P], lpast[:, j, :], ident[:, :])
            end("lpT", ins)
            begin("lfT")
            pe.wait_ge(s_lf, 1)
            for i in range(NTILE):
                n = ROWS[i]
                c0 = i * P if i < 4 else SEQ + PAST
                ins = T.transpose(bank[3][0:n, i * FH:(i + 1) * FH], lf[0:8, c0:c0 + n], ident[0:8, 0:8])
            end("lfT", ins)

            def attention(i):
                n, t0 = ROWS[i], i * P
                Xi = X[i % 2]
                if i < 4:
                    begin(f"L{i}")
                    Lb = bank[0][:, 0:384].rearrange("p (h c) -> p h c", h=HGH)
                    pe.wait_ge(s_xm, level_operands(i, 2))
                    for h in range(HGH):
                        T.matmul(Lb[0:64, h, 0:64], Xi[:, 0, h, 0:64], Xi[:, 0, h, 64:128], start=True, stop=True)
                        for j in range(2):
                            ins = T.matmul(Lb[64 * j:64 * j + 32, h, 64:96], Xi[:, 1, h, 64 * j:64 * j + 32],
                                           Xi[:, 1, h, 64 * j + 32:64 * j + 64], start=True, stop=True)
                    end(f"L{i}", ins)
                for c, nm in enumerate(("Da", "Db")):
                    begin(f"{nm}{i}")
                    pe.wait_ge(s_xm, level_operands(i + 1, 0))
                    src = bank[1 + c][:, 0:384].rearrange("p (h l t) -> p h l t", h=2, l=6)
                    for hh in range(2):
                        h = 2 * c + hh
                        for lv in range(2, 8):
                            for j in range(n // 32):
                                b = slice(32 * j, 32 * j + 32)
                                tb = slice(t0 + 32 * j, t0 + 32 * j + 32)
                                left, right = (Xi[:, lv, h, b], Xi[:, lv, h, b]) if lv < 7 else (kk[:, h, tb], qs[:, h, tb])
                                ins = T.matmul(src[32 * j:32 * j + 32, hh, lv - 2, :], left, right, start=True, stop=True)
                    end(f"{nm}{i}", ins)

            def output_and_state(i):
                n = ROWS[i]
                begin(f"kT{i}")
                pe.wait_ge(s_qk, i + 1)
                for h in range(HGH):
                    ins = T.transpose(chunk(bank[3])[0:n, h, :], kE[i % 2][:, h, 0:n], ident[:, :])
                end(f"kT{i}", ins)
                begin(f"ho{i}")
                pe.wait_ge(s_att, i + 1)
                if 0 < i < 4:
                    taken(pe, f"S{i - 1}")
                if i == 4:
                    pe.wait_ge(s_S0, 16)
                for h in range(HGH):
                    o = bank[4][0:n, h * P:(h + 1) * P]
                    if i:
                        T.matmul(o, qE[i % 2][:, h, 0:n], (S if i < 4 else S_sample)[:, h, :], start=True, stop=False)
                    ins = T.matmul(o, attT[i % 2][0:n, h, 0:n], v_hg[0:n, i, h * P:(h + 1) * P], start=(i == 0), stop=True)
                end(f"ho{i}", ins)
                begin(f"S{i}")
                taken(pe, f"kT{i}")
                for h in range(HGH):
                    ins = T.matmul(bank[5][:, h * P:(h + 1) * P], kET[0:n, h, :], v_hg[0:n, i, h * P:(h + 1) * P], start=True, stop=True)
                end(f"S{i}", ins)

            for i in range(-1, NTILE):
                if i + 1 < NTILE:
                    attention(i + 1)
                if i >= 0:
                    output_and_state(i)

            pe.wait_ge(s_cache, 32)
            for c in range(2):
                turned(f"kcT{c}", 6 + c, kc[:, c, :], P, 4)
            m = 0
            for n_q, q in enumerate(QT):
                n = ROWS[q]
                qc = slice(q * P, q * P + n)
                for h in range(FH + 1):
                    if h < FH:
                        begin(f"s{q}{h}")
                        r = slice(64 * (h % 2), 64 * (h % 2) + 64)
                        lhs = fqT[r, h // 2, qc]
                        if q < 4:
                            ins = T.matmul(bank[h % 2][0:n, 0:(q + 1) * P], lhs, fkT[r, h // 2, 0:(q + 1) * P], start=True, stop=True)
                        else:
                            taken(pe, "kcT1")
                            T.matmul(bank[h % 2][0:n, 0:PAST], lhs, kcT[r, h // 2, :], start=True, stop=True)
                            ins = T.matmul(bank[h % 2][0:n, PAST:PAST + n], lhs, fkT[r, h // 2, qc], start=True, stop=True)
                        end(f"s{q}{h}", ins)
                    if h == 1 and n_q:
                        fox_values(pe, T, n_q - 1, QT[n_q - 1], FH - 1, end)
                    if h:
                        hh = h - 1
                        begin(f"t{q}{hh}")
                        m += 1
                        pe.wait_ge(s_pexp, m)
                        tb = chunk(bank[2 + h % 2])
                        widths = [P] * (q + 1) if q < 4 else [P, P, NDEC]
                        for j, w in enumerate(widths):
                            ins = T.transpose(tb[0:w, j, 0:n], pp[hh % 2][0:n, j * P:j * P + w], ident[0:n, 0:n])
                        end(f"t{q}{hh}", ins)
                        if hh == 1:
                            begin(f"fo{q}")
                        if hh:
                            fox_values(pe, T, n_q, q, hh - 1)
            fox_values(pe, T, 4, QT[4], FH - 1, end)

            for i in range(NTILE):
                n = ROWS[i]
                pe.wait_ge(s_fo, QT.index(i) + 1)
                turned(f"m{i}0", 0, G[:, i, :], n, 4)
                turned(f"m{i}1", 1, foxo[:, i, :], n, 4)
            taken(pe, "m40")
            taken(pe, "m41")
            pe.wait_ge(s_mod1, 96)
            for k in range(4):
                loaded(pe, f"wo{k}")

            def turn_h2(i):
                pe.wait_ge(s_h2, i + 1)
                for c in range(2):
                    turned(f"r{i}{c}", c, h2[i][:, c * 512:(c + 1) * 512], ROWS[i], 4)

            def router(i):
                n = ROWS[i]
                if i == 0:
                    begin("lg")
                taken(pe, f"r{i}0")
                taken(pe, f"r{i}1")
                for k in range(KT):
                    ins = T.matmul(bank[2][0:n, i * NE:(i + 1) * NE], h2T[i % 2][:, k, 0:n], wrt[:, k, :], start=(k == 0), stop=(k == KT - 1))
                if i == NTILE - 1:
                    end("lg", ins)

            for i in range(4):
                for c in range(2):
                    b = bank[4 + (2 * i + c) % 4]
                    begin(f"y{i}{c}")
                    for k in range(KT):
                        ins = T.matmul(b[:, :], hT[:, k, i * P:(i + 1) * P], wslot(f"wo{k // 2}", D)[:, k % 2, c * 512:(c + 1) * 512],
                                       start=(k == 0), stop=(k == KT - 1))
                    end(f"y{i}{c}", ins)
                if i == 3:
                    router(0)
                if i >= 2:
                    turn_h2(i - 2)
            begin("y40")
            for k in range(KT):
                for j in range(4):
                    ins = T.matmul(bank[4][32 * j:32 * j + 32, 0:256], hT[:, k, SEQ:], wslot(f"wo{k // 2}", D)[:, k % 2, j * 256:(j + 1) * 256],
                                   start=(k == 0), stop=(k == KT - 1))
            end("y40", ins)
            router(1)
            for i in range(2, NTILE):
                turn_h2(i)
                router(i)
            begin("cnt")
            pe.wait_ge(s_mk, 1)
            pe.wait_ge(s_rc, 1)
            for j in range(NTILE):
                ins = T.matmul(bank[4][:, 0:NE], ones, msk[:, j, :], start=(j == 0), stop=(j == NTILE - 1))
            end("cnt", ins)
            begin("pos")
            for i in range(NTILE):
                for j in range(i + 1):
                    ins = T.matmul(bank[3][:, i * NE:(i + 1) * NE], tri if j == i else ones, msk[:, j, :], start=(j == 0), stop=(j == i))
            end("pos", ins)

            def transpose_rows():
                for k in range(KT):
                    ins = T.transpose(bank[k // 4][:, (k % 4) * ET:(k % 4 + 1) * ET], xg[0:ET, k * P:(k + 1) * P], ident[0:ET, 0:ET])
                ins.then_inc(s_xp, 1)

            def transpose_hidden(t, c):
                pe.wait_ge(s_he, t * 2 + (c + 1))
                pe.sem_inc(s_begun, 1)
                for f in range(2):
                    ins = T.transpose(bank[4 + c][:, f * ET:(f + 1) * ET], he[0:ET, (2 * c + f) * P:(2 * c + f + 1) * P],
                                      ident[0:ET, 0:ET])
                ins.then_inc(s_ht, 1)

            taken(pe, "pos")
            pe.wait_ge(s_rd, 1)
            pe.wait_ge(s_gath, 16)
            transpose_rows()

            def expert(par, e, loads_done):
                Wg, Wu, Wd = wexp(par)
                pe.wait_ge(s_we[par], loads_done)
                nt = pe.value_load(ntile_i[0:1, bass.ds(e, 1)], min_val=1, max_val=CAPT)
                base = pe.value_load(base_i[0:1, bass.ds(e, 1)], min_val=0, max_val=MAXT)
                with pe.Fori(0, nt) as i:
                    t = base + i
                    pe.wait_ge(s_xta, t + 1)
                    pe.wait_ge(s_xtb, t + 1)
                    for c in range(2):
                        for k in range(KT):
                            for half, w in enumerate((Wg, Wu)):
                                ins = T.matmul(bank[2 + c][ET * half:ET * half + ET, 0:256], XT[:, k, :],
                                               w[:, k, c * 256:(c + 1) * 256], start=(k == 0), stop=(k == KT - 1))
                        ins.then_inc(s_gu, 1)
                    transpose_hidden(t, 0)
                    pe.wait_ge(s_gath, t * 16 + 32)
                    pe.sem_inc(s_begun, 1)
                    transpose_rows()
                    transpose_hidden(t, 1)
                    pe.wait_ge(s_yea, t + 1)
                    pe.wait_ge(s_yeb, t + 1)
                    for f in range(FT):
                        if f % 2 == 0:
                            pe.wait_ge(s_hc, t * 2 + (f // 2 + 1))
                        for half in range(2):
                            ins = T.matmul(bank[6][ET * half:ET * half + ET, :], heT[:, f, :],
                                           Wd[:, f, half * 512:(half + 1) * 512], start=(f == 0), stop=(f == FT - 1))
                    ins.then_inc(s_yd, 1)

            with pe.Fori(0, NE // 3) as three:
                for par in range(3):
                    expert(par, three * 3 + par, three * 48 + 48)
            expert(0, NE - 1, (NE // 3 + 1) * 48)


_INS = ['x_prompt', 'x_sample', 'cache_fox_k', 'cache_fox_v', 'cache_fox_logf', 'state_hgrn', 'c_prompt', 'c_sample',
        'norm_mix_gain', 'norm_ffn_gain', 'w_ada', 'b_ada', 'w_in', 'hg_lower_bounds', 'hg_norm_gain', 'fox_f_bias',
        'fox_out_gain', 'w_out', 'w_router', 'b_router', 'w_exp_gate', 'w_exp_up', 'w_exp_down', 'final_norm_gain']
_OUTS = [('y_prompt', (1, 512, 1024)), ('y_sample', (1, 32, 1024)), ('hgrn_state_prompt', (1, 1, 4, 128, 128)),
         ('fox_k_prompt', (1, 1, 512, 8, 64)), ('fox_v_prompt', (1, 1, 512, 8, 64)), ('fox_logf_prompt', (1, 1, 512, 8)),
         ('hgrn_state_sample', (1, 1, 4, 128, 128)), ('fox_k_sample', (1, 1, 32, 8, 64)), ('fox_v_sample', (1, 1, 32, 8, 64)),
         ('fox_logf_sample', (1, 1, 32, 8))]


def kernel(**inputs):
    import numpy as _np
    import concourse.bacc as _bacc
    from concourse import mybir as _mybir
    from concourse.bass_utils import run_bass_kernel_spmd as _run

    nc = _bacc.Bacc("TRN2", target_bir_lowering=False, num_devices=1)
    arrays, args, outs = {}, {}, {}
    for name in _INS:
        if name == 'hg_lower_bounds':
            continue
        v = _np.ascontiguousarray(inputs[name])
        arrays[f"in_{name}"] = v
        args[name] = nc.dram_tensor(f"in_{name}", v.shape, _mybir.dt.from_np(v.dtype), kind="ExternalInput").ap()
    for name, shape in _OUTS:
        outs[name] = nc.dram_tensor(f"out_{name}", shape, _mybir.dt.float32, kind="ExternalOutput").ap()
    build(nc, args, outs)
    r = _run(nc, [arrays], core_ids=[0])
    return tuple(r.results[0][f"out_{name}"] for name, _ in _OUTS)
```

```python
from contextlib import ExitStack

import concourse.bass as bass
from concourse import mybir

F32 = mybir.dt.float32
I32 = mybir.dt.int32
ALU = mybir.AluOpType
ACT = mybir.ActivationFunctionType
AX = mybir.AxisListType

P = 128
D = 1024
KT = D // P
SEQ, NDEC, PAST = 512, 32, 256
TOK = SEQ + NDEC
HALF = TOK // 2
NTILE = 5
ROWS = [P] * 4 + [NDEC]
HGH, HW = 4, 512
FH, FD = 8, 64
NE, NG, EPG = 16, 4, 4
DE = 512
FT = DE // P
ET = 64
CAPT = (TOK + ET - 1) // ET
MAXT = NE + 2 * TOK // ET
EPS = 1e-6
SLOT = 2048
LEVELS = [64, 32, 16, 8, 4, 2, 1]
NEG = -1e30


def wide(ap):
    return ap.unsqueeze(2).broadcast_to([P, NTILE, NE])


def levels(n):
    return [i for i, half in enumerate(LEVELS) if 2 * half <= n]


def bcast(ap, parts):
    return ap.partition_broadcast(parts)


def build(nc, a, out):
    ctx = ExitStack()
    with ctx:
        def sb(name, shape, dt=F32):
            return ctx.enter_context(nc.sbuf_tensor(name, shape, dt))

        def sem(name):
            return ctx.enter_context(nc.semaphore(name))

        W = sb("weights", [P, 12 * SLOT])
        x = sb("x", [P, NTILE, D])
        hT = sb("hT", [P, KT, TOK])
        R = sb("R", [P, 18560])
        ident = sb("ident", [P, P])
        cpad = sb("cpad", [P, KT, 32])
        st = sb("stats", [P, 160])
        bank = [ctx.enter_context(nc.psum_tensor(f"bank{i}", [P, 512], F32)) for i in range(8)]

        def view(t, off, *shape):
            n = 1
            for s in shape:
                n *= s
            v = t[:, off:off + n]
            if len(shape) == 2:
                v = v.rearrange("p (a b) -> p a b", b=shape[1])
            if len(shape) == 3:
                v = v.rearrange("p (a b c) -> p a b c", b=shape[1], c=shape[2])
            return v

        hflat = hT[:, :, :].rearrange("p k t -> p (k t)")
        WA = 8 * SLOT
        qs = view(R, 0, HGH, TOK)
        kk = view(R, 2176, HGH, TOK)
        bb = view(R, 4352, HGH, TOK)
        v_hg = view(R, 6528, NTILE, HW)
        G = view(R, 9088, NTILE, HW)
        v_fox = view(R, 11648, NTILE, HW)
        fqT = view(R, 14208, 4, TOK)
        fkT = view(R, 16384, 4, TOK)
        foxo = v_hg
        xflat = x[:, :, :].rearrange("p n d -> p (n d)")
        X = [view(t, 0, 7, HGH, P) for t in (W, xflat)]
        E = [view(t, 3584, HGH, P) for t in (W, xflat)]
        qE = [view(t, 4096, HGH, P) for t in (W, xflat)]
        kE = [view(t, 4608, HGH, P) for t in (W, xflat)]
        attT = [view(W, 5120 + 512 * n, HGH, P) for n in range(2)]
        squares = view(W, WA + 5632, HGH, P)
        S_sample = view(W, 6144, HGH, P)
        kET = view(W, WA + 5120, HGH, P)
        att6 = view(W, WA + 6144, 2, 6, 32)
        attd = view(W, WA + 6528, HGH, 32)
        S = view(W, WA + 6656, HGH, P)
        hgain = view(W, WA + 7168, HW)
        lmask = view(W, WA + 7680, 6, 32)
        ip, it, ix = (view(W, WA + 6144 + 32 * n, 32).bitcast(I32) for n in range(3))
        mgt, mxf, mtmp = (view(W, WA + 6240 + 32 * n, 32) for n in range(3))
        h1 = [view(W, WA, D), view(W, WA + D, D)]
        fr = view(W, WA, TOK)
        ex = view(W, WA + 544, TOK)
        lg = view(W, WA + 1088, TOK)
        fkt = [view(W, WA + 1632, HW), view(W, WA + 2144, HW)]
        cf = view(W, WA + 3584, 800)
        msb = view(W, WA + 4608, HW)
        badd = view(W, WA + 5120, HW)
        ssel = view(W, WA + 2656, 800)
        lfo = view(W, WA + 3456, NTILE, FH)
        lpast = view(W, WA + 3496, 2, FH)
        fbias = view(W, WA + 3512, 1)
        crow = view(R, 5120, P)
        modT = view(R, 5248, 2, 2 * KT)
        gainT = view(R, 5280, KT)
        ckB = view(W, WA, FH, SEQ)
        ckS = view(W, 4 * SLOT, FH, PAST + NDEC)
        fgain = view(W, 4 * SLOT + 2304, HW)
        kc = view(hflat, 0, 2, HW)
        vc = view(hflat, D, 2, HW)
        kcT = view(hflat, 2 * D, 4, PAST)
        lf = view(W, 6656, 800)
        pp = [view(W, 0, 512), view(W, 512, 512)]
        pT = [view(W, 1024, 4, P), view(W, 1536, 4, P)]
        osq = view(W, 2048, HW)
        wff = view(W, WA + 7872, KT, FH)
        fq_odd = view(R, 4352, 4, TOK)
        mod1 = view(R, 0, 2, 2 * D)
        mod2 = view(W, WA + 4096, 2, D)
        ngain = view(W, WA + 7168, D)
        wrt = view(R, 5776, KT, NE)
        gt = [view(W, WA + 3072, 512), view(W, WA + 3584, 512)]
        h2 = [view(R, 6528 + n * D, D) for n in range(NTILE)]
        h2T = [view(W, WA + 6144, KT, P), view(W, WA + 7168, KT, P)]

        def dram(name, shape, dt=F32):
            return nc.dram_tensor(name, shape, dt, kind="Internal").ap()
        mod_d = dram("mod_d", (2, 6 * D))
        ck_d = dram("ck_d", (FH, SEQ))
        cks_d = dram("cks_d", (FH, PAST + NDEC))
        h2_d = dram("h2_d", (TOK, D))
        y_d = dram("y_d", (2 * TOK, D))

        plan, where = [], {}

        def grp(name, b, eng):
            where[name] = len(plan)
            plan.append((name, b, eng))

        grp("cT", 0, "act")
        for i in range(NTILE):
            grp(f"hT{i}0", 2 + 2 * (i % 2), "act")
            grp(f"hT{i}1", 3 + 2 * (i % 2), "act")
        grp("ada0", 1, "dve")
        grp("modT", 0, "dve")
        for h in range(HGH):
            grp(f"hq{h}0", 4 + 2 * (h % 2), "act")
            grp(f"hq{h}1", 5 + 2 * (h % 2), "act")
        for i in range(NTILE):
            grp(f"hg{i}", 2 + i % 2, "act")
        for h in range(HGH):
            grp(f"hf{h}0", 4 + 2 * (h % 2), "dve")
            grp(f"hf{h}1", 5 + 2 * (h % 2), "dve")
        grp("ada1", 1, "dve")
        for i in range(NTILE):
            grp(f"hi{i}", 2 + i % 2, "dve")
        for i in range(NTILE):
            grp(f"fk{i}", 4 + i % 2, "act")
            if i:
                grp(f"fkT{i - 1}", 6, "dve")
        grp("fkT4", 6, "dve")
        grp("ada2", 0, "dve")
        grp("ff0", 0, "dve")
        grp("ff1", 1, "dve")
        grp("lpT", 2, "dve")
        schedule = [("fv", i) for i in range(NTILE)] + [("fq", h, c) for h in range(4) for c in range(2)]
        for step, after in reversed(list(zip(range(-1, NTILE), (1, 4, 6, 8, 10, 11)))):
            schedule.insert(after + 1, ("hgrn", step))
        schedule.insert(1, ("lfT",))
        for item in schedule:
            if item[0] == "lfT":
                grp("lfT", 3, "dve")
            elif item[0] == "fv":
                grp(f"fv{item[1]}", 6 + item[1] % 2, "dve")
            elif item[0] == "fq":
                grp(f"fq{item[1]}{item[2]}", 6 + (item[2] + 1) % 2, "act")
            else:
                i = item[1]
                if i + 1 < NTILE:
                    if i + 1 < 4:
                        grp(f"L{i + 1}", 0, "dve")
                    grp(f"Da{i + 1}", 1, "dve")
                    grp(f"Db{i + 1}", 2, "dve")
                if i >= 0:
                    grp(f"kT{i}", 3, "act")
                    grp(f"ho{i}", 4, "dve")
                    grp(f"S{i}", 5, "dve")
        QT = [3, 2, 1, 0, 4]
        for n, q in enumerate(QT):
            if n == 3:
                grp("kcT0", 6, "act")
                grp("kcT1", 7, "act")
            for h in range(FH + 1):
                if h < FH:
                    grp(f"s{q}{h}", h % 2, "dve")
                if h == 1 and n:
                    grp(f"fo{QT[n - 1]}", 4 + (n - 1) % 2, "dve")
                if h:
                    grp(f"t{q}{h - 1}", 2 + h % 2, "act")
        grp(f"fo{QT[4]}", 4, "dve")
        for i in range(NTILE):
            grp(f"m{i}0", (0, 2)[i % 2], "act")
        for i in range(NTILE):
            grp(f"m{i}1", (1, 3)[i % 2], "dve")
        for i in range(NTILE):
            for c in range(2 if i < 4 else 1):
                grp(f"y{i}{c}", 4 + (2 * i + c) % 4, "dve")
            if i >= 2:
                grp(f"r{i - 2}0", 0, "act")
                grp(f"r{i - 2}1", 1, "act")
        for i in (3, 4):
            grp(f"r{i}0", 0, "act")
            grp(f"r{i}1", 1, "act")
        grp("lg", 2, "dve")
        grp("pos", 3, "dve")
        grp("tab", 5, "dve")

        pe_done = sem("pe_done")
        read_out = {"act": sem("act_read_out"), "dve": sem("dve_read_out")}
        rank, before, last = {}, {}, {}
        count = {"act": 0, "dve": 0}
        for name, b, eng in plan:
            count[eng] += 1
            rank[name] = (eng, count[eng])
            before[name] = last.get(b)
            last[b] = name

        def filled(eng, name):
            eng.wait_ge(pe_done, where[name] + 1)

        def taken(eng, name):
            who, n = rank[name]
            eng.wait_ge(read_out[who], n)

        order = {"act": [], "dve": []}

        def read(eng, name, ins):
            assert rank[name] == (eng, len(order[eng]) + 1), name
            order[eng].append(name)
            ins.then_inc(read_out[eng], 1)

        s_ident = sem("ident_ready")
        s_iota = sem("mask_iotas_ready")
        s_cpad = sem("cpad_zeroed")
        s_x = [sem(f"x_in{i}") for i in range(NTILE)]
        s_c = sem("c_in")
        s_small = sem("small_in")
        s_badd = sem("ada_bias_in")
        s_modw = sem("mod_rows_out")
        s_w = [sem(f"slot{i}_in") for i in range(8)]
        s_ss = sem("x_squares_summed")
        s_h1 = sem("x_normalised")
        s_modT = sem("modT_ready")
        s_hma = sem("hT_low_modulated")
        s_hmd = sem("hT_high_modulated")
        s_qs = sem("q_scaled")
        s_G = sem("gate_gained")
        s_ln = sem("softplus_ready")
        s_kx = sem("k_exponent_ready")
        s_kk = sem("k_ready")
        s_lf = sem("fox_logf_ready")
        s_cf = sem("fox_cumsum_ready")
        s_kout = [sem(f"fox_k_stored{i}") for i in range(2)]
        s_vout = sem("fox_v_stored")
        s_lout = sem("fox_logf_stored")
        s_ckw = sem("ck_rows_out")
        s_ckr = sem("ck_rows_in")
        s_cache = sem("caches_in")
        s_sout = sem("state_stored")
        s_S0 = sem("sample_state_in")
        s_lv = sem("level_exponents")
        s_ke = sem("end_exponents")
        s_le = sem("level_exps")
        s_zero = sem("attention_zeroed")
        s_xm = sem("level_operands_ready")
        s_qk = sem("qE_kE_ready")
        s_att = sem("attention_ready")
        s_sq = sem("ho_squares_summed")
        s_split = sem("queries_split")
        s_mask = sem("ck_masked")
        s_pexp = sem("fox_exp_ready")
        s_fq = sem("fox_squares_summed")
        s_fo = sem("fox_out_ready")
        s_mod1 = sem("mod12_in")
        s_x2 = sem("x2_half_ready")
        s_x2q = sem("x2_squares_summed")
        s_h2a = sem("h2_scaled")
        s_h2 = sem("h2_ready")
        s_h2s = sem("h2_sample_ready")
        s_h2w = [sem(f"h2_stored{i}") for i in range(2)]
        s_brt = sem("router_weights_in")
        s_rc = sem("routing_constants_ready")
        s_lx = sem("logits_centered")
        s_lex = sem("logits_exp")
        s_mk = sem("expert_mask_ready")
        s_oh = sem("onehots_ready")
        s_rd = sem("routing_ready")
        s_dv = sem("dve_step")
        s_ac = sem("act_step")
        s_pl = sem("pool_step")

        steps = {"dve": 0, "act": 0, "pool": 0}

        def vlink(dve, ins):
            steps["dve"] += 1
            ins.then_inc(s_dv, 1)
            dve.wait_ge(s_dv, steps["dve"])

        def alink(act, ins):
            steps["act"] += 1
            ins.then_inc(s_ac, 1)
            act.wait_ge(s_ac, steps["act"])

        def plink(pool, ins):
            steps["pool"] += 1
            ins.then_inc(s_pl, 1)
            pool.wait_ge(s_pl, steps["pool"])

        def both(eng, pair):
            eng.wait_ge(pair[0], 48)
            eng.wait_ge(pair[1], 32)

        def level_operands(i, n):
            return sum(len(levels(ROWS[j])) for j in range(i)) + n

        block = ctx.enter_context(nc.Block())
        w_ada = a["w_ada"].rearrange("l (k p) n -> p (l k) n", p=P)
        w_in = a["w_in"].rearrange("l (k p) n -> p (l k) n", p=P)
        w_out = a["w_out"].rearrange("l (k p) n -> p (l k) n", p=P)
        HQ, HF, HI, HG, FQ, FK, FV, FF = (512 * i for i in range(8))

        ring = [(f"ada0_{k}", k % 6, 1) for k in range(KT)]
        ring += [("hq", 6, 2), ("hg", 4, 2)] + [(f"ada1_{k}", k, 1) for k in range(4)]
        ring += [("hf", 6, 2), ("hi", 4, 2)] + [(f"ada1_{k}", k - 4, 1) for k in range(4, 8)]
        ring += [("fk", 6, 2)] + [(f"ada2_{k}", k, 1) for k in range(4)]
        ring += [("fv", 4, 2)] + [(f"ada2_{k}", k - 4, 1) for k in range(4, 8)]
        ring += [("fq", 6, 2)]
        ring += [(f"wo{k}", (2, 3, 6, 7)[k], 1) for k in range(4)]
        lastuse = {"hq": "hq31", "hg": "hg4", "hf": "hf31", "hi": "hi4", "fk": "fk4", "fv": "fv4", "fq": "fq31"}
        for r, first in enumerate(("hT00", "hf00", "fk0")):
            for k in range(KT):
                lastuse[f"ada{r}_{k}"] = first if k < (2 if r == 0 else 4) else f"ada{r}"
        loads = {}
        slot_count = [0] * 8
        slot_owner = [None] * 8
        for name, s, n in ring:
            slot_count[s] += 16
            loads[name] = (s, slot_count[s], n, [slot_owner[j] for j in range(s, s + n)])
            for j in range(s, s + n):
                slot_owner[j] = name

        def loaded(eng, name):
            s, value, _, _ = loads[name]
            eng.wait_ge(s_w[s], value)

        def wslot(name, width):
            s, _, n, _ = loads[name]
            return view(W, s * SLOT, n * SLOT // width, width)

        s_we = [[sem(f"expert_buffer{n}_{c}_in") for c in ("even", "odd")] for n in range(3)]
        s_released = sem("memory_released")
        s_gath = sem("rows_gathered")
        s_idx = sem("index_copied")
        s_xp = sem("rows_transposed")
        s_xta = sem("xT_low_ready")
        s_xtb = sem("xT_high_ready")
        s_gu = sem("gate_up_half_done")
        s_sil = sem("silu_done")
        s_he = sem("hidden_ready")
        s_begun = sem("transposes_begun")
        s_ht = sem("hidden_transposed")
        s_hc = sem("hiddenT_ready")
        s_yd = sem("down_done")
        s_yea = sem("y_low_read")
        s_yeb = sem("y_high_read")
        s_yst = sem("y_stored")
        xg = view(R, 0, D)
        XT = view(R, D, KT, ET)
        heT = view(R, D + 512, FT, ET)
        hs = view(R, 2 * D, DE)
        he = view(R, 2 * D + 512, DE)
        ysb = view(R, 3 * D, D)
        T0 = 4 * D
        prb = view(R, T0, NTILE, NE)
        sel = view(R, T0 + 80, NTILE, NE)
        msk6 = view(R, 5904, NTILE + 1, NE)
        msk = msk6[:, 0:NTILE, :]
        cmps = [view(R, 320 * n, NTILE * NG, EPG, EPG) for n in range(2)]
        before4 = view(R, T0 + 160, EPG, EPG)
        gts = view(R, T0 + 240, NTILE, NE)
        t80 = [view(R, T0 + 320 + 80 * n, NTILE, NE) for n in range(6)]
        g20 = [view(R, T0 + 800 + 20 * n, NTILE, NG) for n in range(8)]
        brt = view(R, T0 + 960, NE)
        s5 = [view(R, T0 + 992 + 8 * n, NTILE) for n in range(6)]
        gA, gB = view(R, T0 + 912, NTILE), view(R, T0 + 920, NTILE)
        tri = view(R, T0 + 1072, P)
        ones = view(R, T0 + 1200, P)
        tf = [view(R, T0 + 1328 + 16 * n, NE) for n in range(4)]
        cnt_i = view(R, T0 + 1392, NE).bitcast(I32)
        ntile_i = view(R, T0 + 1408, NE).bitcast(I32)
        base_i = view(R, T0 + 1424, NE + 1).bitcast(I32)
        idx1 = view(R, T0 + 1441, 1).bitcast(I32)
        idx2 = view(R, T0 + 1442, 1).bitcast(I32)
        dst = view(R, T0 + 1444, 2 * NTILE)
        dst_i = view(R, T0 + 1454, 2 * NTILE).bitcast(I32)
        tile_i = view(R, T0 + 1072 - 32, 2 * NTILE).bitcast(I32)
        dst_r = view(R, T0 + 976, 2 * NTILE)
        dst_t = view(R, T0 + 1056, 2 * NTILE)
        entry = view(R, T0 + 1464, 2 * NTILE, 2)
        iota_r = view(R, T0 + 1484, ET)
        iota_t = view(R, T0 + 1548, MAXT + 2)
        tseq = view(R, T0 + 1584, MAXT + 2, 2).bitcast(I32)
        row_hot = view(R, 640, 2 * NTILE, ET)
        tile_hot = view(R, 1280, 2 * NTILE, MAXT + 2)
        tile_entry = view(R, 1664, 2 * NTILE, MAXT + 2, 2)
        ya = [view(W, 6 * SLOT + n * D, D) for n in range(NTILE)]
        yb = [view(W, 6 * SLOT + (NTILE + n) * D, D) for n in range(NTILE)]
        gateF = view(hflat, 0, 2, D)
        fing = view(hflat, 2 * D, D)
        jk = view(hflat, 3 * D, D)
        s_ya = [sem(f"y_rows_in{i}") for i in range(NTILE)]
        s_ph3 = sem("final_in")
        s_ga = sem("higher_output_gated")
        s_gated = sem("combined_and_gated")
        s_comb = sem("residual_added")
        s_fsq = sem("final_square")
        s_fin = sem("final_ready")
        s_out = [sem(f"y_out{i}") for i in range(2)]

        wg = a["w_exp_gate"].rearrange("l e (k p) f -> p (l e) k f", p=P)
        wu = a["w_exp_up"].rearrange("l e (k p) f -> p (l e) k f", p=P)
        wd = a["w_exp_down"].rearrange("l e (k p) f -> p (l e) k f", p=P)

        wmem = [(W, 0), (W, 6 * SLOT), (R, 18560 - 6 * SLOT)]

        def wexp(par):
            t, b = wmem[par]
            return (view(t, b, KT, DE), view(t, b + 2 * SLOT, KT, DE), view(t, b + 4 * SLOT, FT, D))

        def load_piece(sp, par, place, e, piece, two_before):
            if two_before:
                sp.wait_ge(*two_before)
            dst = wexp(par)[piece // 2]
            src = (wg, wu, wd)[piece // 2][:, bass.ds(e, 1), :, :].rearrange("p o k f -> p (o k) f")
            ks = dst.shape[1] // 2
            ks = slice((piece % 2) * ks, (piece % 2 + 1) * ks)
            sp.dma_start(dst[:, ks, :], src[:, ks, :]).then_inc(s_we[par][place % 2], 16)

        def load_x(sp):
            for i in range(4):
                sp.dma_start(x[:, i, :], a["x_prompt"][0, i * P:(i + 1) * P, :]).then_inc(s_x[i], 16)
            sp.dma_start(x[0:NDEC, 4, :], a["x_sample"][0]).then_inc(s_x[4], 16)

        @block.sync
        def _(sp):
            sp.dma_start(crow[0:8, :], a["c_prompt"].rearrange("b (k q) -> (b k) q", q=P)).then_inc(s_c, 16)
            sp.dma_start(crow[8:16, :], a["c_sample"].rearrange("b (k q) -> (b k) q", q=P)).then_inc(s_c, 16)
            sp.dma_start(crow[16:24, :], a["norm_mix_gain"].rearrange("l (k q) -> (l k) q", q=P)).then_inc(s_c, 16)
            load_x(sp)
            cols = {"hq": HQ, "hg": HG, "hf": HF, "hi": HI, "fk": FK, "fv": FV, "fq": FQ}
            for name, _, _ in ring:
                s, value, n, owners = loads[name]
                if name == "wo0":
                    taken(sp, "S3")
                    load_x(sp)
                    sp.wait_ge(s_sout, 32)
                for o in dict.fromkeys(owners):
                    if o is not None:
                        filled(sp, lastuse[o])
                if name.startswith("ada"):
                    r, k = int(name[3]), int(name[5])
                    sp.dma_start(wslot(name, SLOT)[:, 0, :], w_ada[:, k, r * SLOT:(r + 1) * SLOT]).then_inc(s_w[s], 16)
                elif name.startswith("wo"):
                    k = int(name[2])
                    sp.dma_start(wslot(name, D), w_out[:, 2 * k:2 * k + 2, :]).then_inc(s_w[s], 16)
                else:
                    sp.dma_start(wslot(name, HW), w_in[:, :, cols[name]:cols[name] + HW]).then_inc(s_w[s], 16)
            recent = [None, None]

            def first_pieces(e, places, pieces):
                for place, piece in zip(places, pieces):
                    load_piece(sp, e, place, e, piece, recent.pop(0))
                    recent.append((s_we[e][place % 2], 16 * (place // 2 + 1)))

            sp.wait_ge(s_fo, NTILE)
            sp.wait_ge(s_vout, 16 * NTILE)
            first_pieces(0, range(4), (0, 1, 4, 5))
            first_pieces(2, range(3), (5, 4, 3))
            filled(sp, "y40")
            first_pieces(0, (4, 5), (2, 3))
            first_pieces(1, (0, 1), (0, 1))
            sp.wait_ge(s_x2, 2 * NTILE)
            first_pieces(1, (2, 3), (2, 3))
            filled(sp, "lg")
            first_pieces(1, (4, 5), (4, 5))
            both(sp, s_h2w)
            sp.wait_ge(s_gath, 16)
            first_pieces(2, range(3, 6), (0, 1, 2))
            for gi in range(2):
                n = P if gi == 0 else NDEC
                sp.dma_start(gateF[0:n, gi, :], bcast(mod_d[gi, 5 * D:6 * D], n)).then_inc(s_ph3, 16)
            sp.dma_start(fing, bcast(a["final_norm_gain"], P)).then_inc(s_ph3, 16)
            sp.wait_ge(s_rd, 1)

            def next_expert(par, e, uses):
                done = sp.value_load(base_i[0:1, bass.ds(e - 2, 1)], min_val=1, max_val=MAXT)
                for piece in range(6):
                    if piece == 0:
                        sp.wait_ge(s_gu, done * 2)
                        sp.sem_inc(s_released, 1)
                    if piece == 4:
                        sp.wait_ge(s_yd, done)
                        sp.sem_inc(s_released, 1)
                    if piece < 2:
                        before = (s_we[par - 1][piece], uses * 48 + 48 if par else uses * 48)
                    else:
                        before = (s_we[par][piece % 2], uses * 48 + 16 * (piece // 2))
                    load_piece(sp, par, piece, e, piece, before)

            with sp.Fori(1, NE // 3) as three:
                for par in range(3):
                    next_expert(par, three * 3 + par, three)
            next_expert(0, NE - 1, NE // 3)
            total = sp.value_load(base_i[0:1, NE:NE + 1], min_val=NE, max_val=MAXT)
            sp.wait_ge(s_yd, total)
            sp.wait_ge(s_yst, total * 16 + 16)

            def load_y(i):
                n = ROWS[i]
                sp.dma_start(ya[i][0:n, :], y_d[i * P:i * P + n, :]).then_inc(s_ya[i], 16)
                sp.dma_start(yb[i][0:n, :], y_d[TOK + i * P:TOK + i * P + n, :]).then_inc(s_ya[i], 16)

            for i in range(NTILE):
                load_y(i)
            for i in range(NTILE):
                n = ROWS[i]
                sp.wait_ge(s_fin, i + 1)
                sp.dma_start(out["y_prompt"][0, i * P:i * P + n, :] if i < 4 else out["y_sample"][0],
                             ya[i][0:n, :]).then_inc(s_out[i % 2], 16)
            both(sp, s_out)
            both(sp, s_kout)
            sp.wait_ge(s_vout, 16 * NTILE)
            sp.wait_ge(s_lout, 32)
            sp.wait_ge(s_sout, 32)

        @block.gpsimd
        def _(pool):
            g = nc.gpsimd
            plink(pool, g.memset(st[:], 0.0))
            plink(pool, g.memset(st[:, 126:127], EPS))
            plink(pool, g.memset(ident[:], 0.0))
            g.affine_select(ident[:], ident[:], [[-1, P]], ALU.not_equal, 1.0, base=0,
                            channel_multiplier=1).then_inc(s_ident, 1)
            g.memset(cpad[:], 0.0).then_inc(s_cpad, 1)
            g.iota(ip, [[0, 32]], base=0, channel_multiplier=1)
            g.iota(it, [[1, 32]], base=0, channel_multiplier=0).then_inc(s_iota, 1)
            bada = a["b_ada"].rearrange("l (r j n) -> r (l j) n", r=3, j=4)
            plink(pool, g.memset(badd, 0.0))

            def bias_rows(r):
                for gi in range(2):
                    pool.dma_start(badd[gi:gi + 97:32, :], bada[r]).then_inc(s_badd, 16)

            def mod_rows(r):
                taken(pool, f"ada{r}")
                for gi in range(2):
                    pool.dma_start(mod_d[gi, r * SLOT:(r + 1) * SLOT].rearrange("(j n) -> j n", j=4),
                                   msb[gi:gi + 97:32, :]).then_inc(s_modw, 16)
                pool.wait_ge(s_modw, 32 * r)

            bias_rows(0)
            taken(pool, "ada0")
            pool.dma_start(hgain, bcast(a["hg_norm_gain"][0], P)).then_inc(s_small, 16)
            pool.dma_start(wff, w_in[:, :, FF:FF + FH]).then_inc(s_small, 16)
            pool.dma_start(fbias[0:8, :], a["fox_f_bias"].rearrange("l h -> h l")).then_inc(s_small, 16)
            pool.dma_start(lpast, a["cache_fox_logf"].rearrange("l b (j p) h -> p (l b j) h", p=P)).then_inc(s_small, 16)
            bias_rows(1)
            pool.wait_ge(s_small, 64)
            for h in range(HGH):
                taken(pool, f"hq{h}1")
                g.tensor_scalar(qs[:, h, :], qs[:, h, :], float(P) ** -0.5, None, ALU.mult).then_inc(s_qs, 1)
            for i in range(NTILE):
                n = ROWS[i]
                taken(pool, f"hg{i}")
                g.tensor_tensor(G[0:n, i, :], G[0:n, i, :], hgain[0:n, :], ALU.mult).then_inc(s_G, 1)
            kout = out["fox_k_prompt"].rearrange("l b t h d -> (l b t) (h d)")
            vout = out["fox_v_prompt"].rearrange("l b t h d -> (l b t) (h d)")
            kous = out["fox_k_sample"].rearrange("l b t h d -> (l b t) (h d)")
            vous = out["fox_v_sample"].rearrange("l b t h d -> (l b t) (h d)")
            mod_rows(1)
            bias_rows(2)
            for i in range(NTILE):
                taken(pool, f"fk{i}")
                pool.dma_start(kout[i * P:(i + 1) * P, :] if i < 4 else kous, fkt[i % 2][0:ROWS[i], :]).then_inc(s_kout[i % 2], 16)
            mod_rows(2)

            def exponents(i):
                n, t0 = ROWS[i], i * P
                for lv in levels(n):
                    H = LEVELS[lv]
                    bv = bb[:, :, t0:t0 + n].rearrange("p h (c w) -> p h c w", w=2 * H)
                    Xv = X[i % 2][:, lv, :, 0:n].rearrange("p h (c w) -> p h c w", w=2 * H)
                    anc = bv[:, :, :, H - 1:H].broadcast_to([P, HGH, n // (2 * H), H])
                    g.tensor_tensor(Xv[:, :, :, 0:H], anc, bv[:, :, :, 0:H], ALU.subtract)
                    g.tensor_tensor(Xv[:, :, :, H:], bv[:, :, :, H:], anc, ALU.subtract).then_inc(s_lv, 1)

            taken(pool, "hi0")
            exponents(0)
            exponents(1)
            pool.dma_start(S_sample, a["state_hgrn"].rearrange("l b h k v -> k (l b h) v")).then_inc(s_S0, 16)
            taken(pool, "lfT")
            pool.wait_ge(s_cf, 1)
            pool.dma_start(out["fox_logf_prompt"].rearrange("l b (i p) h -> p (l b i) h", p=P), lfo[:, 0:4, :]).then_inc(s_lout, 16)
            pool.dma_start(out["fox_logf_sample"][0, 0], lfo[0:NDEC, 4, :]).then_inc(s_lout, 16)
            pool.dma_start(ck_d, cf[0:8, 0:SEQ]).then_inc(s_ckw, 16)
            pool.dma_start(cks_d, cf[0:8, SEQ:SEQ + PAST + NDEC]).then_inc(s_ckw, 16)
            filled(pool, "Db0")
            exponents(2)
            pool.wait_ge(s_ckw, 32)
            pool.wait_ge(s_lout, 32)
            both(pool, s_kout)
            pool.dma_start(ckB.rearrange("p h t -> p (h t)"), bcast(ck_d.rearrange("h t -> (h t)"), P)).then_inc(s_ckr, 16)
            for i in range(3):
                taken(pool, f"fv{i}")
                pool.dma_start(vout[i * P:(i + 1) * P, :] if i < 4 else vous, v_fox[0:ROWS[i], i, :]).then_inc(s_vout, 16)
            filled(pool, "Db1")
            exponents(3)
            for i in range(3, NTILE):
                taken(pool, f"fv{i}")
                pool.dma_start(vout[i * P:(i + 1) * P, :] if i < 4 else vous, v_fox[0:ROWS[i], i, :]).then_inc(s_vout, 16)
            filled(pool, "fv4")
            pool.dma_start(ckS[0:NDEC].rearrange("p h t -> p (h t)"),
                           bcast(cks_d.rearrange("h t -> (h t)"), NDEC)).then_inc(s_ckr, 16)
            pool.dma_start(fgain, bcast(a["fox_out_gain"][0], P)).then_inc(s_ckr, 16)
            filled(pool, "Db2")
            exponents(4)

            def mask_future(q):
                blk = ckB[:, :, q * P:(q + 1) * P] if q < 4 else ckS[0:NDEC, :, PAST:]
                g.affine_select(blk, blk, [[0, FH], [-1, ROWS[q]]], ALU.is_ge, NEG, base=0,
                                channel_multiplier=1).then_inc(s_mask, 1)

            pool.wait_ge(s_ckr, 48)
            mask_future(QT[0])
            pool.wait_ge(s_le, sum(len(levels(n)) + 2 for n in ROWS))
            pool.wait_ge(s_mask, 1)
            plink(pool, g.memset(fq_odd[0:64], 0.0))
            for h in range(4):
                taken(pool, f"fq{h}1")
                g.tensor_copy(fq_odd[64:128, h, :], fqT[64:128, h, :]).then_inc(s_split, 1)
                pool.wait_ge(s_split, 2 * h + 1)
                g.memset(fqT[64:128, h, :], 0.0).then_inc(s_split, 1)
                pool.wait_ge(s_split, 2 * h + 2)
            sp_o = out["hgrn_state_prompt"].rearrange("l b h k v -> k (l b h) v")
            ss_o = out["hgrn_state_sample"].rearrange("l b h k v -> k (l b h) v")
            taken(pool, "S3")
            pool.dma_start(sp_o, S).then_inc(s_sout, 16)
            taken(pool, "S4")
            pool.dma_start(ss_o, S_sample).then_inc(s_sout, 16)
            pool.dma_start(kc, a["cache_fox_k"].rearrange("l b (j p) h d -> p (l b j) (h d)", p=P)).then_inc(s_cache, 16)
            pool.dma_start(vc, a["cache_fox_v"].rearrange("l b (j p) h d -> p (l b j) (h d)", p=P)).then_inc(s_cache, 16)
            taken(pool, "ho4")
            for gi in range(2):
                n = P if gi == 0 else NDEC
                pool.dma_start(mod1[0:n, gi, :], bcast(mod_d[gi, SLOT:2 * SLOT], n)).then_inc(s_mod1, 16)
                pool.dma_start(mod2[0:n, gi, :], bcast(mod_d[gi, 4 * D:5 * D], n)).then_inc(s_mod1, 16)
            pool.dma_start(ngain, bcast(a["norm_ffn_gain"][0], P)).then_inc(s_mod1, 16)
            for n, q in enumerate(QT[1:]):
                taken(pool, f"s{QT[n]}{FH - 1}")
                mask_future(q)
            taken(pool, "fo4")
            pool.dma_start(wrt, a["w_router"].rearrange("(k p) e -> p k e", p=P)).then_inc(s_brt, 16)
            pool.dma_start(brt, bcast(a["b_router"], P)).then_inc(s_brt, 16)
            g.memset(ones, 1.0)
            plink(pool, g.memset(tri, 1.0))
            g.affine_select(tri, tri, [[1, P]], ALU.is_gt, 0.0, base=0, channel_multiplier=-1)
            g.memset(msk6[:, NTILE, :], 0.0)
            plink(pool, g.memset(before4, 1.0))
            g.affine_select(before4, before4, [[1, EPG], [-1, EPG]], ALU.is_gt, 0.0, base=0, channel_multiplier=0)
            g.iota(iota_r, [[1, ET]], base=0, channel_multiplier=0, allow_small_or_imprecise_dtypes=True)
            g.iota(iota_t, [[1, MAXT + 2]], base=0, channel_multiplier=0, allow_small_or_imprecise_dtypes=True)
            for c in range(2):
                g.iota(entry[:, c * NTILE:(c + 1) * NTILE, 0], [[P, NTILE]], base=0, channel_multiplier=1,
                       allow_small_or_imprecise_dtypes=True)
                ins = g.iota(entry[:, c * NTILE:(c + 1) * NTILE, 1], [[P, NTILE]], base=(c - 8) * TOK, channel_multiplier=1,
                             allow_small_or_imprecise_dtypes=True)
            ins.then_inc(s_rc, 1)

            def residual(i):
                n = ROWS[i]
                pool.wait_ge(s_x[i], 32)
                for c in range(2):
                    taken(pool, f"y{i}{c if i < 4 else 0}")
                    xs = x[0:n, i, c * 512:(c + 1) * 512]
                    g.tensor_tensor(xs, xs, gt[c][0:n, :], ALU.add).then_inc(s_x2, 1)

            def shift_h2(i):
                n, gi = ROWS[i], i // 4
                pool.wait_ge(s_h2a, i + 1)
                g.tensor_tensor(h2[i][0:n, :], h2[i][0:n, :], mod1[0:n, gi, D:2 * D], ALU.add).then_inc(s_h2, 1)
                pool.wait_ge(s_h2, i + 1)
                pool.dma_start(h2_d[i * P:i * P + n, :], h2[i][0:n, :]).then_inc(s_h2w[i % 2], 16)

            residual(0)
            for i in range(1, 4):
                residual(i)
                shift_h2(i - 1)
            shift_h2(3)
            pool.wait_ge(s_h2s, 1)
            pool.dma_start(h2_d[SEQ:TOK, :], h2[4][0:NDEC, :]).then_inc(s_h2w[0], 16)
            pool.wait_ge(s_rd, 1)
            total = pool.value_load(base_i[0:1, NE:NE + 1], min_val=NE, max_val=MAXT)
            both(pool, s_h2w)
            pool.dma_start(ysb[0:1, :], h2_d[0:1, :]).then_inc(s_yst, 16)

            last_token, last_y = pool.to_reg(TOK - 1), pool.to_reg(2 * TOK - 1)

            gathers, scatters = pool.alloc_register("gathers"), pool.alloc_register("scatters")
            pool.reg_mov(gathers, 0)
            pool.reg_mov(scatters, 1)

            def gather():
                pool.reg_add(gathers, gathers, 1)
                pool.indirect_dma_start(xg[0:ET], None, h2_d, bass.IndirectOffsetOnAxis(ap=idx1[0:ET], axis=0),
                                        bounds_check=last_token, oob_is_err=False).then_inc(s_gath, 16)

            g.tensor_copy(idx1[0:ET], tseq[0:ET, 0, 0:1]).then_inc(s_idx, 1)
            pool.wait_ge(s_idx, 1)
            gather()
            pool.wait_ge(s_xp, 1)
            g.tensor_copy(idx1[0:ET], tseq[0:ET, 1, 0:1]).then_inc(s_idx, 1)
            pool.wait_ge(s_idx, 2)
            gather()
            with pool.Fori(0, total) as t:
                pool.wait_ge(s_xp, t + 2)
                g.tensor_copy(idx1[0:ET], tseq[0:ET, bass.ds(t + 2, 1), 0]).then_inc(s_idx, 1)
                pool.wait_ge(s_idx, t * 2 + 3)
                gather()
                pool.wait_ge(s_yst, t * 16 + 16)
                g.tensor_copy(idx2[0:ET], tseq[0:ET, bass.ds(t, 1), 1]).then_inc(s_idx, 1)
                pool.wait_ge(s_idx, t * 2 + 4)
                pool.wait_ge(s_yea, t + 2)
                pool.wait_ge(s_yeb, t + 2)
                pool.reg_add(scatters, scatters, 1)
                pool.indirect_dma_start(y_d, bass.IndirectOffsetOnAxis(ap=idx2[0:ET], axis=0), ysb[0:ET], None,
                                        bounds_check=last_y, oob_is_err=False).then_inc(s_yst, 16)
            pool.wait_ge(s_gath, pool.snap(gathers, min_val=1, max_val=MAXT + 2) * 16)
            pool.wait_ge(s_yst, pool.snap(scatters, min_val=1, max_val=MAXT + 1) * 16)
            for i in range(NTILE):
                n = ROWS[i]
                pool.wait_ge(s_gated, i + 1)
                g.tensor_tensor(x[0:n, i, :], x[0:n, i, :], ya[i][0:n, :], ALU.add).then_inc(s_comb, 1)

        @block.scalar
        def _(act):
            A = nc.scalar

            filled(act, "cT")
            act.wait_ge(s_cpad, 1)
            A.copy(gainT, bank[0][:, 16:24])
            read("act", "cT", A.activation(cpad[:, :, 0:2].rearrange("p k g -> p g k"),
                                           bank[0][:, 0:16].rearrange("p (g k) -> p g k", g=2), ACT.Silu))
            act.wait_ge(s_ident, 1)
            for i in range(NTILE):
                n = ROWS[i]
                act.wait_ge(s_x[i], 16)
                if i:
                    act.wait_ge(s_ss, i)
                A.activation(h1[0][0:n, :], x[0:n, i, :], ACT.Square, accum_out=st[0:n, i:i + 1]).then_inc(s_ss, 1)
            for i in range(NTILE):
                n = ROWS[i]
                for c in range(2):
                    filled(act, f"hT{i}{c}")
                    read("act", f"hT{i}{c}", A.copy(hT[:, 4 * c:4 * c + 4, i * P:i * P + n],
                                                    bank[2 + 2 * (i % 2) + c][:, :].rearrange("p (k t) -> p k t", k=4)[:, :, 0:n]))
            act.wait_ge(s_modT, 1)
            taken(act, "hT41")
            for k in range(4):
                for gi, ts in ((0, slice(0, SEQ)), (1, slice(SEQ, TOK))):
                    ins = A.activation(hT[:, k, ts], hT[:, k, ts], ACT.Identity, bias=modT[:, gi, k:k + 1],
                                       scale=modT[:, gi, KT + k:KT + k + 1])
                ins.then_inc(s_hma, 1)
            for h in range(HGH):
                for c in range(2):
                    filled(act, f"hq{h}{c}")
                    read("act", f"hq{h}{c}", A.activation(qs[:, h, c * HALF:(c + 1) * HALF],
                                                          bank[4 + 2 * (h % 2) + c][:, 0:HALF], ACT.Silu))
            for i in range(NTILE):
                filled(act, f"hg{i}")
                b = bank[2 + i % 2]
                if i < 4:
                    read("act", f"hg{i}", A.activation(G[:, i, :], b[:, :], ACT.Silu))
                else:
                    for j in range(4):
                        ins = A.activation(G[0:NDEC, 4, j * P:(j + 1) * P], b[32 * j:32 * j + 32, 0:P], ACT.Silu)
                    read("act", f"hg{i}", ins)
            for h in range(HGH):
                taken(act, f"hf{h}1")
                alink(act, A.activation(ex, fr, ACT.Abs))
                alink(act, A.activation(ex, ex, ACT.Exp, scale=-1.0))
                A.activation(ex, ex, ACT.Ln, bias=1.0).then_inc(s_ln, 1)
                act.wait_ge(s_kx, h + 1)
                A.activation(kk[:, h, :], fr, ACT.Exp).then_inc(s_kk, 1)
            for i in range(NTILE):
                n = ROWS[i]
                filled(act, f"fk{i}")
                if i >= 2:
                    act.wait_ge(s_kout[i % 2], 16 * (i // 2))
                    filled(act, f"fkT{i - 2}")
                b = bank[4 + i % 2]
                if i < 4:
                    read("act", f"fk{i}", A.copy(fkt[i % 2], b[:, :]))
                else:
                    for j in range(4):
                        ins = A.copy(fkt[0][0:NDEC, j * P:(j + 1) * P], b[32 * j:32 * j + 32, 0:P])
                    read("act", f"fk{i}", ins)
            seen = {"lv": 0}

            def exp_levels(i):
                n = ROWS[i]
                for lv in levels(n):
                    seen["lv"] += 1
                    act.wait_ge(s_lv, seen["lv"])
                    A.activation(X[i % 2][:, lv, :, 0:n], X[i % 2][:, lv, :, 0:n], ACT.Exp).then_inc(s_le, 1)

            def exp_ends(i):
                n = ROWS[i]
                act.wait_ge(s_ke, i + 1)
                A.activation(E[i % 2][:, :, 0:n], bb[:, :, i * P:i * P + n], ACT.Exp).then_inc(s_le, 1)
                A.activation(kE[i % 2][:, :, 0:n], kE[i % 2][:, :, 0:n], ACT.Exp).then_inc(s_le, 1)

            taken(act, "ff1")
            alink(act, A.activation(ssel[0:8, 0:TOK], cf[0:8, 0:TOK], ACT.Abs))
            alink(act, A.activation(ssel[0:8, 0:TOK], ssel[0:8, 0:TOK], ACT.Exp, scale=-1.0))
            A.activation(ssel[0:8, 0:TOK], ssel[0:8, 0:TOK], ACT.Ln, bias=1.0).then_inc(s_ln, 1)
            exp_levels(0)
            exp_ends(0)
            exp_levels(1)
            for item in schedule:
                if item[0] == "fq":
                    h, c = item[1:]
                    filled(act, f"fq{h}{c}")
                    read("act", f"fq{h}{c}", A.copy(fqT[:, h, c * HALF:(c + 1) * HALF],
                                                    bank[6 + (c + 1) % 2][:, 0:HALF]))
                if item[0] == "hgrn":
                    i = item[1]
                    if i >= 0:
                        n = ROWS[i]
                        if i + 2 < NTILE:
                            exp_levels(i + 2)
                        filled(act, f"kT{i}")
                        read("act", f"kT{i}", A.copy(kET[0:n], bank[3][0:n, :].rearrange("p (h k) -> p h k", h=HGH)))
                        filled(act, f"ho{i}")
                        if i:
                            act.wait_ge(s_sq, 4 * i)
                        for h in range(HGH):
                            A.activation(squares[0:n, h, :], bank[4][0:n, h * P:(h + 1) * P],
                                         ACT.Square, accum_out=st[0:n, 10 + 4 * i + h:11 + 4 * i + h]).then_inc(s_sq, 1)
                    if i + 2 < NTILE:
                        exp_ends(i + 2)
            def fox_squares(n_q):
                q = QT[n_q]
                n = ROWS[q]
                taken(act, f"fo{q}")
                if n_q:
                    act.wait_ge(s_fq, n_q)
                A.activation(osq[0:n, :], foxo[0:n, q, :], ACT.Square, accum_out=st[0:n, 80 + n_q:81 + n_q]).then_inc(s_fq, 1)

            m = 0
            for n_q, q in enumerate(QT):
                n = ROWS[q]
                nb = q + 1 if q < 4 else 3
                L = (q + 1) * P if q < 4 else PAST + NDEC
                if n_q == 3:
                    for c in range(2):
                        filled(act, f"kcT{c}")
                        read("act", f"kcT{c}", A.copy(kcT[:, :, c * P:(c + 1) * P], bank[6 + c][:, :].rearrange("p (a b) -> p a b", a=4)))
                for h in range(FH + 1):
                    if h < FH:
                        taken(act, f"s{q}{h}")
                        A.activation(pp[h % 2][0:n, 0:L], pp[h % 2][0:n, 0:L], ACT.Exp, bias=st[0:n, 50 + h:51 + h], scale=-1.0,
                                     accum_out=st[0:n, 60 + 8 * (n_q % 2) + h:61 + 8 * (n_q % 2) + h]).then_inc(s_pexp, 1)
                        m += 1
                    if h:
                        hh = h - 1
                        filled(act, f"t{q}{hh}")
                        src = bank[2 + h % 2][:, :].rearrange("p (a b) -> p a b", a=4)
                        if q < 4:
                            ins = A.copy(pT[h % 2][:, 0:nb, :], src[:, 0:nb, :])
                        else:
                            alink(act, A.copy(pT[h % 2][:, 0:2, 0:NDEC], src[:, 0:2, 0:NDEC]))
                            ins = A.copy(pT[h % 2][0:NDEC, 2, 0:NDEC], src[0:NDEC, 2, 0:NDEC])
                        read("act", f"t{q}{hh}", ins)
                    if n_q and h == 2:
                        fox_squares(n_q - 1)
            fox_squares(4)
            for i in range(NTILE):
                n = ROWS[i]
                filled(act, f"m{i}0")
                if i == 0:
                    filled(act, "fo4")
                read("act", f"m{i}0", A.copy(hT[:, 0:4, i * P:i * P + n],
                                             bank[(0, 2)[i % 2]][:, :].rearrange("p (k t) -> p k t", k=4)[:, :, 0:n]))
            def square_x2(i):
                n = ROWS[i]
                act.wait_ge(s_x2, 2 * i + 2)
                A.activation(h2[i][0:n, :], x[0:n, i, :], ACT.Square, accum_out=st[0:n, 90 + i:91 + i]).then_inc(s_x2q, 1)

            def h2_turned(i):
                n = ROWS[i]
                if i == 0:
                    act.wait_ge(s_sout, 32)
                for c in range(2):
                    filled(act, f"r{i}{c}")
                    read("act", f"r{i}{c}", A.copy(h2T[i % 2][:, 4 * c:4 * c + 4, 0:n],
                                                   bank[c][:, :].rearrange("p (k t) -> p k t", k=4)[:, :, 0:n]))

            square_x2(0)
            square_x2(1)
            for i in range(NTILE):
                h2_turned(i)
                if i + 2 < NTILE:
                    square_x2(i + 2)
            act.wait_ge(s_lx, 1)
            A.activation(prb, prb, ACT.Exp).then_inc(s_lex, 1)
            def xt_low():
                A.copy(XT[:, 0:4, :], bank[0][:, 0:4 * ET].rearrange("p (k t) -> p k t", k=4)).then_inc(s_xta, 1)

            act.wait_ge(s_rd, 1)
            act.sem_inc(s_yea, 1)
            total = act.value_load(base_i[0:1, NE:NE + 1], min_val=NE, max_val=MAXT)
            act.wait_ge(s_xp, 1)
            xt_low()

            def silu(t, c):
                act.wait_ge(s_gu, t * 2 + (c + 1))
                A.activation(hs[ET:2 * ET, c * 256:(c + 1) * 256], bank[2 + c][0:ET, 0:256], ACT.Silu).then_inc(s_sil, 1)

            def y_low(t):
                act.wait_ge(s_yd, t)
                act.wait_ge(s_yst, t * 16)
                A.copy(ysb[0:ET, 0:512], bank[6][0:ET, :]).then_inc(s_yea, 1)

            silu(0, 0)
            silu(0, 1)
            act.wait_ge(s_xp, 2)
            xt_low()
            with act.Fori(1, total) as t:
                silu(t, 0)
                y_low(t)
                silu(t, 1)
                act.wait_ge(s_xp, t + 2)
                xt_low()
            y_low(total)
            def gate_a(i):
                n = ROWS[i]
                act.wait_ge(s_ya[i], 32)
                A.activation(ya[i][0:n, :], ya[i][0:n, :], ACT.Copy, scale=gA[0:n, i:i + 1]).then_inc(s_ga, 1)

            gate_a(0)
            gate_a(1)
            gate_a(2)
            for i in range(NTILE):
                n = ROWS[i]
                if i + 3 < NTILE:
                    gate_a(i + 3)
                act.wait_ge(s_comb, i + 1)
                if i:
                    act.wait_ge(s_fsq, i)
                A.activation(jk[0:n, :], x[0:n, i, :], ACT.Square, accum_out=st[0:n, 100 + i:101 + i]).then_inc(s_fsq, 1)

        def route(dve, V):
            vlink(dve, V.memset(prb, 0.0))
            filled(dve, "lg")
            lb = bank[2][:, 0:NTILE * NE].rearrange("p (n e) -> p n e", e=NE)
            vlink(dve, V.tensor_copy(prb[:, 0:4, :], lb[:, 0:4, :]))
            read("dve", "lg", V.tensor_copy(prb[0:NDEC, 4, :], lb[0:NDEC, 4, :]))
            taken(dve, "lg")
            vlink(dve, V.tensor_reduce(s5[0], prb, AX.X, ALU.max))
            V.tensor_tensor(prb, prb, wide(s5[0]), ALU.subtract).then_inc(s_lx, 1)
            dve.wait_ge(s_lex, 1)
            vlink(dve, V.tensor_reduce(s5[1], prb, AX.X, ALU.add))
            vlink(dve, V.reciprocal(s5[1], s5[1]))
            vlink(dve, V.tensor_tensor(prb, prb, wide(s5[1]), ALU.mult))
            dve.wait_ge(s_brt, 32)
            vlink(dve, V.tensor_tensor(sel, prb, brt.unsqueeze(1).broadcast_to([P, NTILE, NE]), ALU.add))

            def ranks(values, rk):
                n = values.shape[1]
                greater, equal = (c[:, 0:n] for c in cmps)
                other, own = (values.unsqueeze(d).broadcast_to([P, n, EPG, EPG]) for d in (2, 3))
                V.tensor_tensor(greater, other, own, ALU.is_gt)
                vlink(dve, V.tensor_tensor(equal, other, own, ALU.is_equal))
                vlink(dve, V.tensor_tensor(equal, equal, before4.unsqueeze(1).broadcast_to([P, n, EPG, EPG]), ALU.mult))
                vlink(dve, V.tensor_tensor(greater, greater, equal, ALU.add))
                vlink(dve, V.tensor_reduce(rk, greater, AX.X, ALU.add))

            fours = "p n (g j) -> p (n g) j"
            sel4, rk4, msk4 = (v.rearrange(fours, j=EPG) for v in (sel, t80[0], msk))
            dve.wait_ge(s_rc, 1)
            ranks(sel4, rk4)
            vlink(dve, V.tensor_scalar(msk, t80[0], 2.0, None, ALU.is_lt))
            vlink(dve, V.tensor_tensor(t80[1], sel, msk, ALU.mult))
            vlink(dve, V.tensor_reduce(g20[1].rearrange("p n g -> p (n g)"), t80[1].rearrange(fours, j=EPG), AX.X, ALU.add))
            ranks(g20[1], g20[2])
            vlink(dve, V.tensor_scalar(g20[3], g20[2], 0.0, None, ALU.is_equal))
            vlink(dve, V.tensor_tensor(msk4, msk4, g20[3].rearrange("p n g -> p (n g)").unsqueeze(2).broadcast_to([P, NTILE * NG, EPG]), ALU.mult))
            vlink(dve, V.memset(msk[32:64, 4, :], 0.0))
            V.memset(msk[64:128, 4, :], 0.0).then_inc(s_mk, 1)
            dve.wait_ge(s_mk, 1)
            filled(dve, "pos")
            vlink(dve, V.tensor_scalar(cnt_i, bank[3][:, NTILE * NE:(NTILE + 1) * NE], float(ET - 1), None, ALU.add))
            vlink(dve, V.tensor_scalar(cnt_i, cnt_i, -ET, None, ALU.bitwise_and))
            vlink(dve, V.tensor_scalar(tf[1], cnt_i, 1.0 / ET, 1.0, ALU.mult, ALU.max))
            vlink(dve, V.tensor_tensor_scan(tf[2], tf[1], tf[1], 0.0, ALU.add, ALU.bypass))
            vlink(dve, V.tensor_tensor(tf[3], tf[2], tf[1], ALU.subtract))
            vlink(dve, V.tensor_scalar(tf[3], tf[3], float(ET), 1.0, ALU.mult, ALU.add))
            pb = bank[3][:, 0:NTILE * NE].rearrange("p (n e) -> p n e", e=NE)
            read("dve", "pos", V.tensor_tensor(t80[2], pb, tf[3].unsqueeze(1).broadcast_to([P, NTILE, NE]), ALU.add))
            taken(dve, "pos")
            vlink(dve, V.tensor_tensor(t80[2], t80[2], msk, ALU.mult))
            V.tensor_reduce(s5[4], t80[2], AX.X, ALU.max)
            vlink(dve, V.tensor_reduce(s5[5], t80[2], AX.X, ALU.add))
            V.tensor_scalar(dst[:, 0:NTILE], s5[4], -1.0, None, ALU.add)
            vlink(dve, V.scalar_tensor_tensor(dst[:, NTILE:], s5[5], -1.0, s5[4], ALU.add, ALU.subtract))
            vlink(dve, V.tensor_copy(dst_i, dst))
            vlink(dve, V.tensor_scalar(tile_i, dst_i, 6, None, ALU.arith_shift_right))
            vlink(dve, V.tensor_copy(dst_t, tile_i))
            vlink(dve, V.scalar_tensor_tensor(dst_r, dst_t, -float(ET), dst, ALU.mult, ALU.add))
            V.tensor_tensor(row_hot, iota_r.unsqueeze(1).broadcast_to([P, 2 * NTILE, ET]),
                            dst_r.unsqueeze(2).broadcast_to([P, 2 * NTILE, ET]), ALU.is_equal)
            vlink(dve, V.tensor_tensor(tile_hot, iota_t.unsqueeze(1).broadcast_to([P, 2 * NTILE, MAXT + 2]),
                                       dst_t.unsqueeze(2).broadcast_to([P, 2 * NTILE, MAXT + 2]), ALU.is_equal))
            V.tensor_tensor(tile_entry, tile_hot.unsqueeze(3).broadcast_to([P, 2 * NTILE, MAXT + 2, 2]),
                            entry.unsqueeze(2).broadcast_to([P, 2 * NTILE, MAXT + 2, 2]), ALU.mult).then_inc(s_oh, 1)
            V.tensor_copy(ntile_i[0:1, :], tf[1][0:1, :])
            V.memset(base_i[0:1, 0:1], 0)
            vlink(dve, V.tensor_copy(base_i[0:1, 1:NE + 1], tf[2][0:1, :]))
            filled(dve, "tab")
            tb = bank[5][0:ET, 0:2 * (MAXT + 2)].rearrange("p (t c) -> p t c", c=2)
            V.tensor_copy(tseq[0:ET, :, 0], tb[:, :, 0])
            read("dve", "tab", V.tensor_scalar(tseq[0:ET, :, 1], tb[:, :, 1], float(8 * TOK), None, ALU.add))
            taken(dve, "tab")
            dve.sem_inc(s_rd, 1)
            vlink(dve, V.tensor_tensor(gts, prb, msk, ALU.mult))
            vlink(dve, V.tensor_reduce(s5[3], gts, AX.X, ALU.add))
            V.memset(s5[3][32:64, 4:5], 1.0)
            vlink(dve, V.memset(s5[3][64:128, 4:5], 1.0))
            vlink(dve, V.reciprocal(s5[3], s5[3]))
            vlink(dve, V.tensor_tensor(gts, gts, wide(s5[3]), ALU.mult))
            vlink(dve, V.tensor_tensor(t80[3], t80[2], wide(s5[4]), ALU.is_equal))
            vlink(dve, V.tensor_tensor(t80[3], t80[3], gts, ALU.mult))
            V.tensor_reduce(gA, t80[3], AX.X, ALU.add)
            vlink(dve, V.tensor_tensor(t80[4], gts, t80[3], ALU.subtract))
            vlink(dve, V.tensor_reduce(gB, t80[4], AX.X, ALU.add))

        @block.vector
        def _(dve):
            V = nc.vector

            def rstd(y, ss, width):
                n, w = y.shape[0], y.shape[1]
                v, t = st[0:n, 110:110 + w], st[0:n, 118:118 + w]
                vlink(dve, V.tensor_scalar(v, ss, 1.0 / width, EPS, ALU.mult, ALU.add))
                yi = y.bitcast(I32)
                vlink(dve, V.tensor_scalar(yi, v.bitcast(I32), 1, None, ALU.logical_shift_right))
                vlink(dve, V.tensor_scalar(yi, yi, -1.0, float(0x5f3759df), ALU.mult, ALU.add))
                for _ in range(3):
                    if w == 1:
                        vlink(dve, V.scalar_tensor_tensor(t, y, v, y, ALU.mult, ALU.mult))
                    else:
                        vlink(dve, V.tensor_tensor(t, y, y, ALU.mult))
                        vlink(dve, V.tensor_tensor(t, t, v, ALU.mult))
                    vlink(dve, V.tensor_scalar(t, t, -0.5, 1.5, ALU.mult, ALU.add))
                    vlink(dve, V.tensor_tensor(y, y, t, ALU.mult))

            dve.wait_ge(s_iota, 1)
            vlink(dve, V.tensor_scalar(ip, ip, 31, None, ALU.bitwise_and))
            vlink(dve, V.tensor_tensor(ix, ip, it, ALU.bitwise_xor))
            vlink(dve, V.tensor_tensor(mgt, it, ip, ALU.is_gt))
            vlink(dve, V.tensor_copy(mxf, ix))
            for n, half in enumerate(LEVELS[2:]):
                vlink(dve, V.tensor_scalar(mtmp, mxf, float(half), None, ALU.is_ge))
                vlink(dve, V.scalar_tensor_tensor(mtmp, mxf, float(2 * half), mtmp, ALU.is_lt, ALU.mult))
                vlink(dve, V.tensor_tensor(lmask[:, n, :], mtmp, mgt, ALU.mult))
            vlink(dve, V.tensor_scalar(lmask[:, 5, :], mxf, 0.0, None, ALU.is_equal))
            dve.wait_ge(s_ss, NTILE)
            rstd(st[:, 5:10], st[:, 0:5], D)
            for i in range(NTILE):
                n = ROWS[i]
                if i >= 2:
                    filled(dve, f"hT{i - 2}1")
                V.tensor_scalar(h1[i % 2][0:n, :], x[0:n, i, :], st[0:n, 5 + i:6 + i], None, ALU.mult).then_inc(s_h1, 1)
            dve.wait_ge(s_badd, 32)
            filled(dve, "ada0")
            read("dve", "ada0", V.tensor_tensor(msb, bank[1][:, :], badd, ALU.add))
            filled(dve, "modT")
            mt = bank[0][:, :].rearrange("p (q j c) -> p j q c", q=4, j=4)
            for gi in range(2):
                for r in range(2):
                    ins = V.tensor_copy(modT[:, gi, r * KT:(r + 1) * KT].rearrange("p (j q) -> p j q", q=4), mt[:, 2 * r:2 * r + 2, :, gi])
            read("dve", "modT", ins)
            taken(dve, "modT")
            for gi in range(2):
                sc = modT[:, gi, KT:]
                ins = V.scalar_tensor_tensor(sc, sc, 1.0, gainT, ALU.add, ALU.mult)
            ins.then_inc(s_modT, 1)
            dve.wait_ge(s_modT, 1)
            taken(dve, "hT41")
            for k in range(4, KT):
                for gi, ts in ((0, slice(0, SEQ)), (1, slice(SEQ, TOK))):
                    ins = V.tensor_scalar(hT[:, k, ts], hT[:, k, ts], modT[:, gi, KT + k:KT + k + 1], modT[:, gi, k:k + 1],
                                          ALU.mult, ALU.add)
                ins.then_inc(s_hmd, 1)
            filled(dve, "hT41")
            for h in range(HGH):
                if h:
                    dve.wait_ge(s_kk, h)
                for c in range(2):
                    filled(dve, f"hf{h}{c}")
                    read("dve", f"hf{h}{c}", V.tensor_copy(fr[:, c * HALF:(c + 1) * HALF], bank[4 + 2 * (h % 2) + c][:, 0:HALF]))
                taken(dve, f"hf{h}1")
                dve.wait_ge(s_ln, h + 1)
                vlink(dve, V.scalar_tensor_tensor(lg, fr, 0.0, ex, ALU.min, ALU.subtract))
                V.tensor_tensor(fr, lg, fr, ALU.subtract).then_inc(s_kx, 1)
                for i in range(NTILE):
                    cs = slice(i * P, i * P + ROWS[i])
                    ins = V.tensor_tensor_scan(bb[:, h, cs], lg[:, cs], lg[:, cs], 0.0, ALU.add, ALU.bypass)
                vlink(dve, ins)
            dve.wait_ge(s_badd, 64)
            filled(dve, "modT")
            filled(dve, "ada1")
            read("dve", "ada1", V.tensor_tensor(msb, bank[1][:, :], badd, ALU.add))
            for i in range(NTILE):
                filled(dve, f"hi{i}")
                b = bank[2 + i % 2]
                if i < 4:
                    read("dve", f"hi{i}", V.tensor_copy(v_hg[:, i, :], b[:, :]))
                else:
                    for j in range(4):
                        ins = V.tensor_copy(v_hg[0:NDEC, 4, j * P:(j + 1) * P], b[32 * j:32 * j + 32, 0:P])
                    read("dve", f"hi{i}", ins)
            for i in range(NTILE):
                n = ROWS[i]
                filled(dve, f"fkT{i}")
                read("dve", f"fkT{i}", V.tensor_copy(fkT[:, :, i * P:i * P + n], bank[6][:, :].rearrange("p (a b) -> p a b", a=4)[:, :, 0:n]))
            dve.wait_ge(s_badd, 96)
            dve.wait_ge(s_modw, 32)
            filled(dve, "ada2")
            read("dve", "ada2", V.tensor_tensor(msb, bank[0][:, :], badd, ALU.add))
            known = {"le": 0}

            def end_exponents(i):
                n = ROWS[i]
                bt = bb[:, :, i * P:i * P + n]
                V.tensor_tensor(kE[i % 2][:, :, 0:n], bt[:, :, n - 1:n].broadcast_to([P, HGH, n]), bt, ALU.subtract).then_inc(s_ke, 1)

            def operands(i):
                n, t0 = ROWS[i], i * P
                for lv in levels(n):
                    H = LEVELS[lv]
                    known["le"] += 1
                    dve.wait_ge(s_le, known["le"])
                    Xv = X[i % 2][:, lv, :, 0:n].rearrange("p h (c w) -> p h c w", w=2 * H)
                    kv = kk[:, :, t0:t0 + n].rearrange("p h (c w) -> p h c w", w=2 * H)
                    qv = qs[:, :, t0:t0 + n].rearrange("p h (c w) -> p h c w", w=2 * H)
                    V.tensor_tensor(Xv[:, :, :, 0:H], Xv[:, :, :, 0:H], kv[:, :, :, 0:H], ALU.mult)
                    V.tensor_tensor(Xv[:, :, :, H:], Xv[:, :, :, H:], qv[:, :, :, H:], ALU.mult).then_inc(s_xm, 1)

            def end_operands(i):
                n, t0 = ROWS[i], i * P
                known["le"] += 2
                dve.wait_ge(s_le, known["le"])
                V.tensor_tensor(qE[i % 2][:, :, 0:n], E[i % 2][:, :, 0:n], qs[:, :, t0:t0 + n], ALU.mult)
                V.tensor_tensor(kE[i % 2][:, :, 0:n], kE[i % 2][:, :, 0:n], kk[:, :, t0:t0 + n], ALU.mult).then_inc(s_qk, 1)

            for c in range(2):
                filled(dve, f"ff{c}")
                read("dve", f"ff{c}", V.tensor_scalar(cf[0:8, c * HALF:(c + 1) * HALF], bank[c][0:8, 0:HALF], fbias[0:8, 0:1], None, ALU.add))
            filled(dve, "lpT")
            read("dve", "lpT", V.tensor_copy(lf[0:8, SEQ:SEQ + PAST], bank[2][0:8, 0:PAST]))
            dve.wait_ge(s_ln, HGH + 1)
            taken(dve, "ff1")
            vlink(dve, V.scalar_tensor_tensor(lf[0:8, 0:SEQ], cf[0:8, 0:SEQ], 0.0, ssel[0:8, 0:SEQ], ALU.min, ALU.subtract))
            V.scalar_tensor_tensor(lf[0:8, SEQ + PAST:], cf[0:8, SEQ:TOK], 0.0, ssel[0:8, SEQ:TOK], ALU.min, ALU.subtract).then_inc(s_lf, 1)
            dve.wait_ge(s_lf, 1)
            vlink(dve, V.tensor_tensor_scan(cf[0:8, 0:SEQ], lf[0:8, 0:SEQ], lf[0:8, 0:SEQ], 0.0, ALU.add, ALU.bypass))
            vlink(dve, V.tensor_tensor_scan(cf[0:8, SEQ:], lf[0:8, SEQ:SEQ + 288], lf[0:8, SEQ:SEQ + 288], 0.0, ALU.add, ALU.bypass))
            V.tensor_scalar(cf[0:8, :], cf[0:8, :], -float(FD) ** 0.5, None, ALU.mult).then_inc(s_cf, 1)
            dve.wait_ge(s_qs, HGH)
            end_exponents(0)
            operands(0)
            end_operands(0)
            for n in range(2):
                V.memset(attT[n], 0.0).then_inc(s_zero, 1)
            dve.wait_ge(s_zero, 2)
            dve.wait_ge(s_G, NTILE)

            def attention(i):
                n = ROWS[i]
                at = attT[i % 2]
                if i < 4:
                    filled(dve, f"L{i}")
                    Lb = bank[0][:, 0:384].rearrange("p (h c) -> p h c", h=HGH)
                    V.tensor_copy(at[0:64, :, 64:128], Lb[0:64, :, 0:64])
                    V.tensor_copy(at[0:32, :, 32:64], Lb[0:32, :, 64:96])
                    read("dve", f"L{i}", V.tensor_copy(at[64:96, :, 96:128], Lb[64:96, :, 64:96]))
                for c, nm in enumerate(("Da", "Db")):
                    filled(dve, f"{nm}{i}")
                    src = bank[1 + c][0:n, 0:384].rearrange("p (h l t) -> p h l t", h=2, l=6)
                    for hh in range(2):
                        ins = V.tensor_tensor(att6[0:n, hh], src[:, hh], lmask[0:n], ALU.mult)
                    read("dve", f"{nm}{i}", ins)
                    taken(dve, f"{nm}{i}")
                    vlink(dve, V.tensor_reduce(attd[0:n, 2 * c:2 * c + 2, :], att6[0:n].rearrange("p h l t -> p h t l"), AX.X, ALU.add))
                for j in range((n + 31) // 32):
                    ins = V.tensor_copy(at[32 * j:32 * j + 32, :, 32 * j:32 * j + 32], attd[32 * j:32 * j + 32, :, :])
                ins.then_inc(s_att, 1)

            def output_and_state(i):
                n = ROWS[i]
                dve.wait_ge(s_sq, 4 * i + 4)
                rstd(st[0:n, 30:34], st[0:n, 10 + 4 * i:14 + 4 * i], P)
                for h in range(HGH):
                    ins = V.scalar_tensor_tensor(G[0:n, i, h * P:(h + 1) * P], bank[4][0:n, h * P:(h + 1) * P], st[0:n, 30 + h:31 + h],
                                                 G[0:n, i, h * P:(h + 1) * P], ALU.mult, ALU.mult)
                read("dve", f"ho{i}", ins)
                filled(dve, f"S{i}")
                St = S if i < 4 else S_sample
                for h in range(HGH):
                    if i == 0:
                        ins = V.tensor_copy(St[:, h, :], bank[5][:, h * P:(h + 1) * P])
                    else:
                        ins = V.scalar_tensor_tensor(St[:, h, :], St[:, h, :], E[i % 2][:, h, n - 1:n], bank[5][:, h * P:(h + 1) * P], ALU.mult, ALU.add)
                read("dve", f"S{i}", ins)
                taken(dve, f"S{i}")

            for item in schedule:
                if item[0] == "lfT":
                    filled(dve, "lfT")
                    vlink(dve, V.tensor_copy(lfo[:, 0:4, :], bank[3][:, 0:32].rearrange("p (a b) -> p a b", a=4)))
                    read("dve", "lfT", V.tensor_copy(lfo[0:NDEC, 4, :], bank[3][0:NDEC, 32:40]))
                if item[0] == "fv":
                    i = item[1]
                    filled(dve, f"fv{i}")
                    b = bank[6 + i % 2]
                    if i < 4:
                        read("dve", f"fv{i}", V.tensor_copy(v_fox[:, i, :], b[:, :]))
                    else:
                        for j in range(4):
                            ins = V.tensor_copy(v_fox[0:NDEC, 4, j * P:(j + 1) * P], b[32 * j:32 * j + 32, 0:P])
                        read("dve", f"fv{i}", ins)
                if item[0] == "hgrn":
                    i = item[1]
                    if i + 1 < NTILE:
                        attention(i + 1)
                    if 0 < i + 2 < NTILE:
                        operands(i + 2)
                    if i >= 0:
                        output_and_state(i)
                    if 0 < i + 2 < NTILE:
                        end_exponents(i + 2)
                        end_operands(i + 2)
            dve.wait_ge(s_ckr, 48)

            def fox_normalise(n_q):
                q = QT[n_q]
                n = ROWS[q]
                filled(dve, f"fo{q}")
                dve.wait_ge(s_pexp, (n_q + 1) * FH)
                ls = 60 + 8 * (n_q % 2)
                vlink(dve, V.reciprocal(st[0:n, ls:ls + 8], st[0:n, ls:ls + 8]))
                read("dve", f"fo{q}", V.tensor_tensor(
                    foxo[0:n, q, :].rearrange("p (h d) -> p h d", h=FH), bank[4 + n_q % 2][0:n, :].rearrange("p (h d) -> p h d", h=FH),
                    st[0:n, ls:ls + 8].unsqueeze(2).broadcast_to([n, FH, FD]), ALU.mult))

            for n_q, q in enumerate(QT):
                n = ROWS[q]
                L = (q + 1) * P if q < 4 else PAST + NDEC
                cb = (ckB if q < 4 else ckS)
                dve.wait_ge(s_mask, 1 + n_q)
                for h in range(FH):
                    m = n_q * FH + h
                    filled(dve, f"s{q}{h}")
                    if m >= 2:
                        pq, ph = (QT[(m - 2) // FH], (m - 2) % FH)
                        filled(dve, f"t{pq}{ph}")
                    read("dve", f"s{q}{h}", V.tensor_tensor_reduce(pp[h % 2][0:n, 0:L], bank[h % 2][0:n, 0:L], cb[0:n, h, 0:L],
                                                                   -float(FD) ** -0.5, 3e38, ALU.add, ALU.min, st[0:n, 50 + h:51 + h]))
                    if n_q and h == 1:
                        fox_normalise(n_q - 1)
            fox_normalise(4)
            dve.wait_ge(s_fq, NTILE)
            rstd(st[:, 85:90], st[:, 80:85], HW)
            for i in range(NTILE):
                n, c = ROWS[i], 85 + QT.index(i)
                V.scalar_tensor_tensor(foxo[0:n, i, :], foxo[0:n, i, :], st[0:n, c:c + 1], fgain[0:n, :], ALU.mult, ALU.mult).then_inc(s_fo, 1)
            for i in range(NTILE):
                n = ROWS[i]
                filled(dve, f"m{i}1")
                read("dve", f"m{i}1", V.tensor_copy(hT[:, 4:8, i * P:i * P + n],
                                                    bank[(1, 3)[i % 2]][:, :].rearrange("p (k t) -> p k t", k=4)[:, :, 0:n]))
            dve.wait_ge(s_mod1, 80)
            for gi in range(2):
                n = P if gi == 0 else NDEC
                sc = mod2[0:n, gi, :]
                ins = V.scalar_tensor_tensor(sc, sc, 1.0, ngain[0:n, :], ALU.add, ALU.mult)
            vlink(dve, ins)

            def scale_h2(i):
                n, gi = ROWS[i], i // 4
                dve.wait_ge(s_x2q, i + 1)
                rstd(st[0:n, 95 + i:96 + i], st[0:n, 90 + i:91 + i], D)
                V.scalar_tensor_tensor(h2[i][0:n, :], x[0:n, i, :], st[0:n, 95 + i:96 + i], mod2[0:n, gi, :],
                                       ALU.mult, ALU.mult).then_inc(s_h2a, 1)

            for i in range(4):
                for c in range(2):
                    filled(dve, f"y{i}{c}")
                    if i:
                        dve.wait_ge(s_x2, 2 * (i - 1) + c + 1)
                    read("dve", f"y{i}{c}", V.tensor_tensor(gt[c], bank[4 + (2 * i + c) % 4][:, :],
                                                            mod1[:, 0, c * 512:(c + 1) * 512], ALU.mult))
                if i:
                    scale_h2(i - 1)
            filled(dve, "y40")
            dve.wait_ge(s_x2, 8)
            for j in range(4):
                ins = V.tensor_tensor(gt[j // 2][0:32, (j % 2) * 256:(j % 2) * 256 + 256], bank[4][32 * j:32 * j + 32, 0:256],
                                      mod1[0:32, 1, j * 256:(j + 1) * 256], ALU.mult)
            read("dve", "y40", ins)
            dve.wait_ge(s_x[4], 32)
            taken(dve, "y40")
            for c in range(2):
                xs = x[0:NDEC, 4, c * 512:(c + 1) * 512]
                V.tensor_tensor(xs, xs, gt[c][0:NDEC, :], ALU.add).then_inc(s_x2, 1)
            scale_h2(3)
            scale_h2(4)
            dve.wait_ge(s_h2a, NTILE)
            V.tensor_tensor(h2[4][0:NDEC, :], h2[4][0:NDEC, :], mod1[0:NDEC, 1, D:2 * D], ALU.add).then_inc(s_h2s, 1)
            route(dve, V)
            def xt_high():
                V.tensor_copy(XT[:, 4:8, :], bank[1][:, 0:4 * ET].rearrange("p (k t) -> p k t", k=4)).then_inc(s_xtb, 1)

            def hidden(t, c):
                dve.wait_ge(s_sil, t * 2 + (c + 1))
                fs = slice(c * 256, (c + 1) * 256)
                V.tensor_tensor(he[0:ET, fs], hs[ET:2 * ET, fs], bank[2 + c][ET:2 * ET, 0:256], ALU.mult).then_inc(s_he, 1)

            def hidden_t(t, c):
                dve.wait_ge(s_ht, t * 2 + (c + 1))
                V.tensor_copy(heT[:, 2 * c:2 * c + 2, :], bank[4 + c][:, 0:2 * ET].rearrange("p (f t) -> p f t", f=2)).then_inc(s_hc, 1)

            dve.wait_ge(s_rd, 1)
            dve.sem_inc(s_yeb, 1)
            total = dve.value_load(base_i[0:1, NE:NE + 1], min_val=NE, max_val=MAXT)
            dve.wait_ge(s_xp, 1)
            xt_high()

            def y_high(t):
                dve.wait_ge(s_yd, t)
                dve.wait_ge(s_yst, t * 16)
                V.tensor_copy(ysb[0:ET, 512:1024], bank[6][ET:2 * ET, :]).then_inc(s_yeb, 1)

            hidden(0, 0)
            hidden(0, 1)
            hidden_t(0, 0)
            dve.wait_ge(s_xp, 2)
            xt_high()
            hidden_t(0, 1)
            with dve.Fori(1, total) as t:
                hidden(t, 0)
                y_high(t)
                hidden(t, 1)
                hidden_t(t, 0)
                dve.wait_ge(s_xp, t + 2)
                xt_high()
                hidden_t(t, 1)
            y_high(total)
            dve.wait_ge(s_ph3, 48)

            def combine(i):
                n, gi = ROWS[i], i // 4
                A_, B_ = ya[i][0:n, :], yb[i][0:n, :]
                dve.wait_ge(s_ga, i + 1)
                vlink(dve, V.scalar_tensor_tensor(A_, B_, gB[0:n, i:i + 1], A_, ALU.mult, ALU.add))
                V.tensor_tensor(A_, A_, gateF[0:n, gi, :], ALU.mult).then_inc(s_gated, 1)

            def roots(first, stop):
                dve.wait_ge(s_fsq, stop)
                rstd(st[:, 105 + first:105 + stop], st[:, 100 + first:100 + stop], D)

            def normalise(i):
                n = ROWS[i]
                V.scalar_tensor_tensor(ya[i][0:n, :], x[0:n, i, :], st[0:n, 105 + i:106 + i], fing[0:n, :],
                                       ALU.mult, ALU.mult).then_inc(s_fin, 1)

            for i in range(NTILE):
                combine(i)
            roots(0, 3)
            normalise(0)
            normalise(1)
            normalise(2)
            roots(3, NTILE)
            normalise(3)
            normalise(4)

        def fox_values(pe, T, n_q, q, h, end=None):
            n = ROWS[q]
            taken(pe, f"t{q}{h}")
            widths = [P] * (q + 1) if q < 4 else [P, P, NDEC]
            hc = slice(h * FD, (h + 1) * FD)
            for j, w in enumerate(widths):
                if q < 4:
                    v = v_fox[:, j, hc]
                else:
                    v = vc[:, j, hc] if j < 2 else v_fox[0:NDEC, 4, hc]
                ins = T.matmul(bank[4 + n_q % 2][0:n, hc], pT[(h + 1) % 2][0:w, j, 0:n], v, start=(j == 0), stop=(j == len(widths) - 1))
            if end:
                end(f"fo{q}", ins)

        @block.tensor
        def _(pe):
            T = nc.tensor
            issued = []

            def begin(name):
                if before[name]:
                    taken(pe, before[name])

            def end(name, ins):
                assert where[name] == len(issued), (name, len(issued), plan[len(issued)])
                issued.append(name)
                ins.then_inc(pe_done, 1)

            def chunk(b, k4=4):
                return b[:, :].rearrange("p (k t) -> p k t", k=k4)

            pe.wait_ge(s_ident, 1)
            pe.wait_ge(s_c, 48)
            end("cT", T.transpose(bank[0][:, 0:24], crow[0:24, :], ident[0:24, 0:24]))

            def ada(r, b, first, stop):
                if first == 0:
                    begin(f"ada{r}")
                for k in range(first, stop):
                    loaded(pe, f"ada{r}_{k}")
                    w = wslot(f"ada{r}_{k}", SLOT)[:, 0, :]
                    for j in range(4):
                        ins = T.matmul(bank[b][32 * j:32 * j + 32, :], cpad[:, k, :], w[:, j * 512:(j + 1) * 512],
                                       start=(k == 0), stop=(k == KT - 1))
                if stop == KT:
                    end(f"ada{r}", ins)

            def turned(name, b, src, n, blocks):
                begin(name)
                for j in range(blocks):
                    ins = T.transpose(chunk(bank[b])[:, j, 0:n], src[0:n, j * P:(j + 1) * P], ident[0:n, 0:n])
                end(name, ins)

            def feature_block(name, h, c, b):
                w = wslot(name, HW)
                begin(f"{name}{h}{c}")
                for n in range(KT):
                    k = n // 2 + (KT // 2) * (n % 2)
                    if name == "hq" and h == 0 and c == 0:
                        pe.wait_ge((s_hma, s_hmd)[n % 2], n // 2 + 1)
                    ins = T.matmul(bank[b][:, 0:HALF], w[:, k, h * P:(h + 1) * P], hT[:, k, c * HALF:(c + 1) * HALF],
                                   start=(n == 0), stop=(n == KT - 1))
                end(f"{name}{h}{c}", ins)

            def feature_major(name):
                loaded(pe, name)
                for h in range(4):
                    for c in range(2):
                        feature_block(name, h, c, 4 + 2 * (h % 2) + c)

            def token_major(name, i, b):
                w = wslot(name, HW)
                begin(f"{name}{i}")
                for k in range(KT):
                    if i < 4:
                        ins = T.matmul(bank[b][:, :], hT[:, k, i * P:(i + 1) * P], w[:, k, :], start=(k == 0), stop=(k == KT - 1))
                    else:
                        for j in range(4):
                            ins = T.matmul(bank[b][32 * j:32 * j + 32, 0:P], hT[:, k, SEQ:], w[:, k, j * P:(j + 1) * P],
                                           start=(k == 0), stop=(k == KT - 1))
                end(f"{name}{i}", ins)

            taken(pe, "cT")
            ada(0, 1, 0, 2)
            for i in range(NTILE):
                pe.wait_ge(s_h1, i + 1)
                for c in range(2):
                    turned(f"hT{i}{c}", 2 + 2 * (i % 2) + c, h1[i % 2][:, c * 512:(c + 1) * 512], ROWS[i], 4)
            ada(0, 1, 2, KT)
            taken(pe, "ada0")
            turned("modT", 0, msb, P, 4)
            feature_major("hq")
            loaded(pe, "hg")
            for i in range(NTILE):
                token_major("hg", i, 2 + i % 2)
            ada(1, 1, 0, 4)
            feature_major("hf")
            ada(1, 1, 4, KT)
            loaded(pe, "hi")
            for i in range(NTILE):
                token_major("hi", i, 2 + i % 2)
            ada(2, 0, 0, 4)
            loaded(pe, "fk")
            for i in range(NTILE):
                token_major("fk", i, 4 + i % 2)
                if i:
                    taken(pe, f"fk{i - 1}")
                    turned(f"fkT{i - 1}", 6, fkt[(i - 1) % 2], ROWS[i - 1], 4)
            taken(pe, "fk4")
            turned("fkT4", 6, fkt[0], NDEC, 4)
            ada(2, 0, 4, KT)
            pe.wait_ge(s_small, 64)
            for c in range(2):
                begin(f"ff{c}")
                for k in range(KT):
                    ins = T.matmul(bank[c][0:FH, 0:HALF], wff[:, k, :], hT[:, k, c * HALF:(c + 1) * HALF],
                                   start=(k == 0), stop=(k == KT - 1))
                end(f"ff{c}", ins)
            begin("lpT")
            for j in range(2):
                ins = T.transpose(bank[2][0:FH, j * P:(j + 1) * P], lpast[:, j, :], ident[:, :])
            end("lpT", ins)
            def attention(i):
                n, t0 = ROWS[i], i * P
                Xi = X[i % 2]
                if i < 4:
                    begin(f"L{i}")
                    Lb = bank[0][:, 0:384].rearrange("p (h c) -> p h c", h=HGH)
                    pe.wait_ge(s_xm, level_operands(i, 2))
                    for h in range(HGH):
                        T.matmul(Lb[0:64, h, 0:64], Xi[:, 0, h, 0:64], Xi[:, 0, h, 64:128], start=True, stop=True)
                        for j in range(2):
                            ins = T.matmul(Lb[64 * j:64 * j + 32, h, 64:96], Xi[:, 1, h, 64 * j:64 * j + 32],
                                           Xi[:, 1, h, 64 * j + 32:64 * j + 64], start=True, stop=True)
                    end(f"L{i}", ins)
                for c, nm in enumerate(("Da", "Db")):
                    begin(f"{nm}{i}")
                    pe.wait_ge(s_xm, level_operands(i + 1, 0))
                    src = bank[1 + c][:, 0:384].rearrange("p (h l t) -> p h l t", h=2, l=6)
                    for hh in range(2):
                        h = 2 * c + hh
                        for lv in range(2, 8):
                            for j in range(n // 32):
                                b = slice(32 * j, 32 * j + 32)
                                tb = slice(t0 + 32 * j, t0 + 32 * j + 32)
                                left, right = (Xi[:, lv, h, b], Xi[:, lv, h, b]) if lv < 7 else (kk[:, h, tb], qs[:, h, tb])
                                ins = T.matmul(src[32 * j:32 * j + 32, hh, lv - 2, :], left, right, start=True, stop=True)
                    end(f"{nm}{i}", ins)

            def output_and_state(i):
                n = ROWS[i]
                begin(f"kT{i}")
                pe.wait_ge(s_qk, i + 1)
                for h in range(HGH):
                    ins = T.transpose(chunk(bank[3])[0:n, h, :], kE[i % 2][:, h, 0:n], ident[:, :])
                end(f"kT{i}", ins)
                begin(f"ho{i}")
                pe.wait_ge(s_att, i + 1)
                if 0 < i < 4:
                    taken(pe, f"S{i - 1}")
                if i == 4:
                    pe.wait_ge(s_S0, 16)
                for h in range(HGH):
                    o = bank[4][0:n, h * P:(h + 1) * P]
                    if i:
                        T.matmul(o, qE[i % 2][:, h, 0:n], (S if i < 4 else S_sample)[:, h, :], start=True, stop=False)
                    ins = T.matmul(o, attT[i % 2][0:n, h, 0:n], v_hg[0:n, i, h * P:(h + 1) * P], start=(i == 0), stop=True)
                end(f"ho{i}", ins)
                begin(f"S{i}")
                taken(pe, f"kT{i}")
                for h in range(HGH):
                    ins = T.matmul(bank[5][:, h * P:(h + 1) * P], kET[0:n, h, :], v_hg[0:n, i, h * P:(h + 1) * P], start=True, stop=True)
                end(f"S{i}", ins)

            loaded(pe, "fv")
            for item in schedule:
                if item[0] == "lfT":
                    begin("lfT")
                    pe.wait_ge(s_lf, 1)
                    for i in range(NTILE):
                        n = ROWS[i]
                        c0 = i * P if i < 4 else SEQ + PAST
                        ins = T.transpose(bank[3][0:n, i * FH:(i + 1) * FH], lf[0:8, c0:c0 + n], ident[0:8, 0:8])
                    end("lfT", ins)
                elif item[0] == "fv":
                    token_major("fv", item[1], 6 + item[1] % 2)
                elif item[0] == "fq":
                    if item[1:] == (0, 0):
                        loaded(pe, "fq")
                    feature_block("fq", *item[1:], 6 + (item[2] + 1) % 2)
                else:
                    i = item[1]
                    if i + 1 < NTILE:
                        attention(i + 1)
                    if i >= 0:
                        output_and_state(i)

            m = 0
            for n_q, q in enumerate(QT):
                n = ROWS[q]
                qc = slice(q * P, q * P + n)
                if n_q == 3:
                    pe.wait_ge(s_cache, 32)
                    for c in range(2):
                        turned(f"kcT{c}", 6 + c, kc[:, c, :], P, 4)
                for h in range(FH + 1):
                    if h < FH:
                        begin(f"s{q}{h}")
                        if n_q == 0:
                            pe.wait_ge(s_split, 2 * (h // 2) + 2)
                        lhs = (fq_odd if h % 2 else fqT)[:, h // 2, qc]
                        if q < 4:
                            ins = T.matmul(bank[h % 2][0:n, 0:(q + 1) * P], lhs, fkT[:, h // 2, 0:(q + 1) * P], start=True, stop=True)
                        else:
                            taken(pe, "kcT1")
                            T.matmul(bank[h % 2][0:n, 0:PAST], lhs, kcT[:, h // 2, :], start=True, stop=True)
                            ins = T.matmul(bank[h % 2][0:n, PAST:PAST + n], lhs, fkT[:, h // 2, qc], start=True, stop=True)
                        end(f"s{q}{h}", ins)
                    if h == 1 and n_q:
                        fox_values(pe, T, n_q - 1, QT[n_q - 1], FH - 1, end)
                    if h:
                        hh = h - 1
                        begin(f"t{q}{hh}")
                        m += 1
                        pe.wait_ge(s_pexp, m)
                        tb = chunk(bank[2 + h % 2])
                        widths = [P] * (q + 1) if q < 4 else [P, P, NDEC]
                        for j, w in enumerate(widths):
                            ins = T.transpose(tb[0:w, j, 0:n], pp[hh % 2][0:n, j * P:j * P + w], ident[0:n, 0:n])
                        end(f"t{q}{hh}", ins)
                        if hh == 1:
                            begin(f"fo{q}")
                        if hh:
                            fox_values(pe, T, n_q, q, hh - 1)
            fox_values(pe, T, 4, QT[4], FH - 1, end)

            for i in range(NTILE):
                n = ROWS[i]
                turned(f"m{i}0", (0, 2)[i % 2], G[:, i, :], n, 4)
            for i in range(NTILE):
                n = ROWS[i]
                pe.wait_ge(s_fo, i + 1)
                turned(f"m{i}1", (1, 3)[i % 2], foxo[:, i, :], n, 4)
            taken(pe, "m40")
            taken(pe, "m41")
            for k in range(4):
                loaded(pe, f"wo{k}")

            def turn_h2(i):
                pe.wait_ge(*((s_h2, i + 1) if i < 4 else (s_h2s, 1)))
                for c in range(2):
                    turned(f"r{i}{c}", c, h2[i][:, c * 512:(c + 1) * 512], ROWS[i], 4)

            def router(i):
                n = ROWS[i]
                if i == 0:
                    begin("lg")
                    pe.wait_ge(s_brt, 32)
                taken(pe, f"r{i}0")
                taken(pe, f"r{i}1")
                for k in range(KT):
                    ins = T.matmul(bank[2][0:n, i * NE:(i + 1) * NE], h2T[i % 2][:, k, 0:n], wrt[:, k, :], start=(k == 0), stop=(k == KT - 1))
                if i == NTILE - 1:
                    end("lg", ins)

            for i in range(4):
                for c in range(2):
                    b = bank[4 + (2 * i + c) % 4]
                    begin(f"y{i}{c}")
                    for k in range(KT):
                        ins = T.matmul(b[:, :], hT[:, k, i * P:(i + 1) * P], wslot(f"wo{k // 2}", D)[:, k % 2, c * 512:(c + 1) * 512],
                                       start=(k == 0), stop=(k == KT - 1))
                    end(f"y{i}{c}", ins)
                if i == 3:
                    router(0)
                if i >= 2:
                    turn_h2(i - 2)
            begin("y40")
            for k in range(KT):
                for j in range(4):
                    ins = T.matmul(bank[4][32 * j:32 * j + 32, 0:256], hT[:, k, SEQ:], wslot(f"wo{k // 2}", D)[:, k % 2, j * 256:(j + 1) * 256],
                                   start=(k == 0), stop=(k == KT - 1))
            end("y40", ins)
            router(1)
            for i in range(2, NTILE):
                turn_h2(i)
                router(i)
            begin("pos")
            pe.wait_ge(s_mk, 1)
            pe.wait_ge(s_rc, 1)
            flat = msk6.rearrange("p n e -> p (n e)")
            ends = (NTILE + 1) * NE
            T.matmul(bank[3][:, 0:ends], tri, flat, start=True, stop=False)
            for j in range(1, NTILE + 1):
                ins = T.matmul(bank[3][:, j * NE:ends], ones, flat[:, 0:ends - j * NE], start=False, stop=(j == NTILE))
            end("pos", ins)

            begin("tab")
            pe.wait_ge(s_oh, 1)
            for j in range(2 * NTILE):
                ins = T.matmul(bank[5][0:ET, 0:2 * (MAXT + 2)], row_hot[:, j, :], tile_entry[:, j, :, :].rearrange("p t c -> p (t c)"),
                               start=(j == 0), stop=(j == 2 * NTILE - 1))
            end("tab", ins)

            def transpose_rows():
                for k in range(KT):
                    ins = T.transpose(bank[k // 4][:, (k % 4) * ET:(k % 4 + 1) * ET], xg[0:ET, k * P:(k + 1) * P], ident[0:ET, 0:ET])
                ins.then_inc(s_xp, 1)

            def transpose_hidden(t, c):
                pe.wait_ge(s_he, t * 2 + (c + 1))
                pe.sem_inc(s_begun, 1)
                for f in range(2):
                    ins = T.transpose(bank[4 + c][:, f * ET:(f + 1) * ET], he[0:ET, (2 * c + f) * P:(2 * c + f + 1) * P],
                                      ident[0:ET, 0:ET])
                ins.then_inc(s_ht, 1)

            taken(pe, "tab")
            pe.wait_ge(s_rd, 1)
            pe.wait_ge(s_gath, 16)
            transpose_rows()

            def expert(par, e, loads_done):
                Wg, Wu, Wd = wexp(par)
                for c in range(2):
                    pe.wait_ge(s_we[par][c], loads_done)
                nt = pe.value_load(ntile_i[0:1, bass.ds(e, 1)], min_val=1, max_val=CAPT)
                base = pe.value_load(base_i[0:1, bass.ds(e, 1)], min_val=0, max_val=MAXT)
                with pe.Fori(0, nt) as i:
                    t = base + i
                    pe.wait_ge(s_xta, t + 1)
                    pe.wait_ge(s_xtb, t + 1)
                    for c in range(2):
                        for k in range(KT):
                            for half, w in enumerate((Wg, Wu)):
                                ins = T.matmul(bank[2 + c][ET * half:ET * half + ET, 0:256], XT[:, k, :],
                                               w[:, k, c * 256:(c + 1) * 256], start=(k == 0), stop=(k == KT - 1))
                        ins.then_inc(s_gu, 1)
                    transpose_hidden(t, 0)
                    pe.wait_ge(s_gath, t * 16 + 32)
                    pe.sem_inc(s_begun, 1)
                    transpose_rows()
                    transpose_hidden(t, 1)
                    pe.wait_ge(s_yea, t + 1)
                    pe.wait_ge(s_yeb, t + 1)
                    for f in range(FT):
                        if f % 2 == 0:
                            pe.wait_ge(s_hc, t * 2 + (f // 2 + 1))
                        for half in range(2):
                            ins = T.matmul(bank[6][ET * half:ET * half + ET, :], heT[:, f, :],
                                           Wd[:, f, half * 512:(half + 1) * 512], start=(f == 0), stop=(f == FT - 1))
                    ins.then_inc(s_yd, 1)

            with pe.Fori(0, NE // 3) as three:
                for par in range(3):
                    expert(par, three * 3 + par, three * 48 + 48)
            expert(0, NE - 1, (NE // 3 + 1) * 48)


_INS = ['x_prompt', 'x_sample', 'cache_fox_k', 'cache_fox_v', 'cache_fox_logf', 'state_hgrn', 'c_prompt', 'c_sample',
        'norm_mix_gain', 'norm_ffn_gain', 'w_ada', 'b_ada', 'w_in', 'hg_lower_bounds', 'hg_norm_gain', 'fox_f_bias',
        'fox_out_gain', 'w_out', 'w_router', 'b_router', 'w_exp_gate', 'w_exp_up', 'w_exp_down', 'final_norm_gain']
_OUTS = [('y_prompt', (1, 512, 1024)), ('y_sample', (1, 32, 1024)), ('hgrn_state_prompt', (1, 1, 4, 128, 128)),
         ('fox_k_prompt', (1, 1, 512, 8, 64)), ('fox_v_prompt', (1, 1, 512, 8, 64)), ('fox_logf_prompt', (1, 1, 512, 8)),
         ('hgrn_state_sample', (1, 1, 4, 128, 128)), ('fox_k_sample', (1, 1, 32, 8, 64)), ('fox_v_sample', (1, 1, 32, 8, 64)),
         ('fox_logf_sample', (1, 1, 32, 8))]


def kernel(**inputs):
    import numpy as _np
    import concourse.bacc as _bacc
    from concourse import mybir as _mybir
    from concourse.bass_utils import run_bass_kernel_spmd as _run

    nc = _bacc.Bacc("TRN2", target_bir_lowering=False, num_devices=1)
    arrays, args, outs = {}, {}, {}
    for name in _INS:
        if name == 'hg_lower_bounds':
            continue
        v = _np.ascontiguousarray(inputs[name])
        arrays[f"in_{name}"] = v
        args[name] = nc.dram_tensor(f"in_{name}", v.shape, _mybir.dt.from_np(v.dtype), kind="ExternalInput").ap()
    for name, shape in _OUTS:
        outs[name] = nc.dram_tensor(f"out_{name}", shape, _mybir.dt.float32, kind="ExternalOutput").ap()
    build(nc, args, outs)
    r = _run(nc, [arrays], core_ids=[0])
    return tuple(r.results[0][f"out_{name}"] for name, _ in _OUTS)
```
